# Optimizing a Trainium2 kernel written in Bass

```python
import math
import jax, jax.numpy as jnp
from jax import lax
import numpy as np

D_MODEL = 1024
BATCH = 1
SEQ = 512
DEPTH = 1

MEM_LEN = 256
RMS_EPS = 1e-6
SB_HEADS = 16
SB_HEAD_DIM = 64
SB_WIDTH = SB_HEADS * SB_HEAD_DIM
SB_BLOCK = 128
SSM_EXPAND = 2
SSM_INNER = SSM_EXPAND * D_MODEL
SSM_HEAD_DIM = 64
SSM_HEADS = SSM_INNER // SSM_HEAD_DIM
SSM_GROUPS = 4
SSM_STATE = 128
SSM_CONV = 4
SSM_CHUNK = 128
SSM_CONV_DIM = SSM_INNER + 2 * SSM_GROUPS * SSM_STATE
XA_HEADS = 4
XA_HEAD_DIM = D_MODEL // XA_HEADS
FFN_HIDDEN = ((8 * D_MODEL + 767) // 768) * 256
IN_SIZES = (SB_WIDTH, SB_WIDTH, SB_WIDTH, SSM_INNER, SSM_CONV_DIM, SSM_HEADS, D_MODEL, D_MODEL)
IN_WIDTH = 3 * SB_WIDTH + SSM_INNER + SSM_CONV_DIM + SSM_HEADS + 2 * D_MODEL


def _split(a, sizes):
    idx = tuple(int(i) for i in np.cumsum(sizes)[:-1])
    return jnp.split(a, idx, axis=-1)

def rms_norm(x, g):
    xf = x.astype(jnp.float32)
    y = xf * lax.rsqrt(jnp.mean(xf * xf, axis=-1, keepdims=True) + RMS_EPS)
    return (y * g.astype(jnp.float32)).astype(x.dtype)

def stick_breaking_attention(q, k, v):
    bsz, seq = q.shape[0], q.shape[1]
    qf = jnp.swapaxes(q.astype(jnp.float32), 1, 2) * (SB_HEAD_DIM ** -0.5)
    kf = jnp.swapaxes(k.astype(jnp.float32), 1, 2)
    vf = jnp.swapaxes(v.astype(jnp.float32), 1, 2)
    outs = []
    for blk in range(seq // SB_BLOCK):
        t0 = blk * SB_BLOCK
        t1 = t0 + SB_BLOCK
        z = jnp.einsum('bhtd,bhsd->bhts', qf[:, :, t0:t1], kf[:, :, :t1])
        causal = jnp.arange(t1)[None, :] < (t0 + jnp.arange(SB_BLOCK))[:, None]
        log_1mb = jnp.where(causal, jax.nn.log_sigmoid(-z), 0.0)
        tail = lax.cumsum(log_1mb, axis=3, reverse=True)
        w = jnp.where(causal, jnp.exp(z + tail), 0.0)
        outs.append(jnp.einsum('bhts,bhsd->bhtd', w, vf[:, :, :t1]))
    o = jnp.concatenate(outs, axis=2)
    return jnp.swapaxes(o, 1, 2).reshape(bsz, seq, SB_WIDTH)

def ssd_chunked(x, dt, a, bm, cm):
    b, l, h, p = x.shape
    g, n = bm.shape[2], bm.shape[3]
    e = h // g
    c = l // SSM_CHUNK
    xc = (x * dt[..., None]).reshape(b, c, SSM_CHUNK, g, e, p)
    a_dt = (dt * a).reshape(b, c, SSM_CHUNK, g, e).transpose(0, 1, 3, 4, 2)
    a_cs = jnp.cumsum(a_dt, axis=-1)
    bc = bm.reshape(b, c, SSM_CHUNK, g, n)
    cc = cm.reshape(b, c, SSM_CHUNK, g, n)
    tril = jnp.tril(jnp.ones((SSM_CHUNK, SSM_CHUNK), dtype=bool))
    decay = jnp.exp(jnp.where(tril, a_cs[..., :, None] - a_cs[..., None, :], -jnp.inf))
    cb = jnp.einsum('bclgn,bcsgn->bcgls', cc, bc)
    y_diag = jnp.einsum('bcgls,bcgels,bcsgep->bclgep', cb, decay, xc)
    decay_to_end = jnp.exp(a_cs[..., -1:] - a_cs)
    states = jnp.einsum('bclgn,bcgel,bclgep->bcgepn', bc, decay_to_end, xc)
    chunk_decay = jnp.exp(a_cs[..., -1])

    def step(prev, inp):
        st, dec = inp
        return prev * dec[..., None, None] + st, prev

    init = jnp.zeros((b, g, e, p, n), dtype=states.dtype)
    _, prev_states = lax.scan(step, init, (jnp.moveaxis(states, 1, 0), jnp.moveaxis(chunk_decay, 1, 0)))
    prev_states = jnp.moveaxis(prev_states, 0, 1)
    y_off = jnp.einsum('bclgn,bcgepn,bcgel->bclgep', cc, prev_states, jnp.exp(a_cs))
    return (y_diag + y_off).reshape(b, l, h, p)

def ssd_branch(z, xbc, dt_raw, conv_w, conv_b, dt_bias, a_log, d_skip, g_norm):
    bsz, seq = xbc.shape[0], xbc.shape[1]
    xbc = lax.conv_general_dilated(
        xbc, conv_w[:, None, :].astype(xbc.dtype), window_strides=(1,),
        padding=[(SSM_CONV - 1, 0)], dimension_numbers=('NWC', 'WIO', 'NWC'),
        feature_group_count=SSM_CONV_DIM)
    xbc = jax.nn.silu(xbc.astype(jnp.float32) + conv_b.astype(jnp.float32))
    xs, bm, cm = _split(xbc, (SSM_INNER, SSM_GROUPS * SSM_STATE, SSM_GROUPS * SSM_STATE))
    dt = jax.nn.softplus(dt_raw.astype(jnp.float32) + dt_bias.astype(jnp.float32))
    a = -jnp.exp(a_log.astype(jnp.float32))
    xh = xs.reshape(bsz, seq, SSM_HEADS, SSM_HEAD_DIM)
    y = ssd_chunked(xh, dt, a,
                    bm.reshape(bsz, seq, SSM_GROUPS, SSM_STATE),
                    cm.reshape(bsz, seq, SSM_GROUPS, SSM_STATE))
    y = y + d_skip.astype(jnp.float32)[:, None] * xh
    y = y.reshape(bsz, seq, SSM_INNER) * jax.nn.silu(z.astype(jnp.float32))
    yg = y.reshape(bsz, seq, SSM_GROUPS, SSM_INNER // SSM_GROUPS)
    yg = yg * lax.rsqrt(jnp.mean(yg * yg, axis=-1, keepdims=True) + RMS_EPS)
    return yg.reshape(bsz, seq, SSM_INNER) * g_norm.astype(jnp.float32)

def memory_cross_attention(h, mem_n, w_xq, w_xkv, w_xo):
    bsz, seq = h.shape[0], h.shape[1]
    q = (h @ w_xq).reshape(bsz, seq, XA_HEADS, XA_HEAD_DIM)
    k, v = _split(mem_n @ w_xkv, (D_MODEL, D_MODEL))
    k = k.reshape(bsz, MEM_LEN, XA_HEADS, XA_HEAD_DIM)
    v = v.reshape(bsz, MEM_LEN, XA_HEADS, XA_HEAD_DIM)
    s = jnp.einsum('bshd,bmhd->bhsm', q.astype(jnp.float32), k.astype(jnp.float32)) * (XA_HEAD_DIM ** -0.5)
    p = jax.nn.softmax(s, axis=-1)
    o = jnp.einsum('bhsm,bmhd->bshd', p, v.astype(jnp.float32)).reshape(bsz, seq, D_MODEL)
    return o.astype(h.dtype) @ w_xo

def swiglu(h, w_gu, w_down):
    gate, up = _split(h @ w_gu, (FFN_HIDDEN, FFN_HIDDEN))
    return (jax.nn.silu(gate) * up) @ w_down

def first_inputs(seed: int = 0) -> dict:
    key = jax.random.key(seed)
    ks = jax.random.split(key, 32)
    f32 = jnp.float32

    def dense(k, shape, fan_in):
        return jax.random.normal(k, shape, f32) * (fan_in ** -0.5)

    def gain(k, shape):
        return 1.0 + 0.02 * jax.random.normal(k, shape, f32)

    dt0 = jnp.exp(jax.random.uniform(ks[5], (DEPTH, SSM_HEADS), f32,
                                     minval=math.log(1e-3), maxval=math.log(1e-1)))
    dt_bias = dt0 + jnp.log(-jnp.expm1(-dt0))
    a_log = jnp.log(jax.random.uniform(ks[6], (DEPTH, SSM_HEADS), f32, minval=1.0, maxval=16.0))
    return {
        "x": jax.random.normal(ks[0], (BATCH, SEQ, D_MODEL), f32),
        "mem": jax.random.normal(ks[1], (BATCH, MEM_LEN, D_MODEL), f32),
        "g_pre_mix": gain(ks[2], (DEPTH, D_MODEL)),
        "w_in": dense(ks[3], (DEPTH, D_MODEL, IN_WIDTH), D_MODEL),
        "conv_w": dense(ks[4], (DEPTH, SSM_CONV, SSM_CONV_DIM), SSM_CONV),
        "conv_b": 0.01 * jax.random.normal(ks[7], (DEPTH, SSM_CONV_DIM), f32),
        "dt_bias": dt_bias,
        "a_log": a_log,
        "d_skip": 1.0 + 0.1 * jax.random.normal(ks[8], (DEPTH, SSM_HEADS), f32),
        "g_ssm_norm": gain(ks[9], (DEPTH, SSM_INNER)),
        "w_br_att": dense(ks[10], (DEPTH, SB_WIDTH, D_MODEL), SB_WIDTH),
        "w_br_ssm": dense(ks[11], (DEPTH, SSM_INNER, D_MODEL), SSM_INNER),
        "w_mix_out": dense(ks[12], (DEPTH, D_MODEL, D_MODEL), D_MODEL),
        "g_post_mix": gain(ks[13], (DEPTH, D_MODEL)),
        "g_pre_xa": gain(ks[14], (DEPTH, D_MODEL)),
        "g_mem": gain(ks[15], (DEPTH, D_MODEL)),
        "w_xq": dense(ks[16], (DEPTH, D_MODEL, D_MODEL), D_MODEL),
        "w_xkv": dense(ks[17], (DEPTH, D_MODEL, 2 * D_MODEL), D_MODEL),
        "w_xo": dense(ks[18], (DEPTH, D_MODEL, D_MODEL), D_MODEL),
        "g_post_xa": gain(ks[19], (DEPTH, D_MODEL)),
        "g_pre_ffn": gain(ks[20], (DEPTH, D_MODEL)),
        "w_gu": dense(ks[21], (DEPTH, D_MODEL, 2 * FFN_HIDDEN), D_MODEL),
        "w_down": dense(ks[22], (DEPTH, FFN_HIDDEN, D_MODEL), FFN_HIDDEN),
        "g_post_ffn": gain(ks[23], (DEPTH, D_MODEL)),
    }

def first_block(x, mem, g_pre_mix, w_in, conv_w, conv_b, dt_bias, a_log, d_skip, g_ssm_norm,
              w_br_att, w_br_ssm, w_mix_out, g_post_mix, g_pre_xa, g_mem, w_xq, w_xkv, w_xo,
              g_post_xa, g_pre_ffn, w_gu, w_down, g_post_ffn):
    bsz, seq = x.shape[0], x.shape[1]
    for l in range(DEPTH):
        h = rms_norm(x, g_pre_mix[l])
        q, k, v, z, xbc, dt_raw, ga, gs = _split(h @ w_in[l], IN_SIZES)
        o_att = stick_breaking_attention(
            q.reshape(bsz, seq, SB_HEADS, SB_HEAD_DIM),
            k.reshape(bsz, seq, SB_HEADS, SB_HEAD_DIM),
            v.reshape(bsz, seq, SB_HEADS, SB_HEAD_DIM)).astype(x.dtype)
        o_ssm = ssd_branch(z, xbc, dt_raw, conv_w[l], conv_b[l], dt_bias[l], a_log[l],
                           d_skip[l], g_ssm_norm[l]).astype(x.dtype)
        merged = jax.nn.sigmoid(ga) * (o_att @ w_br_att[l]) + jax.nn.sigmoid(gs) * (o_ssm @ w_br_ssm[l])
        x = x + rms_norm(merged @ w_mix_out[l], g_post_mix[l])
        h = rms_norm(x, g_pre_xa[l])
        mem_n = rms_norm(mem, g_mem[l])
        x = x + rms_norm(memory_cross_attention(h, mem_n, w_xq[l], w_xkv[l], w_xo[l]), g_post_xa[l])
        h = rms_norm(x, g_pre_ffn[l])
        x = x + rms_norm(swiglu(h, w_gu[l], w_down[l]), g_post_ffn[l])
    return x


D_MIX = D_MODEL
ATT_HEADS = 8
ATT_KV_HEADS = 2
ATT_HEAD_DIM = 64
WINDOW = 128
ATT_BLOCK = 128
GLA_HEADS = 4
GLA_DK = 64
GLA_DV = 128
GLA_GATE_RANK = 16
GLA_TAU = 16.0
GLA_CHUNK = 64
PEER_HEADS = 8
PEER_QDIM = 256
N_KEYS = 128
N_EXPERTS = N_KEYS * N_KEYS
PEER_TOPK = 16
PEER_BLOCK = 128
NORM_EPS = 1e-6

ATT_Q_W = ATT_HEADS * ATT_HEAD_DIM
ATT_KV_W = ATT_KV_HEADS * ATT_HEAD_DIM
GLA_QK_W = GLA_HEADS * GLA_DK
GLA_V_W = GLA_HEADS * GLA_DV
IN_SIZES_2 = (ATT_Q_W, ATT_KV_W, ATT_KV_W, GLA_QK_W, GLA_QK_W, GLA_V_W, GLA_V_W, GLA_GATE_RANK)
IN_WIDTH_2 = sum(IN_SIZES_2)


def rms_norm_2(x, w):
    xf = x.astype(jnp.float32)
    y = xf * lax.rsqrt(jnp.mean(xf * xf, axis=-1, keepdims=True) + NORM_EPS)
    return (y * w.astype(jnp.float32)).astype(x.dtype)

def sliding_window_attention(q, k, v, sinks):
    B, S = q.shape[0], q.shape[1]
    nb = S // ATT_BLOCK
    G = ATT_HEADS // ATT_KV_HEADS
    qb = q.reshape(B, nb, ATT_BLOCK, ATT_KV_HEADS, G, ATT_HEAD_DIM)

    def band(t):
        tb = t.reshape(B, nb, ATT_BLOCK, ATT_KV_HEADS, ATT_HEAD_DIM)
        prev = jnp.pad(tb, ((0, 0), (1, 0), (0, 0), (0, 0), (0, 0)))[:, :-1]
        return jnp.concatenate([prev, tb], axis=2)

    kb, vb = band(k), band(v)
    scores = jnp.einsum('bnqhgd,bnkhd->bnhgqk', qb, kb).astype(jnp.float32) * (ATT_HEAD_DIM ** -0.5)
    blk = jnp.arange(nb)[:, None, None]
    qpos = blk * ATT_BLOCK + jnp.arange(ATT_BLOCK)[None, :, None]
    kpos = (blk - 1) * ATT_BLOCK + jnp.arange(2 * ATT_BLOCK)[None, None, :]
    rel = qpos - kpos
    mask = (rel >= 0) & (rel < WINDOW) & (kpos >= 0)
    scores = jnp.where(mask[None, :, None, None], scores, -jnp.inf)
    sink = sinks.astype(jnp.float32).reshape(ATT_KV_HEADS, G)[None, None, :, :, None, None]
    sink = jnp.broadcast_to(sink, scores.shape[:-1] + (1,))
    probs = jax.nn.softmax(jnp.concatenate([scores, sink], axis=-1), axis=-1)[..., :-1]
    out = jnp.einsum('bnhgqk,bnkhd->bnqhgd', probs.astype(v.dtype), vb)
    return out.reshape(B, S, ATT_Q_W)

def gla_chunked(q, k, v, log_a):
    B, S = q.shape[0], q.shape[1]
    nc = S // GLA_CHUNK

    def chunks(t):
        return t.astype(jnp.float32).reshape(B, nc, GLA_CHUNK, GLA_HEADS, t.shape[-1]).transpose(1, 0, 3, 2, 4)

    qc = chunks(q) * (GLA_DK ** -0.5)
    kc, vc, gc = chunks(k), chunks(v), chunks(log_a)
    causal = jnp.tril(jnp.ones((GLA_CHUNK, GLA_CHUNK), dtype=bool))

    def step(state, inp):
        qt, kt, vt, gt = inp
        b = jnp.cumsum(gt, axis=2)
        inter = jnp.einsum('bhtd,bhde->bhte', qt * jnp.exp(b), state)
        diff = b[:, :, :, None, :] - b[:, :, None, :, :]
        decay = jnp.exp(jnp.where(causal[:, :, None], diff, -jnp.inf))
        att = jnp.einsum('bhtd,bhsd,bhtsd->bhts', qt, kt, decay)
        intra = jnp.einsum('bhts,bhse->bhte', att, vt)
        b_last = b[:, :, -1:, :]
        new_state = jnp.exp(b_last[:, :, 0, :, None]) * state + jnp.einsum(
            'bhsd,bhse->bhde', kt * jnp.exp(b_last - b), vt)
        return new_state, inter + intra

    state0 = jnp.zeros((B, GLA_HEADS, GLA_DK, GLA_DV), jnp.float32)
    _, out = lax.scan(step, state0, (qc, kc, vc, gc))
    return out.transpose(1, 0, 3, 2, 4).reshape(B, S, GLA_HEADS, GLA_DV)

def peer_ffn(h, wq, subkeys, u, v):
    B, S, D = h.shape
    q = (h @ wq).reshape(B, S, PEER_HEADS, 2, PEER_QDIM // 2)
    sub_scores = jnp.einsum('bshpk,hpnk->bshpn', q, subkeys).astype(jnp.float32)
    top_v, top_i = lax.top_k(sub_scores, PEER_TOPK)
    cand = (top_v[..., 0, :, None] + top_v[..., 1, None, :]).reshape(B, S, PEER_HEADS, PEER_TOPK * PEER_TOPK)
    cand_i = (top_i[..., 0, :, None] * N_KEYS + top_i[..., 1, None, :]).reshape(B, S, PEER_HEADS, PEER_TOPK * PEER_TOPK)
    best_v, best_pos = lax.top_k(cand, PEER_TOPK)
    expert = jnp.take_along_axis(cand_i, best_pos, axis=-1)
    gates = jax.nn.softmax(best_v, axis=-1).astype(h.dtype)
    nblk = (B * S) // PEER_BLOCK
    xs = h.reshape(nblk, PEER_BLOCK, D)
    es = expert.reshape(nblk, PEER_BLOCK, PEER_HEADS * PEER_TOPK)
    gs = gates.reshape(nblk, PEER_BLOCK, PEER_HEADS * PEER_TOPK)

    def block(args):
        xb, eb, gb = args
        ub = jnp.take(u, eb, axis=0)
        hid = jax.nn.gelu(jnp.einsum('tkd,td->tk', ub, xb), approximate=False) * gb
        vb = jnp.take(v, eb, axis=0)
        return jnp.einsum('tk,tkd->td', hid, vb)

    return lax.map(block, (xs, es, gs)).reshape(B, S, D)

def second_inputs(seed: int = 0) -> dict:
    key = jax.random.key(seed)
    ks = jax.random.split(key, 20)
    f32 = jnp.float32
    nrm = lambda k, shape, s: jax.random.normal(k, shape, f32) * s
    L = DEPTH
    return {
        "x": nrm(ks[0], (BATCH, SEQ, D_MODEL), 1.0),
        "c": nrm(ks[1], (BATCH, D_MODEL), 1.0),
        "w_ada": nrm(ks[2], (L, D_MODEL, 6 * D_MODEL), 0.5 * D_MODEL ** -0.5),
        "b_ada": nrm(ks[3], (L, 6 * D_MODEL), 0.02),
        "norm1_w": 1.0 + nrm(ks[4], (L, D_MODEL), 0.02),
        "w_in": nrm(ks[5], (L, D_MODEL, IN_WIDTH_2), D_MODEL ** -0.5),
        "attn_sinks": nrm(ks[6], (L, ATT_HEADS), 0.5),
        "gla_gate_up": nrm(ks[7], (L, GLA_GATE_RANK, GLA_QK_W), GLA_GATE_RANK ** -0.5),
        "gla_gate_bias": nrm(ks[8], (L, GLA_QK_W), 0.1),
        "gla_norm_w": 1.0 + nrm(ks[9], (L, GLA_DV), 0.02),
        "w_out": nrm(ks[10], (L, D_MIX, D_MODEL), D_MIX ** -0.5),
        "norm2_w": 1.0 + nrm(ks[11], (L, D_MODEL), 0.02),
        "peer_wq": nrm(ks[12], (L, D_MODEL, PEER_HEADS * PEER_QDIM), D_MODEL ** -0.5),
        "peer_subkeys": nrm(ks[13], (L, PEER_HEADS, 2, N_KEYS, PEER_QDIM // 2), (PEER_QDIM // 2) ** -0.5),
        "peer_u": nrm(ks[14], (L, N_EXPERTS, D_MODEL), D_MODEL ** -0.5),
        "peer_v": nrm(ks[15], (L, N_EXPERTS, D_MODEL), (PEER_HEADS * PEER_TOPK) ** -0.5),
        "final_norm_w": 1.0 + nrm(ks[16], (D_MODEL,), 0.02),
    }

def second_block(x, c, w_ada, b_ada, norm1_w, w_in, attn_sinks, gla_gate_up, gla_gate_bias, gla_norm_w,
              w_out, norm2_w, peer_wq, peer_subkeys, peer_u, peer_v, final_norm_w):
    B, S, _ = x.shape
    split_points = np.cumsum(np.array(IN_SIZES_2))[:-1].tolist()
    for l in range(DEPTH):
        mod = jax.nn.silu(c) @ w_ada[l] + b_ada[l]
        shift1, scale1, gate1, shift2, scale2, gate2 = jnp.split(mod[:, None, :], 6, axis=-1)

        h = rms_norm_2(x, norm1_w[l]) * (1.0 + scale1) + shift1
        proj = h @ w_in[l]
        aq, ak, av, gq, gk, gv, gg, glr = jnp.split(proj, split_points, axis=-1)
        att = sliding_window_attention(
            aq.reshape(B, S, ATT_HEADS, ATT_HEAD_DIM),
            ak.reshape(B, S, ATT_KV_HEADS, ATT_HEAD_DIM),
            av.reshape(B, S, ATT_KV_HEADS, ATT_HEAD_DIM),
            attn_sinks[l])
        log_a = jax.nn.log_sigmoid((glr @ gla_gate_up[l] + gla_gate_bias[l]).astype(jnp.float32)) / GLA_TAU
        go = gla_chunked(
            gq.reshape(B, S, GLA_HEADS, GLA_DK),
            gk.reshape(B, S, GLA_HEADS, GLA_DK),
            gv.reshape(B, S, GLA_HEADS, GLA_DV),
            log_a.reshape(B, S, GLA_HEADS, GLA_DK))
        go = rms_norm_2(go, gla_norm_w[l]).reshape(B, S, GLA_V_W).astype(x.dtype) * jax.nn.silu(gg)
        mixed = jnp.concatenate([att, go], axis=-1) @ w_out[l]
        x = x + gate1 * mixed

        h2 = rms_norm_2(x, norm2_w[l]) * (1.0 + scale2) + shift2
        x = x + gate2 * peer_ffn(h2, peer_wq[l], peer_subkeys[l], peer_u[l], peer_v[l])
    return rms_norm_2(x, final_norm_w)


def setup_inputs(seed=0):
    out = dict(first_inputs(seed))
    for name, value in second_inputs(seed + 1).items():
        if name != "x":
            out[name + "_2"] = value
    return out


def reference(
    x, mem, g_pre_mix, w_in, conv_w, conv_b, dt_bias, a_log, d_skip, g_ssm_norm, w_br_att,
    w_br_ssm, w_mix_out, g_post_mix, g_pre_xa, g_mem, w_xq, w_xkv, w_xo, g_post_xa, g_pre_ffn,
    w_gu, w_down, g_post_ffn, c_2, w_ada_2, b_ada_2, norm1_w_2, w_in_2, attn_sinks_2,
    gla_gate_up_2, gla_gate_bias_2, gla_norm_w_2, w_out_2, norm2_w_2, peer_wq_2, peer_subkeys_2,
    peer_u_2, peer_v_2, final_norm_w_2,
):
    x = first_block(
        x, mem, g_pre_mix, w_in, conv_w, conv_b, dt_bias, a_log, d_skip, g_ssm_norm, w_br_att,
        w_br_ssm, w_mix_out, g_post_mix, g_pre_xa, g_mem, w_xq, w_xkv, w_xo, g_post_xa,
        g_pre_ffn, w_gu, w_down, g_post_ffn,
    )
    return second_block(
        x, c_2, w_ada_2, b_ada_2, norm1_w_2, w_in_2, attn_sinks_2, gla_gate_up_2,
        gla_gate_bias_2, gla_norm_w_2, w_out_2, norm2_w_2, peer_wq_2, peer_subkeys_2, peer_u_2,
        peer_v_2, final_norm_w_2,
    )


_drawn_inputs = setup_inputs


def setup_inputs(seed=0):
    import zlib

    import numpy as np

    out = dict(_drawn_inputs(seed))
    spreads = {}
    factors = {'conv_b': 6.051,
     'g_ssm_norm': 4.271,
     'g_post_mix': 3.417,
     'g_pre_xa': 4.412,
     'g_mem': 2.973,
     'g_post_xa': 4.338,
     'g_pre_ffn': 4.05,
     'g_post_ffn': 5.765,
     'b_ada_2': 7.166,
     'norm1_w_2': 8.0,
     'attn_sinks_2': 35.856,
     'gla_gate_up_2': 2.737,
     'gla_gate_bias_2': 8.0,
     'gla_norm_w_2': 8.0,
     'norm2_w_2': 8.0,
     'peer_wq_2': 7.557,
     'peer_subkeys_2': 7.551,
     'peer_u_2': 8.0,
     'peer_v_2': 7.494,
     'final_norm_w_2': 7.352}
    for name, (base, spread) in spreads.items():
        noise = np.random.default_rng([zlib.crc32(name.encode()), seed]).standard_normal(out[name].shape)
        drawn = base * np.exp(spread * noise) if base else spread * noise
        out[name] = __import__('jax').numpy.asarray(drawn.astype(out[name].dtype))
    for name, factor in factors.items():
        out[name] = (out[name] * factor).astype(out[name].dtype)
    return out
```

```python
import numpy as np

import concourse.bass as bass
from concourse import mybir

F32 = mybir.dt.float32
F32R = mybir.dt.float32r
U32 = mybir.dt.uint32
ACT = mybir.ActivationFunctionType
ALU = mybir.AluOpType
AX = mybir.AxisListType.X

P = 128
D = 1024
T = 512
NT = T // P
KD = D // P
MEM = 256
EPS = 1e-6
KB = 1024
SB_HEADS, SB_DIM = 16, 64
SSM_INNER, SSM_HEADS, SSM_GROUPS, SSM_P = 2048, 32, 4, 64
XA_HEADS, XA_DIM = 4, 256
FFN = 2816
KF = FFN // P
OFF_Q, OFF_K, OFF_V, OFF_Z = 0, 1024, 2048, 3072
OFF_XBC = OFF_Z + SSM_INNER
OFF_DT = OFF_XBC + 3072
OFF_GA = OFF_DT + SSM_HEADS
OFF_GS = OFF_GA + D
SW_HEADS, GLA_HEADS = 8, 4
OFF2_AQ, OFF2_AK, OFF2_AV, OFF2_GQ, OFF2_GK, OFF2_GV, OFF2_GG, OFF2_GLR = 0, 512, 640, 768, 1024, 1280, 1792, 2304
PEER_HEADS, TOPK, NKEYS = 8, 16, 128
SLOTS = PEER_HEADS * TOPK
RING = 8
ROUNDS = SLOTS // RING
LOWEST = -3.4028235e38
TOP_LINKS = 16
DVE_SLOTS = (3, 7)
PE_SLOTS = tuple(j for j in range(RING) if j not in DVE_SLOTS)
LEVELS = 7

C_IDENT, C_NEGGE, C_NEGONE, C_LE, C_GT, C_ONE = (P * i for i in range(6))
C_GLA = 6 * P
C_SWA = C_GLA + LEVELS * P
C_IOTA = C_SWA + 2 * P
C_END = C_IOTA + TOPK


def constant_matrices():
    r = np.arange(P)[:, None]
    c = np.arange(P)[None, :]
    parts = [r == c, -(r >= c).astype(np.float32), -np.ones((P, P)), r <= c, r > c, np.ones((P, P))]
    for level in range(LEVELS):
        half = 1 << level
        parts.append((r // (2 * half) == c // (2 * half)) & (r % (2 * half) < half) & (c % (2 * half) >= half))
    parts.append(np.where(c > r, 0.0, -1e30))
    parts.append(np.where(c <= r, 0.0, -1e30))
    parts.append(np.broadcast_to(np.arange(TOPK), (P, TOPK)))
    return np.concatenate([np.asarray(x, np.float32) for x in parts], axis=1)


V_PRE, V_MEM, V_XA, V_FFN, V_N1, V_N2, V_C = (KD * i for i in range(7))
V_SSM = 7 * KD
V_CB = V_SSM + 16
V_CW = V_CB + 24
V_BADA = V_CW + 96
V_GLAN = V_BADA + 32
V_END = V_GLAN + 1
R_DTB, R_ALOG, R_DSK, R_SINK = 0, 32, 64, 96
R_END = 104


def weight_stream(a):
    groups, chunks = [], []

    def group(name, w, segments, ktiles=KD, jobs=4, evac="av"):
        view = w.rearrange("(k p) n -> p k n", p=P)
        first = len(chunks)
        for k0 in range(0, ktiles, 4):
            kn = min(4, ktiles - k0)
            chunks.append((len(groups), k0, kn, [(view[:, k0:k0 + kn, c0:c1], dst, c1 - c0) for c0, c1, dst in segments]))
        groups.append((name, first, len(chunks) - 1, jobs, evac))

    def plain(name, w, c0, n, ktiles=KD, jobs=4, evac="av"):
        for i in range(n):
            group(f"{name}{i}", w, [(c0 + 512 * i, c0 + 512 * i + 512, 0)], ktiles, jobs, evac)

    w_in, w_in2 = a["w_in"], a["w_in_2"]
    plain("q", w_in, OFF_Q, 2)
    plain("k", w_in, OFF_K, 2)
    plain("v", w_in, OFF_V, 2)
    plain("br", a["w_br_att"], 0, 2)
    plain("ga", w_in, OFF_GA, 2, evac="a")
    plain("xbc", w_in, OFF_XBC, 6, evac="a")
    group("dt", w_in, [(OFF_DT, OFF_DT + P, 0)], jobs=1, evac="a")
    plain("z", w_in, OFF_Z, 4, evac="a")
    plain("gs", w_in, OFF_GS, 2, evac="a")
    plain("bs", a["w_br_ssm"], 0, 2, 16, evac="v")
    plain("mix", a["w_mix_out"], 0, 2)
    plain("xk", a["w_xkv"], 0, 2)
    plain("xv", a["w_xkv"], 1024, 2)
    plain("xq", a["w_xq"], 0, 2)
    plain("xo", a["w_xo"], 0, 2)
    for i in range(11):
        group(f"gu{i}", a["w_gu"], [(256 * i, 256 * i + 256, 0), (FFN + 256 * i, FFN + 256 * i + 256, 256)])
    plain("dn", a["w_down"], 0, 2, KF)
    plain("ada", a["w_ada_2"], 0, 12, jobs=1, evac="v")
    group("in0", w_in2, [(OFF2_AQ, OFF2_AQ + 512, 0)])
    group("in1", w_in2, [(OFF2_AK, OFF2_AK + 512, 0)])
    group("in2", w_in2, [(OFF2_GK, OFF2_GK + 256, 0), (OFF2_AK + 64, OFF2_AK + 128, 256), (OFF2_AK, OFF2_AK + 64, 320),
                         (OFF2_GLR, OFF2_GLR + 16, 384)])
    group("in3", w_in2, [(OFF2_GV, OFF2_GV + 512, 0)])
    group("in4", w_in2, [(OFF2_GG, OFF2_GG + 512, 0)])
    plain("out", a["w_out_2"], 0, 2)
    plain("pq", a["peer_wq_2"], 0, 4)
    return groups, chunks


def build_program(nc, a, out):
    from contextlib import ExitStack

    GROUPS, CHUNKS = weight_stream(a)
    G = {name: g for g, (name, *_) in enumerate(GROUPS)}
    acc_before = [sum(x[3] for x in GROUPS[:g]) for g in range(len(GROUPS) + 1)]
    act_evacs = [sum("a" in x[4] for x in GROUPS[:g]) for g in range(len(GROUPS) + 1)]
    dve_evacs = [sum("v" in x[4] for x in GROUPS[:g]) for g in range(len(GROUPS) + 1)]
    last_of_group = {x[2]: g for g, x in enumerate(GROUPS)}
    landed_count = [16 * sum(len(CHUNKS[m][3]) for m in range(n % 2, n + 1, 2)) for n in range(len(CHUNKS))]
    open_chunks_before = [sum(m not in last_of_group for m in range(n)) for n in range(len(CHUNKS) + 1)]

    with ExitStack() as ctx:
        def sem(name):
            return ctx.enter_context(nc.semaphore(name))

        CONST = 16512
        WRAW = CONST + 10 * KB
        WHI = WRAW + 16 * KB
        WLO = WHI + 16 * KB
        XRES = WLO + 16 * KB
        HA = XRES + 16 * KB
        HB = HA + 16 * KB
        M = HB + 16 * KB
        A = M + 16 * KB
        TT = A + 48 * KB

        def at(name, base, off_kb, shape, dt=F32):
            return nc.alloc_sbuf_tensor_at(name, shape, dt, offset=base + int(off_kb * KB))

        cst = at("cst", CONST, 0, [P, C_END])
        vec = at("vec", CONST, 7.625, [P, V_END])
        row = at("row", CONST, 8.625, [P, R_END + 24])
        stat = at("stat", CONST, 9.125, [P, 216])
        newt = stat[:, 184:216].rearrange("p (a n) -> p a n", a=2)
        assert C_END * 4 <= 7.625 * KB and V_END * 4 <= KB and R_END + 24 <= 128
        ident = cst[:, C_IDENT:C_IDENT + P]
        ssq = stat[:, 0:4]
        meps = stat[:, 4:8]
        rstd = stat[:, 8:12]
        ssqy = stat[:, 16:32]
        mepsy = stat[:, 32:48]
        rstdy = stat[:, 48:64]
        smx = stat[:, 64:72]
        snm = stat[:, 72:80]
        ssum = stat[:, 80:88]
        ssk = stat[:, 88:96]
        sden = stat[:, 96:104]
        srec = stat[:, 104:112]

        wraw = at("wraw", WRAW, 0, [P, 2, 4, 512])
        whi = at("whi", WHI, 0, [P, 2, 4, 512], F32R)
        wlo = at("wlo", WLO, 0, [P, 2, 4, 512], F32R)
        x_res = at("x_res", XRES, 0, [P, NT, D])
        hhi = at("hhi", HA, 0, [P, KD, T], F32R)
        hlo = at("hlo", HB, 0, [P, KD, T], F32R)
        u_out = at("u_out", HA, 0, [P, NT, D])
        xn = at("xn", TT, 16, [P, NT, D])
        grow = at("grow", TT, 32, [P, D])
        q_t = at("q_t", A, 0, [P, KD, T])
        k_t = at("k_t", A, 16, [P, KD, T])
        v_s = at("v_s", A, 32, [P, NT, D])
        ohi = at("ohi", A, 0, [P, KD, T], F32R)
        olo = at("olo", M, 0, [P, KD, T], F32R)
        sb_l = at("sb_l", TT, 0, [P, 2, 1280])
        sb_p = at("sb_p", TT, 10, [P, 2, 1280])
        sb_w = at("sb_w", TT, 20, [P, 2, 1280])
        attbr = at("attbr", A, 16, [P, KD, T])
        gate_a = at("gate_a", TT, 0, [P, KD, T])
        merged = at("merged", M, 0, [P, KD, T])
        xs = at("xs", A, 0, [P, NT, SSM_INNER])
        b_t = at("b_t", A, 32, [P, SSM_GROUPS, T])
        c_t = at("c_t", A, 40, [P, SSM_GROUPS, T])
        raw = at("raw", TT, 0, [P, 4, 515])
        cacc = at("cacc", TT, 8.25, [P, 4, T])
        xst = at("xst", TT, 16.25, [P, 4, T])
        segl = at("segl", TT, 0, [P, 2, 8, P])
        dec = at("dec", TT, 8, [P, 2, 8, P])
        xd = at("xd", TT, 16, [P, 2, 8, SSM_P])
        xe = at("xe", TT, 20, [P, 2, 8, SSM_P])
        ysum = at("ysum", TT, 24, [P, 2, 8, SSM_P])
        state = at("state", TT, 28, [P, 512])
        btok = at("btok", TT, 30, [P, 2, P])
        cbm = at("cbm", TT, 31, [P, 2, P])
        dtt = at("dtt", TT, 32, [P, NT, 32])
        adt = at("adt", TT, 32.5, [P, NT, 32])
        eacs = at("eacs", TT, 33, [P, NT, 32])
        dtw = at("dtw", TT, 33.5, [P, NT, 32])
        ecd = at("ecd", TT, 34, [P, NT, 32])
        dta = at("dta", TT, 34.5, [P, NT, 32])
        dtb = at("dtb", TT, 35, [P, NT, 32])
        dt_t = at("dt_t", TT, 35.5, [P, T])
        nega = stat[:, 120:152]
        ztmp = at("ztmp", TT, 0, [P, 2, 4, 512])
        gate_s = at("gate_s", TT, 16, [P, KD, T])
        yhi = at("yhi", A, 0, [P, NT, SSM_INNER], F32R)
        ylo = at("ylo", HA, 0, [P, 16, T], F32R)
        mem_s = at("mem_s", TT, 24, [P, 2, D])
        mem_n = at("mem_n", TT, 16, [P, 2, D])
        mhi = at("mhi", A, 32, [P, KD, MEM], F32R)
        mlo = at("mlo", A, 40, [P, KD, MEM], F32R)
        kx = at("kx", A, 16, [P, KD, MEM])
        vx = at("vx", A, 24, [P, 2, D])
        qx = at("qx", A, 32, [P, KD, T])
        px = at("px", TT, 16, [P, 2, 4, MEM])
        ptx = at("ptx", TT, 0, [P, 8, T])
        guhi = at("guhi", M, 0, [P, KF, T], F32R)
        gulo = at("gulo", M, 44, [P, KF, T], F32R)
        gtmp = at("gtmp", TT, 24, [P, 2, 2, T])
        gate1 = at("gate1", M, 0, [P, D])
        gate2 = at("gate2", M, 4, [P, D])
        modr = at("modr", TT, 0, [P, 2, D])
        modx = at("modx", TT, 8, [P, D])
        cbhi = at("cbhi", TT, 16, [P, KD, P], F32R)
        cblo = at("cblo", TT, 20, [P, KD, P], F32R)
        bada = at("bada", TT, 24, [P, 2, D])
        modc = stat[:, 152:184]
        csil = row[:, R_END:R_END + 8]
        haff = at("haff", TT, 0, [P, KD, T])
        aq_t = at("aq_t", A, 0, [P, 4, T])
        ak_t = at("ak_t", A, 8, [P, T])
        ak_x = at("ak_x", A, 10, [P, T])
        av_t = at("av_t", A, 12, [P, T])
        av_s = at("av_s", A, 14, [P, NT, P])
        gq_t = at("gq_t", A, 16, [P, 2, T])
        gk_t = at("gk_t", A, 20, [P, 2, T])
        gv_s = at("gv_s", A, 24, [P, NT, 512])
        gg_s = at("gg_s", A, 32, [P, NT, 512])
        glr_t = at("glr_t", A, 40, [32, T])
        gup = at("gup", A, 42, [17, 256])
        la_t = at("la_t", A, 43, [P, 2, T])
        sw_s = at("sw_s", TT, 0, [P, SW_HEADS, 2 * P])
        sw_pt = at("sw_pt", TT, 8, [P, 16, P])
        b_cs = at("b_cs", TT, 0, [P, 2, T])
        gl_d = at("gl_d", TT, 4, [P, 2, T])
        gl_q = at("gl_q", TT, 8, [P, 2, T])
        gl_k = at("gl_k", TT, 12, [P, 2, T])
        gl_a = at("gl_a", TT, 16, [P, GLA_HEADS, NT, P])
        gl_m = at("gl_m", TT, 24, [P, 2, NT, P])
        q_in = at("q_in", M, 8, [P, 2, T])
        k_out = at("k_out", M, 12, [P, 2, T])
        k_tok = at("k_tok", TT, 28, [P, NT, 2 * P])
        g_st = at("g_st", TT, 32, [P, 2, P])
        g_dl = at("g_dl", TT, 33, [P, 2, NT])
        ssg = at("ssg", TT, 33.25, [P, 16])
        mpg = at("mpg", TT, 33.5, [P, 16])
        rsg = at("rsg", TT, 33.75, [P, 16])
        go_q = at("go_q", TT, 8, [P, NT, 512])
        go_s = at("go_s", TT, 0, [P, NT, 512])
        u2 = at("u2", TT, 0, [P, NT, D])
        pq_t = at("pq_t", A, 0, [P, 16, T])
        h2_s = at("h2_s", A, 32, [P, NT, D])
        rows = at("rows", HA, 0, [P, RING, D])
        sc = at("sc", WRAW, 0, [P, 16 * NKEYS])
        diag = at("diag", WRAW, 8, [P, RING, P])
        vacc = at("vacc", WRAW, 12, [P, 2, D])
        hid = at("hid", WRAW, 20, [P, SLOTS])
        hidg = at("hidg", WRAW, 20.5, [P, SLOTS])
        hidv = at("hidv", WRAW, 21, [P, SLOTS])
        gatev = at("gatev", WRAW, 21.5, [P, SLOTS])
        gatee = at("gatee", WRAW, 22, [P, SLOTS])
        gates = at("gates", WRAW, 22.5, [P, SLOTS])
        expert = at("expert", WRAW, 23, [P, 2 * SLOTS], U32)
        tk_s = at("tk_s", WRAW, 24, [P, 2, NKEYS])
        tk_r = at("tk_r", WRAW, 25, [P, 2, NKEYS])
        cand = at("cand", WRAW, 26, [P, TOPK, TOPK])
        cand_r = at("cand_r", WRAW, 27, [P, TOPK, TOPK])
        onehot = at("onehot", WRAW, 28, [P, 2, TOPK, TOPK])
        zeros = at("zeros", WRAW, 30, [P, P])
        small = WRAW + 31 * KB
        tv = at("tv", small, 0, [P, 2, TOPK])
        ti = at("ti", small, 0.125, [P, 2, TOPK], U32)
        tif = at("tif", small, 0.25, [P, 2, TOPK])
        bv = at("bv", small, 0.375, [P, TOPK])
        bp = at("bp", small, 0.4375, [P, TOPK], U32)
        bij = at("bij", small, 0.5, [P, 2, TOPK], U32)
        bijf = at("bijf", small, 0.625, [P, 2, TOPK])
        pick_f = at("pick_f", small, 0.75, [P, 2, TOPK])
        expf = at("expf", small, 0.875, [P, TOPK])
        hidu = at("hidu", small, 1, [P, RING])
        hidw = at("hidw", small, 1.0625, [P, RING])
        hidd = at("hidd", small, 1.125, [P, 2])
        idxw = at("idxw", small, 1.25, [P, 2, RING], U32)
        gsum = at("gsum", small, 1.375, [P, PEER_HEADS])
        grec = at("grec", small, 1.4375, [P, PEER_HEADS])
        subk = at("subk", TT, 16, [P, 16, NKEYS])
        peer_g = at("peer_g", TT, 24, [P, D])
        gfin = at("gfin", TT, 28, [P, D])

        ps = ctx.enter_context(nc.psum_tensor("ps", [P, 8, 512], F32))

        def b4(bank, n=4):
            return ps[:, bank, :].rearrange("p (n c) -> p n c", n=n)

        consts_landed = sem("consts_landed")
        x_landed = sem("x_landed")
        landed = [sem("w_landed0"), sem("w_landed1")]
        w_hi = sem("w_hi")
        w_lo = sem("w_lo")
        w_used = sem("w_used")
        acc_ready = sem("acc_ready")
        act_evac = sem("act_evac")
        dve_evac = sem("dve_evac")
        dve_step = sem("dve_step")
        act_step = sem("act_step")
        sq_ready = sem("sq_ready")
        xn_ready = sem("xn_ready")
        tr_ready = sem("tr_ready")
        h_hi = sem("h_hi")
        h_ready = sem("h_ready")
        usq_ready = sem("usq_ready")
        x_ready = sem("x_ready")
        grow_landed = sem("grow_landed")
        z_ready = sem("z_ready")
        l_ready = sem("l_ready")
        sp_ready = sem("sp_ready")
        sp_masked = sem("sp_masked")
        tail_ready = sem("tail_ready")
        w_ready = sem("w_ready")
        w_masked = sem("w_masked")
        o_ready = sem("o_ready")
        o_hi = sem("o_hi")
        o_lo = sem("o_lo")
        root_in = sem("root_in")
        root_out = sem("root_out")
        row_landed = [sem(f"row_landed{j}") for j in range(RING)]
        row_used = [sem(f"row_used{j}") for j in range(RING)]
        S = {}

        def s(name):
            if name not in S:
                S[name] = sem(name)
            return S[name]

        def used(eng, n):
            if n in last_of_group:
                eng.wait_ge(acc_ready, acc_before[last_of_group[n] + 1])
            else:
                eng.wait_ge(w_used, open_chunks_before[n + 1])

        def acc_wait(eng, g, j):
            eng.wait_ge(acc_ready, acc_before[g] + j + 1)

        block = ctx.enter_context(nc.Block())
        NCHUNK = len(CHUNKS)

        def sync_program(sp):
            sp.dma_start(cst[:], a["cst"]).then_inc(consts_landed, 16)
            sp.dma_start(vec[:], a["vec"]).then_inc(consts_landed, 16)
            sp.dma_start(row[:, 0:R_END], a["row"].broadcast_to((P, R_END))).then_inc(consts_landed, 16)
            sp.dma_start(x_res[:], a["x"][0].rearrange("(i p) d -> p i d", p=P)).then_inc(x_landed, 16)
            for n in range(NCHUNK):
                _, _, kn, segments = CHUNKS[n]
                if n >= 2:
                    sp.wait_ge(w_lo, n - 1)
                for src, dst, width in segments:
                    sp.dma_start(wraw[:, n % 2, 0:kn, dst:dst + width], src).then_inc(landed[n % 2], 16)
            for i in range(NT):
                sp.wait_ge(s("out_ready"), i + 1)
                sp.dma_start(out[0].rearrange("(i p) d -> p i d", p=P)[:, i, :], h2_s[:, i, :]).then_inc(s("out_stored"), 16)
            sp.wait_ge(s("out_stored"), 16 * NT)

        def scalar_program(act):
            steps = [0]
            rounded = [0]

            def link(ins):
                steps[0] += 1
                ins.then_inc(act_step, 1)
                act.wait_ge(act_step, steps[0])

            def round_upto(n_last):
                while rounded[0] <= min(n_last, NCHUNK - 1):
                    n = rounded[0]
                    kn = CHUNKS[n][2]
                    act.wait_ge(landed[n % 2], landed_count[n])
                    if n >= 2:
                        used(act, n - 2)
                    act.activation(whi[:, n % 2, 0:kn, :], wraw[:, n % 2, 0:kn, :], ACT.Copy).then_inc(w_hi, 1)
                    rounded[0] += 1

            def group(g, jobs, evac):
                round_upto(GROUPS[g][2] + 2)
                for j in jobs:
                    acc_wait(act, g, j)
                    ins = evac(j, 4 * (g % 2) + j)
                ins.then_inc(act_evac, 1)

            def to_features(dst, base_tile, scale=1.0, n=T):
                return lambda j, bank: act.activation(dst[:, base_tile + j, :], ps[:, bank, 0:n], ACT.Copy, scale=scale)

            def to_tokens(dst, half):
                return lambda j, bank: act.activation(dst[:, j, 512 * half:512 * half + 512], ps[:, bank, :], ACT.Copy)

            roots = [0]

            def root(mid):
                roots[0] += 1
                act.wait_ge(root_in, roots[0])
                act.activation(newt[:, 1, 0:mid.shape[-1]], mid, ACT.Sqrt).then_inc(root_out, 1)

            def rms_squares(r):
                for i in range(NT):
                    if r > 0:
                        act.wait_ge(x_ready, NT * (r - 1) + i + 1)
                    if i > 0:
                        act.wait_ge(sq_ready, NT * r + i)
                    else:
                        act.wait_ge(xn_ready, NT * r) if r else None
                    act.activation(xn[:, 0, :], x_res[:, i, :], ACT.Square, accum_out=ssq[:, i:i + 1]).then_inc(sq_ready, 1)
                root(meps)

            def rms_round(r, gain):
                for k in range(KD):
                    act.wait_ge(tr_ready, KD * r + k + 1)
                    act.activation(hhi[:, k, :], ps[:, k, :], ACT.Copy, scale=vec[:, gain + k:gain + k + 1]).then_inc(h_hi, 1)

            def sublayer_squares(r, u):
                for i in range(NT):
                    if i > 0:
                        act.wait_ge(usq_ready, NT * r + i)
                    act.activation(xn[:, 0, :], u[:, i, :], ACT.Square, accum_out=ssq[:, i:i + 1]).then_inc(usq_ready, 1)
                root(meps)

            round_upto(1)
            act.wait_ge(consts_landed, 48)
            act.wait_ge(x_landed, 16)
            rms_squares(0)
            rms_round(0, V_PRE)
            for i in range(2):
                group(G[f"q{i}"], (0, 1), to_features(q_t, 4 * i, SB_DIM ** -0.5))
            for i in range(2):
                group(G[f"k{i}"], (0, 1), to_features(k_t, 4 * i))
            for i in range(2):
                group(G[f"v{i}"], (0, 1), to_tokens(v_s, i))
            act.preload_act_table_set("natural_log_exp_and_others")

            def log_part(h):
                zb = 3 * (h % 2)
                act.wait_ge(z_ready, h + 1)
                if h >= 2:
                    act.wait_ge(sp_ready, h - 1)
                act.activation(sb_l[:, h % 2, 0:512], ps[:, zb, :], ACT.Abs)
                act.activation(sb_l[:, h % 2, 512:1024], ps[:, zb + 1, :], ACT.Abs)
                link(act.activation(sb_l[:, h % 2, 1024:1280], ps[:, zb + 2, 0:256], ACT.Abs))
                link(act.activation(sb_l[:, h % 2, :], sb_l[:, h % 2, :], ACT.Exp, scale=-1.0))
                act.activation(sb_l[:, h % 2, :], sb_l[:, h % 2, :], ACT.Ln, bias=1.0).then_inc(l_ready, 1)

            def weights_part(h):
                zb = 3 * (h % 2)
                act.wait_ge(tail_ready, h + 1)
                act.activation(sb_w[:, h % 2, 0:512], ps[:, zb, :], ACT.Exp)
                act.activation(sb_w[:, h % 2, 512:1024], ps[:, zb + 1, :], ACT.Exp)
                act.activation(sb_w[:, h % 2, 1024:1280], ps[:, zb + 2, 0:256], ACT.Exp).then_inc(w_ready, 1)

            def round_heads(hp):
                act.wait_ge(o_ready, 2 * hp + 2)
                act.activation(ohi[:, hp, :], ps[:, 6 + hp % 2, :], ACT.Copy).then_inc(o_hi, 1)

            log_part(0)
            for h in range(SB_HEADS):
                if h + 1 < SB_HEADS:
                    log_part(h + 1)
                weights_part(h)
                if h >= 2 and h % 2 == 0:
                    round_heads(h // 2 - 1)
            round_heads(7)
            for i in range(2):
                group(G[f"br{i}"], (0, 1), to_features(attbr, 4 * i))
            for i in range(2):
                group(G[f"ga{i}"], range(4), lambda j, bank: act.activation(gate_a[:, 4 * i + j, :], ps[:, bank, :], ACT.Sigmoid))

            def silu_tiles(f):
                dst = [xst, xst, xst, xst, b_t, c_t][f]
                for j in range(4):
                    act.wait_ge(s("conv_ready"), 4 * f + j + 1)
                    if 1 <= f < 4:
                        act.wait_ge(s("xtr_ready"), 4 * f)
                    act.activation(dst[:, j, :], cacc[:, j, :], ACT.Silu, bias=vec[:, V_CB + 4 * f + j:V_CB + 4 * f + j + 1]).then_inc(s("xs_ready"), 1)

            def x_tokens(f):
                for j in range(2):
                    act.wait_ge(s("xtr_ready"), 4 * f + j + 1)
                    act.activation(xs[:, :, P * (4 * f + j):P * (4 * f + j + 1)], b4(4 * (G[f"xbc{f}"] % 2) + j), ACT.Copy).then_inc(s("xtok_act"), 1)

            for f in range(6):
                if f == 0:
                    act.wait_ge(s("merged_done"), 8)

                def copy_raw(j, bank):
                    if f >= 1:
                        act.wait_ge(s("conv_ready"), 4 * f)
                    return act.activation(raw[:, j, 3:515], ps[:, bank, :], ACT.Copy)
                round_upto(GROUPS[G[f"xbc{f}"]][2] + 2)
                group(G[f"xbc{f}"], range(4), copy_raw)
                if 1 <= f <= 4:
                    x_tokens(f - 1)
                silu_tiles(f)
            group(G["dt"], (0,), lambda j, bank: act.activation(dt_t[:, :], ps[:, bank, :], ACT.Copy))

            act.preload_act_table_set("natural_log_exp_and_others")
            act.activation(nega, row[:, R_ALOG:R_ALOG + 32], ACT.Exp).then_inc(s("dt_act"), 1)
            act.wait_ge(s("dt_dve"), 1)
            link(act.activation(dtb[:], dta[:], ACT.Abs))
            link(act.activation(dtb[:], dtb[:], ACT.Exp, scale=-1.0))
            act.activation(dtb[:], dtb[:], ACT.Ln, bias=1.0).then_inc(s("dt_act"), 1)
            act.wait_ge(s("acs_ready"), 1)
            act.activation(eacs[:], b4(5)[:, :, 0:32], ACT.Exp)
            act.activation(ecd[:], b4(5)[:, :, 32:64], ACT.Exp)
            act.activation(dta[:], b4(5)[:, :, 32:64], ACT.Copy).then_inc(s("dt_act"), 1)
            act.wait_ge(s("dt_dve"), 3)
            act.activation(dtb[:], dtb[:], ACT.Exp).then_inc(s("dt_act"), 1)
            for u in range(16):
                act.wait_ge(s("cb_ready"), u + 1)
                if u >= 2:
                    act.wait_ge(s("y_mm"), u - 1)
                act.activation(btok[:, u % 2, :], ps[:, 4, P:2 * P], ACT.Copy).then_inc(s("btok_ready"), 1)
                act.wait_ge(s("seg_ready"), u + 1)
                act.activation(dec[:, u % 2, 0:4, :], b4(2 * (u % 2)), ACT.Exp)
                act.activation(dec[:, u % 2, 4:8, :], b4(2 * (u % 2) + 1), ACT.Exp).then_inc(s("dec_ready"), 1)
            act.wait_ge(s("y_done"), 16)
            for i in range(4):
                def gate_z(j, bank):
                    if i >= 2:
                        act.wait_ge(s("yz_done"), 4 * (i - 1))
                    return act.activation(ztmp[:, i % 2, j, :], ps[:, bank, :], ACT.Silu)
                group(G[f"z{i}"], range(4), gate_z)
            for i in range(2):
                group(G[f"gs{i}"], range(4), lambda j, bank: act.activation(gate_s[:, 4 * i + j, :], ps[:, bank, :], ACT.Sigmoid))
            root(mepsy)
            act.wait_ge(s("rstdy_ready"), 1)
            for n in range(0, 16, 2):
                i, g = n % 4, n // 4
                ysl = xs[:, i, 512 * g:512 * g + 512]
                act.activation(ysl, ysl, ACT.Copy, scale=rstdy[:, n:n + 1]).then_inc(s("ysc_act"), 1)
            for f in range(16):
                act.wait_ge(s("ytr_ready"), f + 1)
                act.activation(yhi[:, :, P * f:P * f + P], b4(f % 8), ACT.Copy, scale=vec[:, V_SSM + f:V_SSM + f + 1]).then_inc(s("yhi_ready"), 1)
            round_upto(GROUPS[G["bs1"]][2] + 2)
            for k in range(KD):
                act.wait_ge(s("merged_s"), k + 1)
                if k == 0:
                    acc_wait(act, G["bs1"], 3)
                act.activation(ohi[:, k, :], merged[:, k, :], ACT.Copy).then_inc(o_hi, 1)
            act.dma_start(mem_s[:], a["mem"][0].rearrange("(i p) d -> p i d", p=P)).then_inc(s("vectors_landed"), 16)
            act.wait_ge(s("vectors_landed"), 16)
            for i in range(2):
                if i:
                    act.wait_ge(s("msq_ready"), 1)
                act.activation(mem_n[:, 0, :], mem_s[:, i, :], ACT.Square, accum_out=ssq[:, i:i + 1]).then_inc(s("msq_ready"), 1)
            root(meps[:, 0:2])
            act.dma_start(grow[:], a["g_post_mix"].broadcast_to((P, D))).then_inc(grow_landed, 16)
            for i in range(2):
                group(G[f"mix{i}"], (0, 1), to_tokens(u_out, i))
            for k in range(KD):
                act.wait_ge(s("mtr_ready"), k + 1)
                act.activation(mhi[:, k, :], ps[:, k, 0:MEM], ACT.Copy, scale=vec[:, V_MEM + k:V_MEM + k + 1]).then_inc(s("m_hi"), 1)
            act.wait_ge(dve_evac, dve_evacs[G["mix1"] + 1])
            act.wait_ge(act_evac, act_evacs[G["mix1"] + 1])
            sublayer_squares(0, u_out)
            rms_squares(1)
            for i in range(2):
                group(G[f"xk{i}"], (0, 1), to_features(kx, 4 * i, n=MEM))
            for i in range(2):
                group(G[f"xv{i}"], (0, 1), lambda j, bank: act.activation(vx[:, j // 2, 512 * i + 256 * (j % 2):512 * i + 256 * (j % 2) + 256], ps[:, bank, 0:256], ACT.Copy))
            rms_round(1, V_XA)
            for i in range(2):
                group(G[f"xq{i}"], (0, 1), to_features(qx, 4 * i, XA_DIM ** -0.5))
            for i in range(NT):
                act.wait_ge(s("xmax_ready"), i + 1)
                if i >= 2:
                    act.wait_ge(s("ptr_ready"), 2 * (i - 1))
                for h in range(XA_HEADS):
                    act.activation(px[:, i % 2, h, :], ps[:, 2 * (i % 2) + h // 2, 256 * (h % 2):256 * (h % 2) + 256], ACT.Exp,
                                   bias=snm[:, 4 * (i % 2) + h:4 * (i % 2) + h + 1], accum_out=ssum[:, 4 * (i % 2) + h:4 * (i % 2) + h + 1]).then_inc(s("pexp_ready"), 1)
                act.wait_ge(s("ptr_ready"), 2 * i + 1)
                act.activation(ptx[:, 0:4, P * i:P * i + P], b4(4 + 2 * (i % 2)), ACT.Copy).then_inc(s("pt_act"), 1)
            for d in range(0, KD):
                act.wait_ge(s("ox_ready"), d + 1)
                act.activation(ohi[:, d, :], ps[:, d, :], ACT.Copy).then_inc(o_hi, 1)
            act.dma_start(grow[:], a["g_post_xa"].broadcast_to((P, D))).then_inc(grow_landed, 16)
            for i in range(2):
                group(G[f"xo{i}"], (0, 1), to_tokens(u_out, i))
            act.wait_ge(dve_evac, dve_evacs[G["xo1"] + 1])
            act.wait_ge(act_evac, act_evacs[G["xo1"] + 1])
            sublayer_squares(1, u_out)
            rms_squares(2)
            rms_round(2, V_FFN)
            def round_gu(f):
                for j in range(2):
                    act.wait_ge(dve_evac, dve_evacs[G[f"gu{f}"] + 1])
                    act.activation(guhi[:, 2 * f + j, :], gtmp[:, f % 2, j, :], ACT.Copy).then_inc(s("gu_hi"), 1)

            for f in range(11):
                def gate_up(j, bank):
                    if f >= 2:
                        act.wait_ge(s("gu_lo"), 2 * (f - 1))
                    return act.activation(gtmp[:, f % 2, j, :], ps[:, bank, :], ACT.Silu)
                group(G[f"gu{f}"], (0, 1), gate_up)
                round_gu(f)
            act.dma_start(grow[:], a["g_post_ffn"].broadcast_to((P, D))).then_inc(grow_landed, 16)
            for i in range(2):
                group(G[f"dn{i}"], (0, 1), to_tokens(u_out, i))
            act.wait_ge(dve_evac, dve_evacs[G["dn1"] + 1])
            act.wait_ge(act_evac, act_evacs[G["dn1"] + 1])
            sublayer_squares(2, u_out)
            act.wait_ge(usq_ready, 3 * NT)
            act.activation(csil, vec[:, V_C:V_C + KD], ACT.Silu).then_inc(s("c_ready"), 1)
            for v in range(2):
                act.dma_start(bada[:, v, :], a["b_ada"][:, (2 + 3 * v) * D:(3 + 3 * v) * D].broadcast_to((P, D))).then_inc(s("vectors_landed"), 16)
            for i in range(12):
                round_upto(GROUPS[G[f"ada{i}"]][2] + 2)
            act.wait_ge(s("mod_done"), 1)
            rms_squares(3)
            for k in range(KD):
                act.wait_ge(s("aff_ready"), k + 1)
                act.activation(hhi[:, k, :], haff[:, k, :], ACT.Copy).then_inc(h_hi, 1)
            group(G["in0"], (0, 1), to_features(aq_t, 0, 0.125))
            group(G["in1"], (0, 1), lambda j, bank: act.activation([ak_t, av_t][j][:, :], ps[:, bank, :], ACT.Copy))
            group(G["in2"], (0, 1), to_features(gk_t, 0))
            group(G["in3"], (0, 1), to_tokens(gv_s, 0))
            group(G["in4"], (0, 1), to_tokens(gg_s, 0))
            act.preload_act_table_set("natural_log_exp_and_others")
            for b in range(NT):
                lo = P if b == 0 else 0
                act.wait_ge(s("sw_max"), b + 1)
                for h in range(SW_HEADS):
                    act.activation(sw_s[:, h, lo:], sw_s[:, h, lo:], ACT.Exp, bias=snm[:, h:h + 1], accum_out=ssum[:, h:h + 1])
                act.activation(ssk, ssk, ACT.Exp).then_inc(s("sw_exp"), 1)
                for n in range(4):
                    if n % 2 == 0:
                        act.wait_ge(s("sw_tr"), 4 * b + n + 1)
                        if b > 0 and n == 0:
                            act.wait_ge(s("sw_o"), b)
                        m = slice(1, 4, 2) if b == 0 else slice(0, 4)
                        act.activation(sw_pt[:, 4 * n:4 * n + 4, :][:, m, :], b4(4 + n)[:, m, :], ACT.Copy).then_inc(s("sw_pta"), 1)
                act.wait_ge(s("sw_o"), b + 1)
                act.activation(hhi[:, 0:4, P * b:P * b + P], b4(3), ACT.Copy).then_inc(s("sw_ohi"), 1)
            act.dma_start(gup[:], a["gup"]).then_inc(s("vectors_landed"), 16)
            act.wait_ge(s("la_ready"), 1)
            for t2 in range(2):
                act.activation(gl_d[:, t2, :], ps[:, t2, :], ACT.Copy, scale=-1.0)
            act.activation(la_t[:, 0, :], ps[:, 0, :], ACT.Abs)
            link(act.activation(la_t[:, 1, :], ps[:, 1, :], ACT.Abs))
            link(act.activation(la_t[:], la_t[:], ACT.Exp, scale=-1.0))
            act.activation(la_t[:], la_t[:], ACT.Ln, bias=1.0).then_inc(s("gla_act"), 1)
            act.wait_ge(s("bcs_ready"), 8)
            act.activation(gl_q[:], b_cs[:], ACT.Exp).then_inc(s("gla_act"), 1)
            act.wait_ge(s("bd_ready"), 1)
            act.activation(gl_k[:], gl_d[:], ACT.Exp).then_inc(s("gla_act"), 1)
            act.activation(g_dl[:], b_cs[:, :, P - 1::P], ACT.Exp).then_inc(s("gla_act"), 1)
            for lv in range(LEVELS):
                act.wait_ge(s("gd_ready"), lv + 1)
                link(act.activation(gl_d[:], gl_d[:], ACT.Abs))
                act.activation(gl_d[:], gl_d[:], ACT.Exp, scale=-1.0).then_inc(s("gdec_ready"), 1)
            for c in range(NT):
                act.wait_ge(s("ktr_ready"), c + 1)
                act.activation(k_tok[:, c, :], ps[:, 4 + c, 0:256], ACT.Copy).then_inc(s("ktok_ready"), 1)
            act.activation(gg_s[:], gg_s[:], ACT.Silu).then_inc(s("sgg_ready"), 1)
            root(mpg[:])
            for f in range(4):
                act.wait_ge(s("gotr_ready"), f + 1)
                act.activation(hhi[:, 4 + f, :], ps[:, f, :], ACT.Copy, scale=vec[:, V_GLAN:V_GLAN + 1]).then_inc(s("go_hi"), 1)
            for i in range(2):
                group(G[f"out{i}"], (0, 1), to_tokens(u2, i))
            rms_squares(4)
            for k in range(KD):
                act.wait_ge(s("aff_ready"), KD + k + 1)
                act.activation(hhi[:, k, :], haff[:, k, :], ACT.Copy).then_inc(h_hi, 1)
            for i in range(0, 4):
                act.wait_ge(s("back_ready"), 2 * i + 1)
                act.activation(h2_s[:, i, 0:512], ps[:, 2 * i, :], ACT.Copy).then_inc(s("h2_act"), 1)
            act.dma_start(subk[:], a["subk"]).then_inc(s("vectors_landed"), 16)
            act.dma_start(gfin[:], a["g_final"].broadcast_to((P, D))).then_inc(s("vectors_landed"), 16)
            for i in range(4):
                group(G[f"pq{i}"], (0, 1), to_features(pq_t, 4 * i))

            def scores_out(t):
                if t:
                    act.wait_ge(s("head_done"), PEER_HEADS * t)
                act.wait_ge(s("subs_mm"), t + 1)
                for n in range(4):
                    ins = act.activation(sc[:, 512 * n:512 * n + 512], ps[:, 4 + n, :], ACT.Copy)
                ins.then_inc(s("sc_ready"), 1)

            scores_out(0)
            for t in range(NT):
                if t + 1 < NT:
                    scores_out(t + 1)
                act.wait_ge(s("head_done"), PEER_HEADS * (t + 1))
                act.activation(gatee[:], gatev[:], ACT.Exp).then_inc(s("gate_exp"), 1)
                act.wait_ge(s("hid_ready"), ROUNDS * (t + 1))
                act.activation(hidg[:], hid[:], ACT.Gelu).then_inc(s("gelu_ready"), 1)
                act.wait_ge(s("hidv_ready"), t + 1)
                with act.Fori(0, ROUNDS) as i:
                    act.activation(hidw[:], hidv[:, bass.ts(i, RING)], ACT.Copy).then_inc(s("win_ready"), 1)
                    act.wait_ge(s("win_ready"), i + (ROUNDS * t + 1))
                    for j in PE_SLOTS:
                        act.wait_ge(row_used[j], i + (ROUNDS * (2 * t + 1) + 1))
                        act.activation(diag[:, j, :], ident, ACT.Copy, scale=hidw[:, j:j + 1]).then_inc(s("diag_ready"), 1)
                    act.wait_ge(s("diag_ready"), i * len(PE_SLOTS) + len(PE_SLOTS) * (ROUNDS * t + 1))
            for i in range(NT):
                act.wait_ge(x_ready, NT * 4 + i + 1)
                if i:
                    act.wait_ge(usq_ready, 3 * NT + i)
                act.activation(sc[:, 0:D], x_res[:, i, :], ACT.Square, accum_out=ssq[:, i:i + 1]).then_inc(usq_ready, 1)
            root(meps)

        def gpsimd_program(pool):
            rests = [0]

            def rest_upto(n_last):
                while rests[0] <= min(n_last, NCHUNK - 1):
                    n = rests[0]
                    kn = CHUNKS[n][2]
                    pool.wait_ge(w_hi, n + 1)
                    pool.tensor_tensor(wlo[:, n % 2, 0:kn, :], wraw[:, n % 2, 0:kn, :],
                                       whi[:, n % 2, 0:kn, :].bitcast(F32), ALU.subtract).then_inc(w_lo, 1)
                    rests[0] += 1

            def after(name):
                rest_upto(GROUPS[G[name]][2] + 2)

            rest_upto(1)
            pool.wait_ge(consts_landed, 48)
            after("v1")

            def mask_logs(h):
                pool.wait_ge(sp_ready, h + 1)
                for view, n in ((sb_p[:, h % 2, :].rearrange("p (n c) -> p n c", c=256)[:, 0::2, 0:P], 3), (sb_p[:, h % 2, 896:1024], 1)):
                    pattern = [[0, n], [1, P]] if n > 1 else [[1, P]]
                    pool.affine_select(out=view, in_=view, compare_op=ALU.is_gt, fill=0.0, base=0, pattern=pattern,
                                       channel_multiplier=-1).then_inc(sp_masked, 1)

            def mask_weights(h):
                pool.wait_ge(w_ready, h + 1)
                for view, n in ((sb_w[:, h % 2, :].rearrange("p (n c) -> p n c", c=256)[:, 0::2, 0:P], 3), (sb_w[:, h % 2, 896:1024], 1)):
                    pattern = [[0, n], [1, P]] if n > 1 else [[1, P]]
                    pool.affine_select(out=view, in_=view, compare_op=ALU.is_gt, fill=0.0, base=0, pattern=pattern,
                                       channel_multiplier=-1).then_inc(w_masked, 1)

            mask_logs(0)
            for h in range(SB_HEADS):
                if h + 1 < SB_HEADS:
                    mask_logs(h + 1)
                mask_weights(h)
            after("dt")
            pool.wait_ge(s("dt_dve"), 2)
            pool.wait_ge(s("dt_dve"), 4)
            gt = cst[:, C_GT:C_GT + P]
            for u in range(16):
                g, c = u // 4, u % 4
                if u >= 2:
                    pool.wait_ge(s("seg_ready"), u - 1)
                pool.tensor_tensor(segl[:, u % 2], gt.unsqueeze(1).to_broadcast([P, 8, P]),
                                   adt[:, c, 8 * g:8 * g + 8].unsqueeze(2).to_broadcast([P, 8, P]), ALU.mult).then_inc(s("segl_ready"), 1)
                xg = xs[:, c, 512 * g:512 * g + 512].rearrange("p (e q) -> p e q", e=8)
                if u >= 2:
                    pool.wait_ge(s("y_mm"), u - 1)
                pool.tensor_tensor(xd[:, u % 2], xg, dtt[:, c, 8 * g:8 * g + 8].unsqueeze(2).to_broadcast([P, 8, SSM_P]), ALU.mult)
                pool.tensor_tensor(xe[:, u % 2], xg, dtw[:, c, 8 * g:8 * g + 8].unsqueeze(2).to_broadcast([P, 8, SSM_P]), ALU.mult).then_inc(s("xde_ready"), 1)
                pool.wait_ge(s("xde_ready"), u + 1)
                pool.tensor_tensor(xg, xg, row[:, R_DSK + 8 * g:R_DSK + 8 * g + 8].unsqueeze(2).to_broadcast([P, 8, SSM_P]), ALU.mult).then_inc(s("dx_ready"), 1)
            after("gs1")
            pool.wait_ge(s("rstdy_ready"), 1)
            for n in range(1, 16, 2):
                i, g = n % 4, n // 4
                ysl = xs[:, i, 512 * g:512 * g + 512]
                pool.tensor_scalar(ysl, ysl, rstdy[:, n:n + 1], None, ALU.mult).then_inc(s("ysc_pool"), 1)
            after("bs1")
            after("mix1")
            after("xq1")
            after("xo1")
            after("gu10")
            after("dn1")
            after("ada11")
            after("in4")
            pool.wait_ge(s("gla_act"), 2)
            pool.tensor_tensor(q_in[:], gl_q[:], gq_t[:], ALU.mult).then_inc(s("qin_ready"), 1)
            pool.wait_ge(s("gla_act"), 3)
            pool.tensor_tensor(k_out[:], gl_k[:], gk_t[:], ALU.mult).then_inc(s("kout_ready"), 1)
            for lv in range(LEVELS):
                pool.wait_ge(s("gdec_ready"), lv + 1)
                if lv:
                    pool.wait_ge(s("att_ready"), 4 * lv)
                else:
                    pool.wait_ge(s("qin_ready"), 1)
                pool.tensor_tensor(gl_q[:], gl_d[:], gq_t[:], ALU.mult).then_inc(s("glq_ready"), 1)
            after("out1")
            after("pq3")
            for t in range(NT):
                pool.wait_ge(s("head_done"), PEER_HEADS * (t + 1))
                for phase, table in enumerate((a["u"], a["v"])):
                    with pool.Fori(0, ROUNDS // 2) as i:
                        for w in range(2):
                            first = ROUNDS * (2 * t + phase) + w
                            pool.tensor_copy(idxw[:, w, :], expert[:, bass.ds(i * (2 * RING) + (SLOTS * (t % 2) + RING * w), RING)]).then_inc(s("idx_ready"), 1)
                            pool.wait_ge(s("idx_ready"), i * 2 + (first + 1))
                            for j in range(RING):
                                pool.wait_ge(row_used[j], i * 2 + (first + 1))
                                pool.sem_inc(s("waits_pool"), 1)
                                pool.indirect_dma_start(rows[:, j, :], None, table, bass.IndirectOffsetOnAxis(ap=idxw[:, w, j:j + 1], axis=0)).then_inc(row_landed[j], 16)

        def tensor_program(pe):
            def transpose(dst, src):
                return pe.transpose(dst, src, ident)

            def evacuated(name):
                g = G[name]
                pe.wait_ge(act_evac, act_evacs[g + 1])
                pe.wait_ge(dve_evac, dve_evacs[g + 1])

            def project(g, pick):
                name, first, last, jobs, _ = GROUPS[g]
                if g >= 2:
                    pe.wait_ge(act_evac, act_evacs[g - 1])
                    pe.wait_ge(dve_evac, dve_evacs[g - 1])
                ktiles = CHUNKS[last][1] + CHUNKS[last][2]
                for n in range(first, last + 1):
                    _, k0, kn, _ = CHUNKS[n]
                    pe.wait_ge(w_hi, n + 1)
                    pe.wait_ge(w_lo, n + 1)
                    for j in range(jobs):
                        for kk in range(kn):
                            k = k0 + kk
                            lh, ll, rh, rl, dst = pick(j, n % 2, kk, k)
                            pe.matmul(dst, lh, rh, start=k == 0, stop=False)
                            pe.matmul(dst, lh, rl, start=False, stop=False)
                            ins = pe.matmul(dst, ll, rh, start=False, stop=k == ktiles - 1)
                        if n == last:
                            ins.then_inc(acc_ready, 1)
                    if n != last:
                        ins.then_inc(w_used, 1)

            def features(g, xh, xl, n=T, cols=lambda j: (P * j, P * j + P)):
                def pick(j, slot, kk, k):
                    c0, c1 = cols(j)
                    dst = ps[0:c1 - c0, 4 * (g % 2) + j, 0:n]
                    return whi[:, slot, kk, c0:c1], wlo[:, slot, kk, c0:c1], xh(k), xl(k), dst
                project(g, pick)

            def tokens(g, xh, xl):
                def pick(j, slot, kk, k):
                    t = slice(P * j, P * j + P)
                    return xh[:, k, t], xl[:, k, t], whi[:, slot, kk, :], wlo[:, slot, kk, :], ps[:, 4 * (g % 2) + j, :]
                project(g, pick)

            hh, hl = (lambda k: hhi[:, k, :]), (lambda k: hlo[:, k, :])
            oh, ol = (lambda k: ohi[:, k, :]), (lambda k: olo[:, k, :])

            def transpose_normed(r):
                pe.wait_ge(xn_ready, NT * (r + 1))
                for k in range(KD):
                    for i in range(NT):
                        ins = transpose(ps[:, k, P * i:P * i + P], xn[:, i, P * k:P * k + P])
                    ins.then_inc(tr_ready, 1)
                pe.wait_ge(h_ready, KD * (r + 1))

            pe.wait_ge(consts_landed, 48)
            transpose_normed(0)
            for name in ("q0", "q1", "k0", "k1"):
                features(G[name], hh, hl)
            for name in ("v0", "v1"):
                tokens(G[name], hhi, hlo)
            evacuated("v1")
            place = [(0, 0, 512), (1, 0, 384), (2, 0, 256), (1, 384, 128)]

            def scores(h):
                base = 64 * (h % 2)
                if h >= 2:
                    pe.wait_ge(w_ready, h - 1)
                for b in (0, 1, 3, 2):
                    bank, off, n = place[b]
                    ins = pe.matmul(ps[:, 3 * (h % 2) + bank, off:off + n], k_t[base:base + 64, h // 2, P * b:P * b + P],
                                    q_t[base:base + 64, h // 2, P * b:T], start=b != 3, stop=False, skip_group_check=True)
                ins.then_inc(z_ready, 1)

            def tails(h):
                pe.wait_ge(sp_masked, 2 * h + 2)
                p_off = [0, 512, 1024, 896]
                for b in range(4):
                    bank, off, n = place[b]
                    for c in range(b, 4):
                        w = cst[:, C_NEGGE:C_NEGGE + P] if c == b else cst[:, C_NEGONE:C_NEGONE + P]
                        d = P * (c - b)
                        ins = pe.matmul(ps[:, 3 * (h % 2) + bank, off + d:off + n], w,
                                        sb_p[:, h % 2, p_off[c]:p_off[c] + T - P * c], start=False, stop=c == 3, skip_group_check=True)
                ins.then_inc(tail_ready, 1)

            def outputs(h):
                pe.wait_ge(w_masked, 2 * h + 2)
                if h >= 4 and h % 2 == 0:
                    pe.wait_ge(o_hi, h // 2 - 1)
                    pe.wait_ge(o_lo, h // 2 - 1)
                base = 64 * (h % 2)
                w_off = [0, 512, 1024, 896]
                for b in range(4):
                    ins = pe.matmul(ps[base:base + 64, 6 + (h // 2) % 2, P * b:T], v_s[:, b, 64 * h:64 * h + 64],
                                    sb_w[:, h % 2, w_off[b]:w_off[b] + T - P * b], start=b == 0, stop=b == 3, skip_group_check=True)
                ins.then_inc(o_ready, 1)

            scores(0)
            for h in range(SB_HEADS):
                if h + 1 < SB_HEADS:
                    scores(h + 1)
                tails(h)
                if h >= 1:
                    outputs(h - 1)
            outputs(SB_HEADS - 1)
            pe.wait_ge(o_hi, 8)
            pe.wait_ge(o_lo, 8)
            for name in ("br0", "br1"):
                features(G[name], oh, ol)
            for name in ("ga0", "ga1"):
                features(G[name], hh, hl)

            def transpose_x(f):
                pe.wait_ge(s("xs_ready"), 4 * f + 4)
                for j in range(4):
                    for i in range(NT):
                        ins = transpose(ps[:, 4 * (G[f"xbc{f}"] % 2) + j, P * i:P * i + P], xst[:, j, P * i:P * i + P])
                    ins.then_inc(s("xtr_ready"), 1)
                pe.wait_ge(s("xtok_act"), 2 * f + 2)
                pe.wait_ge(s("xtok_dve"), 2 * f + 2)

            for f in range(6):
                features(G[f"xbc{f}"], hh, hl)
                if 1 <= f <= 4:
                    transpose_x(f - 1)
            features(G["dt"], hh, hl)
            evacuated("dt")
            pe.wait_ge(s("conv_ready"), 24)
            for c in range(NT):
                ins = transpose(ps[:, 6, P * c:P * c + P], dt_t[:, P * c:P * c + P])
            ins.then_inc(s("dttr_ready"), 1)
            pe.wait_ge(s("dt_dve"), 2)
            pe.matmul(b4(5)[:, :, 0:32], cst[:, C_LE:C_LE + P], adt[:], start=True, stop=True)
            pe.matmul(b4(5)[:, :, 32:64], cst[:, C_ONE:C_ONE + P], adt[:], start=True, stop=True).then_inc(s("acs_ready"), 1)
            pe.wait_ge(s("dt_act"), 4)

            def inside(u):
                g, c = u // 4, u % 4
                t = slice(P * c, P * c + P)
                if u >= 2:
                    pe.wait_ge(s("dec_ready"), u - 1)
                if u:
                    pe.wait_ge(s("cbm_ready"), u)
                pe.matmul(ps[:, 4, 0:P], b_t[:, g, t], c_t[:, g, t], start=True, stop=True)
                transpose(ps[:, 4, P:2 * P], b_t[:, g, t]).then_inc(s("cb_ready"), 1)
                pe.wait_ge(s("segl_ready"), u + 1)
                for e in range(8):
                    ins = pe.matmul(ps[:, 2 * (u % 2) + e // 4, P * (e % 4):P * (e % 4) + P], segl[:, u % 2, e, :], cst[:, C_LE:C_LE + P], start=True, stop=True)
                ins.then_inc(s("seg_ready"), 1)

            inside(0)
            for u in range(16):
                if u < 15:
                    inside(u + 1)
                g, c = u // 4, u % 4
                pe.wait_ge(s("wmat_ready"), u + 1)
                pe.wait_ge(s("xde_ready"), u + 1)
                if u:
                    pe.wait_ge(s("yadd_ready"), u)
                for e in range(8):
                    pe.matmul(ps[:, 5, 64 * e:64 * e + 64], dec[:, u % 2, e, :], xd[:, u % 2, e, :], start=True, stop=True)
                if c > 0:
                    pe.wait_ge(s("state_ready"), 3 * g + c)
                    pe.matmul(ps[:, 6, :], c_t[:, g, P * c:P * c + P], state[:], start=True, stop=True)
                pe.wait_ge(s("btok_ready"), u + 1)
                pe.matmul(ps[:, 7, :], btok[:, u % 2, :], xe[:, u % 2], start=True, stop=True).then_inc(s("y_mm"), 1)
            pe.wait_ge(s("y_done"), 16)
            for i in range(4):
                tokens(G[f"z{i}"], hhi, hlo)
            for i in range(2):
                features(G[f"gs{i}"], hh, hl)
            pe.wait_ge(s("ysc_act"), 8)
            pe.wait_ge(s("ysc_pool"), 8)
            evacuated("gs1")
            for f in range(16):
                if f >= 8:
                    pe.wait_ge(s("yhi_ready"), f - 7)
                    pe.wait_ge(s("ylo_ready"), f - 7)
                for i in range(NT):
                    ins = transpose(ps[:, f % 8, P * i:P * i + P], xs[:, i, P * f:P * f + P])
                ins.then_inc(s("ytr_ready"), 1)
            pe.wait_ge(s("yhi_ready"), 16)
            pe.wait_ge(s("ylo_ready"), 16)
            for i in range(2):
                features(G[f"bs{i}"], lambda k: yhi[:, :, P * k:P * k + P], lambda k: ylo[:, k, :])
            pe.wait_ge(o_hi, 8 + KD)
            pe.wait_ge(o_lo, 8 + KD)
            for i in range(2):
                tokens(G[f"mix{i}"], ohi, olo)
            pe.wait_ge(s("memn_ready"), 2)
            evacuated("mix1")
            for k in range(KD):
                for i in range(2):
                    ins = transpose(ps[:, k, P * i:P * i + P], mem_n[:, i, P * k:P * k + P])
                ins.then_inc(s("mtr_ready"), 1)
            pe.wait_ge(s("m_lo"), KD)
            for i in range(2):
                features(G[f"xk{i}"], lambda k: mhi[:, k, :], lambda k: mlo[:, k, :], n=MEM)
            for i in range(2):
                g = G[f"xv{i}"]

                def pick(j, slot, kk, k):
                    t, c = slice(P * (j // 2), P * (j // 2) + P), slice(256 * (j % 2), 256 * (j % 2) + 256)
                    return mhi[:, k, t], mlo[:, k, t], whi[:, slot, kk, c], wlo[:, slot, kk, c], ps[:, 4 * (g % 2) + j, 0:256]
                project(g, pick)
            evacuated("xv1")
            transpose_normed(1)
            for i in range(2):
                features(G[f"xq{i}"], hh, hl)
            evacuated("xq1")

            def xa_scores(i):
                if i >= 2:
                    pe.wait_ge(s("pexp_ready"), 4 * (i - 1))
                for h in range(XA_HEADS):
                    for d in range(2):
                        ins = pe.matmul(ps[:, 2 * (i % 2) + h // 2, 256 * (h % 2):256 * (h % 2) + 256],
                                        qx[:, 2 * h + d, P * i:P * i + P], kx[:, 2 * h + d, :], start=d == 0, stop=d == 1)
                ins.then_inc(s("xs_mm"), 1)

            xa_scores(0)
            for i in range(NT):
                if i + 1 < NT:
                    xa_scores(i + 1)
                pe.wait_ge(s("px_ready"), i + 1)
                if i >= 2:
                    pe.wait_ge(s("pt_act"), i - 1)
                    pe.wait_ge(s("pt_dve"), i - 1)
                for n in range(8):
                    ins = transpose(ps[:, 4 + 2 * (i % 2) + n // 4, P * (n % 4):P * (n % 4) + P], px[:, i % 2, n // 2, P * (n % 2):P * (n % 2) + P])
                    if n % 4 == 3:
                        ins.then_inc(s("ptr_ready"), 1)
            pe.wait_ge(s("pt_act"), 4)
            pe.wait_ge(s("pt_dve"), 4)
            for d in range(KD):
                h = d // 2
                for mt in range(2):
                    ins = pe.matmul(ps[:, d, :], vx[:, mt, P * d:P * d + P], ptx[:, 2 * h + mt, :], start=mt == 0, stop=mt == 1)
                ins.then_inc(s("ox_ready"), 1)
            pe.wait_ge(o_hi, 16 + KD)
            pe.wait_ge(o_lo, 16 + KD)
            for i in range(2):
                tokens(G[f"xo{i}"], ohi, olo)
            transpose_normed(2)
            for f in range(11):
                features(G[f"gu{f}"], hh, hl)
            pe.wait_ge(s("gu_hi"), KF)
            pe.wait_ge(s("gu_lo"), KF)
            for i in range(2):
                tokens(G[f"dn{i}"], guhi, gulo)
            pe.wait_ge(s("cb_lo"), 1)
            for i in range(12):
                g = G[f"ada{i}"]

                def pick(j, slot, kk, k):
                    return cbhi[:, k, :], cblo[:, k, :], whi[:, slot, kk, :], wlo[:, slot, kk, :], ps[:, 4 * (g % 2), :]
                project(g, pick)
            evacuated("ada11")
            transpose_normed(3)
            features(G["in0"], hh, hl)
            features(G["in1"], hh, hl)
            features(G["in2"], hh, hl, cols=lambda j: [(0, 128), (128, 256), (256, 384), (384, 400)][j])
            tokens(G["in3"], hhi, hlo)
            tokens(G["in4"], hhi, hlo)
            evacuated("in4")
            for i in range(NT):
                ins = transpose(ps[:, 0, P * i:P * i + P], av_t[:, P * i:P * i + P])
            ins.then_inc(s("avtr_ready"), 1)
            pe.wait_ge(s("av_ready"), 1)
            for b in range(NT):
                if b:
                    pe.wait_ge(s("sw_sc"), 4 * b)
                    pe.wait_ge(s("sw_ohi"), b)
                    pe.wait_ge(s("sw_olo"), b)
                for h in (0, 2, 4, 6, 1, 3, 5, 7):
                    base, kv = 64 * (h % 2), h // 4
                    keys = ak_t if base == 64 * kv else ak_x
                    lo = P if b == 0 else 0
                    c0 = 256 * (h // 2 % 2)
                    ins = pe.matmul(ps[:, 2 * (h % 2) + h // 4, c0 + lo:c0 + 256], aq_t[base:base + 64, h // 2, P * b:P * b + P],
                                    keys[base:base + 64, P * (b - 1) + lo:P * (b + 1)], start=True, stop=True)
                    if h // 2 % 2:
                        ins.then_inc(s("sw_mm"), 1)
                pe.wait_ge(s("sw_p"), b + 1)
                if b:
                    pe.wait_ge(s("sw_pta"), 2 * b)
                    pe.wait_ge(s("sw_ptd"), 2 * b)
                for n in range(4):
                    for m in range(4):
                        q = 4 * n + m
                        if b == 0 and q % 2 == 0:
                            continue
                        ins = transpose(ps[:, 4 + n, P * m:P * m + P], sw_s[:, q // 2, P * (q % 2):P * (q % 2) + P])
                    ins.then_inc(s("sw_tr"), 1)
                pe.wait_ge(s("sw_pta"), 2 * b + 2)
                pe.wait_ge(s("sw_ptd"), 2 * b + 2)
                for h in range(SW_HEADS):
                    base, kv = 64 * (h % 2), h // 4
                    for kh in range(1 if b == 0 else 0, 2):
                        ins = pe.matmul(ps[base:base + 64, 3, P * (h // 2):P * (h // 2) + P], av_s[:, b - 1 + kh, 64 * kv:64 * kv + 64],
                                        sw_pt[:, 2 * h + kh, :], start=kh == (1 if b == 0 else 0), stop=kh == 1, skip_group_check=True)
                ins.then_inc(s("sw_o"), 1)
            pe.wait_ge(s("sw_ohi"), 4)
            pe.wait_ge(s("sw_olo"), 4)
            pe.wait_ge(s("vectors_landed"), 64)
            for t2 in range(2):
                ins = pe.matmul(ps[:, t2, :], gup[:, P * t2:P * t2 + P], glr_t[0:17, :], start=True, stop=True)
            ins.then_inc(s("la_ready"), 1)
            pe.wait_ge(s("kout_ready"), 1)
            for c in range(NT):
                for t2 in range(2):
                    ins = transpose(ps[:, 4 + c, P * t2:P * t2 + P], k_out[:, t2, P * c:P * c + P])
                ins.then_inc(s("ktr_ready"), 1)
            for lv in range(LEVELS + 1):
                if lv < LEVELS:
                    pe.wait_ge(s("glq_ready"), lv + 1)
                    pe.wait_ge(s("glk_ready"), lv + 1)
                q, k = (gl_q, gl_k) if lv < LEVELS else (gq_t, gk_t)
                for h in range(GLA_HEADS):
                    if lv:
                        pe.wait_ge(s("att_masked"), 4 * (lv - 1) + h + 1)
                    base = 64 * (h % 2)
                    for c in range(NT):
                        t = slice(P * c, P * c + P)
                        ins = pe.matmul(ps[:, h, t], k[base:base + 64, h // 2, t], q[base:base + 64, h // 2, t], start=True, stop=True)
                    ins.then_inc(s("att_ready"), 1)
            pe.wait_ge(s("att_added"), 4 * LEVELS)
            pe.wait_ge(s("ktok_ready"), 4)
            for c in range(NT):
                for h in range(GLA_HEADS):
                    base = 64 * (h % 2)
                    dst = ps[:, 4 * (1 - c % 2) + h % 2, P * (h // 2):P * (h // 2) + P]
                    if c >= 2 and h == 0:
                        pe.wait_ge(s("go_ready"), c - 1)
                    pe.matmul(dst, gl_a[:, h, c, :], gv_s[:, c, P * h:P * h + P], start=True, stop=c == 0, skip_group_check=True)
                    if c:
                        pe.wait_ge(s("gst_ready"), c)
                        pe.matmul(dst, q_in[base:base + 64, h // 2, P * c:P * c + P], g_st[base:base + 64, h // 2, :], start=False, stop=True, skip_group_check=True)
                for t2 in range(2):
                    if c:
                        pe.wait_ge(s("gst_ready"), c)
                    ins = pe.matmul(ps[:, 6, 256 * t2:256 * t2 + 256], k_tok[:, c, P * t2:P * t2 + P], gv_s[:, c, 256 * t2:256 * t2 + 256], start=True, stop=True)
                ins.then_inc(s("go_mm"), 1)
            pe.wait_ge(s("gon_ready"), 1)
            for f in range(4):
                for i in range(NT):
                    ins = transpose(ps[:, f, P * i:P * i + P], go_s[:, i, P * f:P * f + P])
                ins.then_inc(s("gotr_ready"), 1)
            pe.wait_ge(s("go_hi"), 4)
            pe.wait_ge(s("go_lo"), 4)
            for i in range(2):
                tokens(G[f"out{i}"], hhi, hlo)
            transpose_normed(4)
            for i in range(NT):
                for k in range(KD):
                    ins = transpose(ps[:, 2 * i + k // 4, P * (k % 4):P * (k % 4) + P], haff[:, k, P * i:P * i + P])
                    if k % 4 == 3:
                        ins.then_inc(s("back_ready"), 1)
            pe.wait_ge(s("h2_act"), 4)
            pe.wait_ge(s("h2_dve"), 4)
            for i in range(4):
                features(G[f"pq{i}"], hh, hl)
            evacuated("pq3")
            pe.wait_ge(s("vectors_landed"), 96)

            def sub_scores(t):
                if t:
                    pe.wait_ge(s("sc_ready"), t)
                for f in range(16):
                    ins = pe.matmul(ps[:, 4 + f // 4, P * (f % 4):P * (f % 4) + P], pq_t[:, f, P * t:P * t + P], subk[:, f, :], start=True, stop=True)
                ins.then_inc(s("subs_mm"), 1)

            sub_scores(0)
            pe.wait_ge(s("zeros_ready"), 1)
            for t in range(NT):
                if t + 1 < NT:
                    sub_scores(t + 1)
                acc = 2 * (t % 2)
                if t >= 2:
                    pe.wait_ge(x_ready, NT * 4 + t - 1)
                for n in range(2):
                    pe.matmul(ps[:, acc + n, :], zeros[:], h2_s[:, t, 512 * n:512 * n + 512], start=True, stop=False, skip_group_check=True)
                with pe.Fori(0, ROUNDS) as i:
                    for jn, j in enumerate(PE_SLOTS):
                        pe.wait_ge(s("diag_ready"), i * len(PE_SLOTS) + (len(PE_SLOTS) * ROUNDS * t + jn + 1))
                        pe.wait_ge(row_landed[j], i * 16 + 16 * (ROUNDS * (2 * t + 1) + 1))
                        for n in range(2):
                            ins = pe.matmul(ps[:, acc + n, :], diag[:, j, :], rows[:, j, 512 * n:512 * n + 512], start=False, stop=False, skip_group_check=True)
                        ins.then_inc(row_used[j], 1)
                for m, j in enumerate(DVE_SLOTS):
                    pe.wait_ge(row_used[j], 2 * ROUNDS * (t + 1) + 1)
                    for n in range(2):
                        ins = pe.matmul(ps[:, acc + n, :], ident, vacc[:, m, 512 * n:512 * n + 512], start=False, stop=m == 1, skip_group_check=True)
                ins.then_inc(s("peer_ready"), 1)

        def vector_program(v):
            steps = [0]

            def link(ins):
                steps[0] += 1
                ins.then_inc(dve_step, 1)
                v.wait_ge(dve_step, steps[0])

            def col(base, k):
                return vec[:, base + k:base + k + 1]

            def group(g, jobs, evac):
                for j in jobs:
                    acc_wait(v, g, j)
                    ins = evac(j, 4 * (g % 2) + j)
                ins.then_inc(dve_evac, 1)

            def to_features(dst, base_tile, scale=None, n=T):
                def evac(j, bank):
                    if scale is None:
                        return v.tensor_copy(dst[:, base_tile + j, :], ps[:, bank, 0:n])
                    return v.tensor_scalar(dst[:, base_tile + j, :], ps[:, bank, 0:n], scale, None, ALU.mult)
                return evac

            def to_tokens(dst, half):
                return lambda j, bank: v.tensor_copy(dst[:, j, 512 * half:512 * half + 512], ps[:, bank, :])

            roots = [0]

            def inverse_root(dst, mid, sums, count):
                v.tensor_scalar(mid, sums, 1.0 / count, EPS, ALU.mult, ALU.add).then_inc(root_in, 1)
                roots[0] += 1
                v.wait_ge(root_out, roots[0])
                n = mid.shape[-1]
                link(v.reciprocal(newt[:, 0, 0:n], newt[:, 1, 0:n]))
                link(v.tensor_tensor(dst, newt[:, 0, 0:n], newt[:, 0, 0:n], ALU.mult))
                link(v.tensor_tensor(dst, dst, mid, ALU.mult))
                link(v.tensor_scalar(dst, dst, -0.5, 1.5, ALU.mult, ALU.add))
                link(v.tensor_tensor(dst, dst, newt[:, 0, 0:n], ALU.mult))

            def rms_scale(r):
                v.wait_ge(sq_ready, NT * (r + 1))
                inverse_root(rstd, meps, ssq, D)
                for i in range(NT):
                    v.tensor_scalar(xn[:, i, :], x_res[:, i, :], rstd[:, i:i + 1], None, ALU.mult).then_inc(xn_ready, 1)

            def rms_rest(r, gain):
                for k in range(KD):
                    v.wait_ge(h_hi, KD * r + k + 1)
                    v.scalar_tensor_tensor(hlo[:, k, :], ps[:, k, :], col(gain, k), hhi[:, k, :].bitcast(F32), ALU.mult, ALU.subtract).then_inc(h_ready, 1)

            def affine(r, mod):
                for k in range(KD):
                    v.wait_ge(tr_ready, KD * r + k + 1)
                    v.tensor_scalar(haff[:, k, :], ps[:, k, :], modc[:, 16 * mod + 8 + k:16 * mod + 9 + k], modc[:, 16 * mod + k:16 * mod + k + 1],
                                    ALU.mult, ALU.add).then_inc(s("aff_ready"), 1)
                for k in range(KD):
                    v.wait_ge(h_hi, KD * r + k + 1)
                    v.tensor_tensor(hlo[:, k, :], haff[:, k, :], hhi[:, k, :].bitcast(F32), ALU.subtract).then_inc(h_ready, 1)

            def add_sublayer(r, name, u):
                v.wait_ge(usq_ready, NT * (r + 1))
                v.wait_ge(grow_landed, 16 * (r + 1))
                inverse_root(rstd, meps, ssq, D)
                for i in range(NT):
                    ins = v.scalar_tensor_tensor(u[:, i, :], u[:, i, :], rstd[:, i:i + 1], grow[:], ALU.mult, ALU.mult)
                link(ins)
                for i in range(NT):
                    v.tensor_tensor(x_res[:, i, :], x_res[:, i, :], u[:, i, :], ALU.add).then_inc(x_ready, 1)

            v.wait_ge(consts_landed, 48)
            rms_scale(0)
            rms_rest(0, V_PRE)
            for i in range(2):
                group(G[f"q{i}"], (2, 3), to_features(q_t, 4 * i, SB_DIM ** -0.5))
            for i in range(2):
                group(G[f"k{i}"], (2, 3), to_features(k_t, 4 * i))
            for i in range(2):
                group(G[f"v{i}"], (2, 3), to_tokens(v_s, i))

            def softplus(h):
                zb = 3 * (h % 2)
                v.wait_ge(l_ready, h + 1)
                if h >= 2:
                    v.wait_ge(tail_ready, h - 1)
                for n, (o, w) in enumerate(((0, 512), (512, 512), (1024, 256))):
                    ins = v.scalar_tensor_tensor(sb_p[:, h % 2, o:o + w], ps[:, zb + n, 0:w], 0.0, sb_l[:, h % 2, o:o + w], ALU.max, ALU.add)
                ins.then_inc(sp_ready, 1)

            def rest_heads(hp):
                v.wait_ge(o_hi, hp + 1)
                v.tensor_tensor(olo[:, hp, :], ps[:, 6 + hp % 2, :], ohi[:, hp, :].bitcast(F32), ALU.subtract).then_inc(o_lo, 1)

            softplus(0)
            for h in range(SB_HEADS):
                if h + 1 < SB_HEADS:
                    softplus(h + 1)
                if h >= 2 and h % 2 == 0:
                    rest_heads(h // 2 - 1)
            rest_heads(7)
            for i in range(2):
                group(G[f"br{i}"], (2, 3), to_features(attbr, 4 * i))
            v.wait_ge(act_evac, act_evacs[G["br1"] + 1])
            v.wait_ge(dve_evac, dve_evacs[G["br1"] + 1])
            for i in range(2):
                v.wait_ge(act_evac, act_evacs[G[f"ga{i}"] + 1])
                for k in range(4 * i, 4 * i + 4):
                    v.tensor_tensor(merged[:, k, :], gate_a[:, k, :], attbr[:, k, :], ALU.mult).then_inc(s("merged_done"), 1)
            v.wait_ge(s("merged_done"), 8)
            link(v.memset(raw[:, :, 0:3], 0.0))

            def x_tokens(f):
                for j in range(2, 4):
                    v.wait_ge(s("xtr_ready"), 4 * f + j + 1)
                    v.tensor_copy(xs[:, :, P * (4 * f + j):P * (4 * f + j + 1)], b4(4 * (G[f"xbc{f}"] % 2) + j)).then_inc(s("xtok_dve"), 1)

            for f in range(6):
                if 1 <= f <= 4:
                    x_tokens(f - 1)
                v.wait_ge(act_evac, act_evacs[G[f"xbc{f}"] + 1])
                if f:
                    v.wait_ge(s("xs_ready"), 4 * f)
                for tap in range(4):
                    for j in range(4):
                        w = col(V_CW, 24 * tap + 4 * f + j)
                        if tap == 0:
                            ins = v.tensor_scalar(cacc[:, j, :], raw[:, j, 0:512], w, None, ALU.mult)
                        else:
                            ins = v.scalar_tensor_tensor(cacc[:, j, :], raw[:, j, tap:tap + 512], w, cacc[:, j, :], ALU.mult, ALU.add)
                        if tap == 3:
                            ins.then_inc(s("conv_ready"), 1)
                    if tap < 3:
                        link(ins)
            v.wait_ge(s("dttr_ready"), 1)
            v.tensor_tensor(dta[:], b4(6)[:, :, 0:32], row[:, R_DTB:R_DTB + 32].unsqueeze(1).to_broadcast([P, NT, 32]), ALU.add).then_inc(s("dt_dve"), 1)
            v.wait_ge(s("dt_act"), 1)
            link(v.tensor_scalar(nega, nega, -1.0, None, ALU.mult))
            v.wait_ge(s("dt_act"), 2)
            link(v.scalar_tensor_tensor(dtt[:], dta[:], 0.0, dtb[:], ALU.max, ALU.add))
            v.tensor_tensor(adt[:], dtt[:], nega.unsqueeze(1).to_broadcast([P, NT, 32]), ALU.mult).then_inc(s("dt_dve"), 1)
            v.wait_ge(s("dt_act"), 3)
            v.tensor_tensor(dtb[:], dta[:], b4(5)[:, :, 0:32], ALU.subtract).then_inc(s("dt_dve"), 1)
            v.wait_ge(s("dt_act"), 4)
            v.tensor_tensor(dtw[:], dtt[:], dtb[:], ALU.mult).then_inc(s("dt_dve"), 1)

            def inside(u):
                v.wait_ge(s("btok_ready"), u + 1)
                v.tensor_tensor(cbm[:, u % 2, :], ps[:, 4, 0:P], cst[:, C_LE:C_LE + P], ALU.mult).then_inc(s("cbm_ready"), 1)
                v.wait_ge(s("dec_ready"), u + 1)
                v.wait_ge(s("cbm_ready"), u + 1)
                v.tensor_tensor(dec[:, u % 2], dec[:, u % 2], cbm[:, u % 2, :].unsqueeze(1).to_broadcast([P, 8, P]), ALU.mult).then_inc(s("wmat_ready"), 1)

            inside(0)
            for u in range(16):
                if u < 15:
                    inside(u + 1)
                g, c = u // 4, u % 4
                hs = slice(8 * g, 8 * g + 8)
                b8 = lambda bank: ps[:, bank, :].rearrange("p (e q) -> p e q", e=8)
                st = state[:].rearrange("p (e q) -> p e q", e=8)
                v.wait_ge(s("y_mm"), u + 1)
                if c == 0:
                    v.tensor_copy(state[:], ps[:, 7, :]).then_inc(s("state_ready"), 1)
                elif c < 3:
                    v.wait_ge(s("state_ready"), 3 * g + c)
                    link(v.tensor_tensor(st, st, ecd[:, c, hs].unsqueeze(2).to_broadcast([P, 8, SSM_P]), ALU.mult))
                    v.tensor_tensor(state[:], state[:], ps[:, 7, :], ALU.add).then_inc(s("state_ready"), 1)
                ys = ysum[:, u % 2]
                if c:
                    link(v.tensor_tensor(ys, b8(6), eacs[:, c, hs].unsqueeze(2).to_broadcast([P, 8, SSM_P]), ALU.mult))
                    v.tensor_tensor(ys, ys, b8(5), ALU.add).then_inc(s("yadd_ready"), 1)
                else:
                    v.tensor_copy(ys, b8(5)).then_inc(s("yadd_ready"), 1)
                v.wait_ge(s("yadd_ready"), u + 1)
                v.wait_ge(s("dx_ready"), u + 1)
                xg = xs[:, c, 512 * g:512 * g + 512].rearrange("p (e q) -> p e q", e=8)
                v.tensor_tensor(xg, xg, ys, ALU.add).then_inc(s("y_done"), 1)
            for i in range(4):
                v.wait_ge(act_evac, act_evacs[G[f"z{i}"] + 1])
                for j in range(NT):
                    ysl = xs[:, j, 512 * i:512 * i + 512]
                    ins = v.tensor_tensor(ysl, ysl, ztmp[:, i % 2, j, :], ALU.mult)
                link(ins)
                for j in range(NT):
                    ysl = xs[:, j, 512 * i:512 * i + 512]
                    n = 4 * i + j
                    v.tensor_tensor_reduce(ztmp[:, i % 2, j, :], ysl, ysl, 1.0, 0.0, ALU.mult, ALU.add, ssqy[:, n:n + 1]).then_inc(s("yz_done"), 1)
            v.wait_ge(s("yz_done"), 16)
            inverse_root(rstdy, mepsy, ssqy, 512)
            v.tensor_copy(row[:, R_END + 8:R_END + 9], rstdy[:, 0:1]).then_inc(s("rstdy_ready"), 1)
            for f in range(16):
                v.wait_ge(s("yhi_ready"), f + 1)
                v.scalar_tensor_tensor(ylo[:, f, :].rearrange("p (i t) -> p i t", i=NT), b4(f % 8), col(V_SSM, f), yhi[:, :, P * f:P * f + P].bitcast(F32),
                                       ALU.mult, ALU.subtract).then_inc(s("ylo_ready"), 1)
            for i in range(2):
                g = G[f"bs{i}"]
                v.wait_ge(act_evac, act_evacs[G["gs1"] + 1])
                group(g, range(4), lambda j, bank: v.tensor_tensor(gate_s[:, 4 * i + j, :], gate_s[:, 4 * i + j, :], ps[:, bank, :], ALU.mult))
                v.wait_ge(dve_evac, dve_evacs[g + 1])
                for k in range(4 * i, 4 * i + 4):
                    v.tensor_tensor(merged[:, k, :], merged[:, k, :], gate_s[:, k, :], ALU.add).then_inc(s("merged_s"), 1)
            for k in range(KD):
                v.wait_ge(o_hi, 8 + k + 1)
                v.tensor_tensor(olo[:, k, :], merged[:, k, :], ohi[:, k, :].bitcast(F32), ALU.subtract).then_inc(o_lo, 1)
            v.wait_ge(s("msq_ready"), 2)
            inverse_root(rstd[:, 0:2], meps[:, 0:2], ssq[:, 0:2], D)
            for i in range(2):
                v.tensor_scalar(mem_n[:, i, :], mem_s[:, i, :], rstd[:, i:i + 1], None, ALU.mult).then_inc(s("memn_ready"), 1)
            for i in range(2):
                group(G[f"mix{i}"], (2, 3), to_tokens(u_out, i))
            for k in range(KD):
                v.wait_ge(s("m_hi"), k + 1)
                v.scalar_tensor_tensor(mlo[:, k, :], ps[:, k, 0:MEM], col(V_MEM, k), mhi[:, k, :].bitcast(F32), ALU.mult, ALU.subtract).then_inc(s("m_lo"), 1)
            add_sublayer(0, "mix", u_out)
            rms_scale(1)
            for i in range(2):
                group(G[f"xk{i}"], (2, 3), to_features(kx, 4 * i, n=MEM))
            for i in range(2):
                group(G[f"xv{i}"], (2, 3), lambda j, bank: v.tensor_copy(vx[:, j // 2, 512 * i + 256 * (j % 2):512 * i + 256 * (j % 2) + 256], ps[:, bank, 0:256]))
            rms_rest(1, V_XA)
            for i in range(2):
                group(G[f"xq{i}"], (2, 3), to_features(qx, 4 * i, XA_DIM ** -0.5))

            def xa_max(i):
                p4 = slice(4 * (i % 2), 4 * (i % 2) + 4)
                v.wait_ge(s("xs_mm"), i + 1)
                if i >= 2:
                    v.wait_ge(s("pexp_ready"), 4 * (i - 1))
                link(v.tensor_reduce(smx[:, p4], ps[:, 2 * (i % 2):2 * (i % 2) + 2, :].rearrange("p b (h m) -> p (b h) m", h=2), AX, ALU.max))
                v.tensor_scalar(snm[:, p4], smx[:, p4], -1.0, None, ALU.mult).then_inc(s("xmax_ready"), 1)

            xa_max(0)
            for i in range(NT):
                if i + 1 < NT:
                    xa_max(i + 1)
                p4 = slice(4 * (i % 2), 4 * (i % 2) + 4)
                v.wait_ge(s("pexp_ready"), 4 * (i + 1))
                link(v.reciprocal(srec[:, p4], ssum[:, p4]))
                v.tensor_tensor(px[:, i % 2], px[:, i % 2], srec[:, p4].unsqueeze(2).to_broadcast([P, XA_HEADS, MEM]), ALU.mult).then_inc(s("px_ready"), 1)
                v.wait_ge(s("ptr_ready"), 2 * i + 2)
                v.tensor_copy(ptx[:, 4:8, P * i:P * i + P], b4(5 + 2 * (i % 2))).then_inc(s("pt_dve"), 1)
            for d in range(KD):
                v.wait_ge(o_hi, 16 + d + 1)
                v.tensor_tensor(olo[:, d, :], ps[:, d, :], ohi[:, d, :].bitcast(F32), ALU.subtract).then_inc(o_lo, 1)
            for i in range(2):
                group(G[f"xo{i}"], (2, 3), to_tokens(u_out, i))
            add_sublayer(1, "xo", u_out)
            rms_scale(2)
            rms_rest(2, V_FFN)
            for f in range(11):
                g = G[f"gu{f}"]
                v.wait_ge(act_evac, act_evacs[g + 1])
                group(g, (2, 3), lambda j, bank: v.tensor_tensor(gtmp[:, f % 2, j - 2, :], gtmp[:, f % 2, j - 2, :], ps[:, bank, :], ALU.mult))
                for j in range(2):
                    v.wait_ge(s("gu_hi"), 2 * f + j + 1)
                    v.tensor_tensor(gulo[:, 2 * f + j, :], gtmp[:, f % 2, j, :], guhi[:, 2 * f + j, :].bitcast(F32), ALU.subtract).then_inc(s("gu_lo"), 1)
            for i in range(2):
                group(G[f"dn{i}"], (2, 3), to_tokens(u_out, i))
            add_sublayer(2, "dn", u_out)
            v.wait_ge(s("c_ready"), 1)
            cs = csil.unsqueeze(2).to_broadcast([P, KD, P])
            link(v.tensor_copy(cbhi[:], cs))
            v.tensor_tensor(cblo[:], cs, cbhi[:].bitcast(F32), ALU.subtract).then_inc(s("cb_lo"), 1)
            v.wait_ge(s("vectors_landed"), 48)
            for i in range(12):
                which, half = i // 2, slice(512 * (i % 2), 512 * (i % 2) + 512)
                g = G[f"ada{i}"]
                if which % 3 == 2:
                    gate = (gate1, gate2)[which // 3]
                    group(g, (0,), lambda j, bank: v.tensor_tensor(gate[:, half], ps[:, bank, :], bada[:, which // 3, half], ALU.add))
                    continue
                mod, scale = which // 3, which % 3
                group(g, (0,), lambda j, bank: v.tensor_copy(modr[:, i // 2 % 2, half], ps[:, bank, :]))
                if i % 2:
                    v.wait_ge(dve_evac, dve_evacs[g + 1])
                    link(v.tensor_tensor(modx[:].rearrange("p (k c) -> p k c", k=KD), modr[:, which % 2, :].rearrange("p (k c) -> p k c", k=KD),
                                         ident.unsqueeze(1).to_broadcast([P, KD, P]), ALU.mult))
                    mc = modc[:, 16 * mod + 8 * scale:16 * mod + 8 * scale + 8]
                    link(v.tensor_reduce(mc, modx[:].rearrange("p (k c) -> p k c", k=KD), AX, ALU.add))
                    link(v.tensor_tensor(mc, mc, vec[:, V_BADA + 16 * mod + 8 * scale:V_BADA + 16 * mod + 8 * scale + 8], ALU.add))
                    if scale:
                        gain = (V_N1, V_N2)[mod]
                        link(v.scalar_tensor_tensor(mc, mc, 1.0, vec[:, gain:gain + 8], ALU.add, ALU.mult))
            v.wait_ge(dve_evac, dve_evacs[G["ada11"] + 1])
            v.tensor_copy(row[:, R_END + 8:R_END + 9], stat[:, 0:1]).then_inc(s("mod_done"), 1)
            rms_scale(3)
            affine(3, 0)
            group(G["in0"], (2, 3), to_features(aq_t, 0, 0.125))
            group(G["in1"], (2, 3), to_features(gq_t, -2, 0.125))
            link(v.memset(glr_t[:], 1.0))
            group(G["in2"], (2, 3), lambda j, bank: v.tensor_copy(ak_x[:, :], ps[:, bank, :]) if j == 2 else v.tensor_copy(glr_t[0:16, :], ps[0:16, bank, :]))
            group(G["in3"], (2, 3), to_tokens(gv_s, 0))
            group(G["in4"], (2, 3), to_tokens(gg_s, 0))
            v.wait_ge(s("avtr_ready"), 1)
            v.tensor_copy(av_s[:], b4(0)).then_inc(s("av_ready"), 1)
            for b in range(NT):
                lo = P if b == 0 else 0
                for n in range(4):
                    v.wait_ge(s("sw_mm"), 4 * b + n + 1)
                    if b and n == 0:
                        v.wait_ge(s("sw_tr"), 4 * b)
                    h0 = 4 * (n % 2) + n // 2
                    ins = v.tensor_tensor(sw_s[:, h0:h0 + 3:2, lo:], ps[:, n, :].rearrange("p (h c) -> p h c", h=2)[:, :, lo:],
                                          cst[:, C_SWA + lo:C_SWA + 256].unsqueeze(1).to_broadcast([P, 2, 256 - lo]), ALU.add)
                    ins.then_inc(s("sw_sc"), 1)
                v.wait_ge(s("sw_sc"), 4 * b + 4)
                link(v.tensor_reduce(smx, sw_s[:, :, lo:], AX, ALU.max))
                link(v.tensor_tensor(smx, smx, row[:, R_SINK:R_SINK + 8], ALU.max))
                v.tensor_scalar(snm, smx, -1.0, None, ALU.mult)
                v.tensor_tensor(ssk, row[:, R_SINK:R_SINK + 8], smx, ALU.subtract).then_inc(s("sw_max"), 1)
                v.wait_ge(s("sw_exp"), b + 1)
                link(v.tensor_tensor(sden, ssum, ssk, ALU.add))
                link(v.reciprocal(srec, sden))
                v.tensor_tensor(sw_s[:, :, lo:], sw_s[:, :, lo:], srec.unsqueeze(2).to_broadcast([P, 8, 256 - lo]), ALU.mult).then_inc(s("sw_p"), 1)
                if b:
                    v.wait_ge(s("sw_o"), b)
                for n in (1, 3):
                    v.wait_ge(s("sw_tr"), 4 * b + n + 1)
                    m = slice(1, 4, 2) if b == 0 else slice(0, 4)
                    v.tensor_copy(sw_pt[:, 4 * n:4 * n + 4, :][:, m, :], b4(4 + n)[:, m, :]).then_inc(s("sw_ptd"), 1)
                v.wait_ge(s("sw_ohi"), b + 1)
                v.tensor_tensor(hlo[:, 0:4, P * b:P * b + P], b4(3), hhi[:, 0:4, P * b:P * b + P].bitcast(F32), ALU.subtract).then_inc(s("sw_olo"), 1)
            v.wait_ge(s("gla_act"), 1)
            link(v.scalar_tensor_tensor(la_t[:], gl_d[:], 0.0, la_t[:], ALU.max, ALU.add))
            link(v.tensor_scalar(la_t[:], la_t[:], -1.0 / 16, None, ALU.mult))
            for t2 in range(2):
                for c in range(NT):
                    v.tensor_tensor_scan(b_cs[:, t2, P * c:P * c + P], cst[:, C_ONE:C_ONE + P], la_t[:, t2, P * c:P * c + P], 0.0, ALU.mult, ALU.add).then_inc(s("bcs_ready"), 1)
            v.wait_ge(s("bcs_ready"), 8)
            b_chunks = b_cs[:].rearrange("p a (c l) -> p (a c) l", c=NT)
            v.tensor_tensor(gl_d[:].rearrange("p a (c l) -> p (a c) l", c=NT), b_chunks[:, :, P - 1:P].to_broadcast([P, 8, P]), b_chunks, ALU.subtract).then_inc(s("bd_ready"), 1)

            def level_difference(lv):
                half = 1 << lv
                view = b_cs[:].rearrange("p a (n l) -> p (a n) l", l=2 * half)
                v.tensor_tensor(gl_d[:].rearrange("p a (n l) -> p (a n) l", l=2 * half), view,
                                view[:, :, half - 1:half].to_broadcast([P, T // half, 2 * half]), ALU.subtract).then_inc(s("gd_ready"), 1)

            v.wait_ge(s("gla_act"), 3)
            for lv in range(LEVELS + 1):
                if lv < LEVELS:
                    if lv:
                        v.wait_ge(s("glq_ready"), lv)
                    level_difference(lv)
                if lv < LEVELS:
                    v.wait_ge(s("gdec_ready"), lv + 1)
                    v.wait_ge(s("kout_ready"), 1)
                    if lv:
                        v.wait_ge(s("att_ready"), 4 * lv)
                    v.tensor_tensor(gl_k[:], gl_d[:], gk_t[:], ALU.mult).then_inc(s("glk_ready"), 1)
                mask = cst[:, C_GLA + P * lv:C_GLA + P * lv + P] if lv < LEVELS else ident
                mask = mask.unsqueeze(1).to_broadcast([P, NT, P])
                for h in range(GLA_HEADS):
                    v.wait_ge(s("att_ready"), 4 * lv + h + 1)
                    if lv == 0:
                        v.tensor_tensor(gl_a[:, h], b4(h), mask, ALU.mult).then_inc(s("att_masked"), 1)
                    else:
                        v.tensor_tensor(gl_m[:, h % 2], b4(h), mask, ALU.mult).then_inc(s("att_masked"), 1)
                        v.wait_ge(s("att_masked"), 4 * lv + h + 1)
                        v.tensor_tensor(gl_a[:, h], gl_a[:, h], gl_m[:, h % 2], ALU.add).then_inc(s("att_added"), 1)
            v.wait_ge(s("gla_act"), 4)
            for c in range(NT):
                v.wait_ge(s("go_mm"), c + 1)
                if c < 3:
                    for t2 in range(2):
                        for hh in range(2):
                            pr = slice(64 * hh, 64 * hh + 64)
                            new = ps[pr, 6, 256 * t2 + P * hh:256 * t2 + P * hh + P]
                            if c == 0:
                                ins = v.tensor_copy(g_st[pr, t2, :], new)
                            else:
                                ins = v.scalar_tensor_tensor(g_st[pr, t2, :], g_st[pr, t2, :], g_dl[pr, t2, c:c + 1], new, ALU.mult, ALU.add)
                    ins.then_inc(s("gst_ready"), 1)
                b0 = 4 * (1 - c % 2)
                v.tensor_copy(go_s[:, c, :].rearrange("p (a b e) -> p b a e", a=2, b=2),
                              ps[:, b0:b0 + 2, 0:256].rearrange("p b (a e) -> p b a e", a=2)).then_inc(s("go_ready"), 1)
                if 0 < c + 1 < 3:
                    v.wait_ge(s("gst_ready"), c + 1)
            v.wait_ge(s("go_ready"), 4)
            link(v.tensor_tensor(go_q[:], go_s[:], go_s[:], ALU.mult))
            link(v.tensor_reduce(ssg[:], go_q[:].rearrange("p i (h e) -> p (i h) e", h=GLA_HEADS), AX, ALU.add))
            inverse_root(rsg[:], mpg[:], ssg[:], P)
            gview = go_s[:].rearrange("p i (h e) -> p (i h) e", h=GLA_HEADS)
            link(v.tensor_tensor(gview, gview, rsg[:].unsqueeze(2).to_broadcast([P, 16, P]), ALU.mult))
            v.wait_ge(s("sgg_ready"), 1)
            v.tensor_tensor(go_s[:], go_s[:], gg_s[:], ALU.mult).then_inc(s("gon_ready"), 1)
            for f in range(4):
                v.wait_ge(s("go_hi"), f + 1)
                v.scalar_tensor_tensor(hlo[:, 4 + f, :], ps[:, f, :], col(V_GLAN, 0), hhi[:, 4 + f, :].bitcast(F32), ALU.mult, ALU.subtract).then_inc(s("go_lo"), 1)
            for i in range(2):
                group(G[f"out{i}"], (2, 3), to_tokens(u2, i))
            v.wait_ge(act_evac, act_evacs[G["out1"] + 1])
            v.wait_ge(dve_evac, dve_evacs[G["out1"] + 1])
            for i in range(NT):
                ins = v.tensor_tensor(u2[:, i, :], u2[:, i, :], gate1[:], ALU.mult)
            link(ins)
            for i in range(NT):
                v.tensor_tensor(x_res[:, i, :], x_res[:, i, :], u2[:, i, :], ALU.add).then_inc(x_ready, 1)
            rms_scale(4)
            affine(4, 1)
            for i in range(NT):
                v.wait_ge(s("back_ready"), 2 * i + 2)
                v.tensor_copy(h2_s[:, i, 512:1024], ps[:, 2 * i + 1, :]).then_inc(s("h2_dve"), 1)
            for i in range(4):
                group(G[f"pq{i}"], (2, 3), to_features(pq_t, 4 * i))
            v.wait_ge(s("sc_ready"), 1)
            v.memset(zeros[:], 0.0).then_inc(s("zeros_ready"), 1)
            for j in range(RING):
                v.sem_inc(row_used[j], 1)
            linked = [0]

            def top_keys(t, i, step):
                step(v.tensor_copy(tk_s[:].rearrange("p a n -> p (a n)"), sc[:, bass.ts(i, 2 * NKEYS)]), fixed=True)
                for h in range(2):
                    ins = v.max(tv[:, h, 0:8], tk_s[:, h, :])
                step(ins, fixed=True)
                for h in range(2):
                    v.max_index(ti[:, h, 0:8], tv[:, h, 0:8], tk_s[:, h, :])
                    ins = v.match_replace(tk_r[:, h, :], tv[:, h, 0:8], tk_s[:, h, :], LOWEST)
                step(ins, fixed=True)
                for h in range(2):
                    ins = v.max(tv[:, h, 8:16], tk_r[:, h, :])
                step(ins, fixed=True)
                for h in range(2):
                    v.max_index(ti[:, h, 8:16], tv[:, h, 8:16], tk_r[:, h, :])
                step(v.tensor_tensor(cand[:], tv[:, 0, :].unsqueeze(2).to_broadcast([P, TOPK, TOPK]),
                                     tv[:, 1, :].unsqueeze(1).to_broadcast([P, TOPK, TOPK]), ALU.add))
                cflat, rflat = cand[:].rearrange("p a b -> p (a b)"), cand_r[:].rearrange("p a b -> p (a b)")
                v.tensor_copy(tif[:], ti[:])
                step(v.max(bv[:, 0:8], cflat), fixed=True)
                v.max_index(bp[:, 0:8], bv[:, 0:8], cflat)
                step(v.match_replace(rflat, bv[:, 0:8], cflat, LOWEST), fixed=True)
                step(v.max(bv[:, 8:16], rflat), fixed=True)
                step(v.max_index(bp[:, 8:16], bv[:, 8:16], rflat))
                v.tensor_scalar(bij[:, 0, :], bp[:], 4, None, ALU.logical_shift_right)
                step(v.tensor_scalar(bij[:, 1, :], bp[:], TOPK - 1, None, ALU.bitwise_and))
                step(v.tensor_copy(bijf[:], bij[:]))
                iota = cst[:, C_IOTA:C_IOTA + TOPK].unsqueeze(1).to_broadcast([P, TOPK, TOPK])
                for h in range(2):
                    ins = v.tensor_tensor(onehot[:, h], bijf[:, h, :].unsqueeze(2).to_broadcast([P, TOPK, TOPK]), iota, ALU.is_equal)
                step(ins)
                for h in range(2):
                    ins = v.tensor_tensor(onehot[:, h], onehot[:, h], tif[:, h, :].unsqueeze(1).to_broadcast([P, TOPK, TOPK]), ALU.mult)
                step(ins)
                step(v.tensor_reduce(pick_f[:], onehot[:], AX, ALU.add))
                step(v.scalar_tensor_tensor(expf[:], pick_f[:, 0, :], float(NKEYS), pick_f[:, 1, :], ALU.mult, ALU.add))
                v.tensor_copy(expert[:, bass.ds(i * TOPK + SLOTS * (t % 2), TOPK)], expf[:])
                step(v.tensor_scalar(bv[:], bv[:], bv[:, 0:1], None, ALU.subtract))
                v.tensor_copy(gatev[:, bass.ts(i, TOPK)], bv[:]).then_inc(s("head_done"), 1)

            def v_slots(t, i, first, step):
                step(v.tensor_copy(hidd[:], hidv[:, bass.ds(i * RING + (first * RING + DVE_SLOTS[0]), 5)][:, 0::4]))
                for m, j in enumerate(DVE_SLOTS):
                    v.wait_ge(row_landed[j], i * 16 + 16 * (ROUNDS * (2 * t + 1) + first + 1))
                    v.scalar_tensor_tensor(vacc[:, m, :], rows[:, j, :], hidd[:, m:m + 1], vacc[:, m, :], ALU.mult, ALU.add).then_inc(row_used[j], 1)
                v.wait_ge(row_used[j], i + (ROUNDS * (2 * t + 1) + first + 2))

            def loop(n, links, body):
                base, k = linked[0], [0]
                with v.Fori(0, n) as i:
                    def step(ins, fixed=False):
                        k[0] += 1
                        ins.then_inc(s("chain"), 1)
                        v.wait_ge(s("chain"), i * links + (base + k[0]))
                        if fixed:
                            v.sem_inc(s("waits_dve"), 1)
                    body(i, step)
                assert k[0] == links, k[0]
                linked[0] += n * links

            def add_peer(t):
                acc = 2 * (t % 2)
                v.wait_ge(s("peer_ready"), t + 1)
                link(v.tensor_tensor(peer_g[:], ps[:, acc:acc + 2, :].rearrange("p b c -> p (b c)"), gate2[:], ALU.mult))
                v.tensor_tensor(x_res[:, t, :], x_res[:, t, :], peer_g[:], ALU.add).then_inc(x_ready, 1)

            loop(PEER_HEADS, TOP_LINKS, lambda i, step: top_keys(0, i, step))
            for t in range(NT):
                def u_rows(i, step):
                    for j in range(RING):
                        v.wait_ge(row_landed[j], i * 16 + 16 * (2 * ROUNDS * t + 1))
                        ins = v.tensor_tensor_reduce(rows[:, j, :], rows[:, j, :], h2_s[:, t, :], 1.0, 0.0, ALU.mult, ALU.add, hidu[:, j:j + 1])
                        ins.then_inc(row_used[j], 1)
                    v.wait_ge(row_used[RING - 1], i + (2 * ROUNDS * t + 2))
                    v.tensor_copy(hid[:, bass.ts(i, RING)], hidu[:]).then_inc(s("hid_ready"), 1)
                    v.wait_ge(s("hid_ready"), i + (ROUNDS * t + 1))
                loop(ROUNDS, 0, u_rows)
                v.wait_ge(s("gate_exp"), t + 1)
                ge = gatee[:].rearrange("p (h k) -> p h k", h=PEER_HEADS)
                link(v.tensor_reduce(gsum[:], ge, AX, ALU.add))
                link(v.reciprocal(grec[:], gsum[:]))
                link(v.tensor_tensor(gates[:].rearrange("p (h k) -> p h k", h=PEER_HEADS), ge, grec[:].unsqueeze(2).to_broadcast([P, PEER_HEADS, TOPK]), ALU.mult))
                v.wait_ge(s("gelu_ready"), t + 1)
                v.tensor_tensor(hidv[:], hidg[:], gates[:], ALU.mult).then_inc(s("hidv_ready"), 1)
                if t:
                    add_peer(t - 1)
                v.wait_ge(s("hidv_ready"), t + 1)
                link(v.memset(vacc[:], 0.0))
                half = ROUNDS // 2

                def v_and_top(i, step):
                    v_slots(t, i, 0, step)
                    top_keys(t + 1, i, step)
                if t + 1 < NT:
                    v.wait_ge(s("sc_ready"), t + 2)
                    loop(half, 1 + TOP_LINKS, v_and_top)
                    loop(half, 1, lambda i, step: v_slots(t, i, half, step))
                else:
                    loop(ROUNDS, 1, lambda i, step: v_slots(t, i, 0, step))
            add_peer(NT - 1)
            v.wait_ge(usq_ready, 4 * NT)
            v.wait_ge(s("vectors_landed"), 96)
            inverse_root(rstd, meps, ssq, D)
            for i in range(NT):
                v.scalar_tensor_tensor(h2_s[:, i, :], x_res[:, i, :], rstd[:, i:i + 1], gfin[:], ALU.mult, ALU.mult).then_inc(s("out_ready"), 1)

        @block.sync
        def _(sp):
            sync_program(sp)

        @block.tensor
        def _(pe):
            tensor_program(pe)

        @block.vector
        def _(v):
            vector_program(v)

        @block.scalar
        def _(act):
            scalar_program(act)

        @block.gpsimd
        def _(pool):
            gpsimd_program(pool)


def lay_out(inputs):
    i = {k: np.asarray(v) for k, v in inputs.items()}

    def cols(v):
        return v.reshape(-1, P).T

    ada = i["b_ada_2"].reshape(6, D)
    arrays = {
        "x": i["x"], "mem": i["mem"], "w_in": i["w_in"][0], "w_br_att": i["w_br_att"][0], "w_br_ssm": i["w_br_ssm"][0],
        "w_mix_out": i["w_mix_out"][0], "w_xq": i["w_xq"][0], "w_xkv": i["w_xkv"][0], "w_xo": i["w_xo"][0],
        "w_gu": i["w_gu"][0], "w_down": i["w_down"][0], "w_ada_2": i["w_ada_2"][0], "w_in_2": i["w_in_2"][0],
        "w_out_2": i["w_out_2"][0], "peer_wq_2": i["peer_wq_2"][0], "u": i["peer_u_2"][0], "v": i["peer_v_2"][0],
        "g_post_mix": i["g_post_mix"], "g_post_xa": i["g_post_xa"], "g_post_ffn": i["g_post_ffn"],
        "g_final": i["final_norm_w_2"].reshape(1, D), "b_ada": i["b_ada_2"],
        "gup": np.concatenate([i["gla_gate_up_2"][0], i["gla_gate_bias_2"]], axis=0),
        "subk": i["peer_subkeys_2"][0].reshape(16, NKEYS, P).transpose(2, 0, 1),
        "cst": constant_matrices(),
        "vec": np.concatenate([cols(i["g_pre_mix"][0]), cols(i["g_mem"][0]), cols(i["g_pre_xa"][0]), cols(i["g_pre_ffn"][0]),
                               cols(i["norm1_w_2"][0]), cols(i["norm2_w_2"][0]), cols(i["c_2"][0]), cols(i["g_ssm_norm"][0]),
                               cols(i["conv_b"][0])] + [cols(i["conv_w"][0, t]) for t in range(4)]
                              + [cols(ada[n]) for n in (0, 1, 3, 4)] + [cols(i["gla_norm_w_2"][0])], axis=1),
        "row": np.concatenate([i["dt_bias"], i["a_log"], i["d_skip"], i["attn_sinks_2"]], axis=1),
    }
    return {k: np.ascontiguousarray(v) for k, v in arrays.items()}


def kernel(**inputs):
    import concourse.bacc as bacc
    from concourse.bass_utils import run_bass_kernel_spmd

    nc = bacc.Bacc("TRN2", target_bir_lowering=False, num_devices=1)
    arrays = lay_out(inputs)
    aps = {k: nc.dram_tensor(f"in_{k}", v.shape, mybir.dt.from_np(v.dtype), kind="ExternalInput").ap() for k, v in arrays.items()}
    out = nc.dram_tensor("out_0", (1, T, D), F32, kind="ExternalOutput").ap()
    build_program(nc, aps, out)
    r = run_bass_kernel_spmd(nc, [{f"in_{k}": v for k, v in arrays.items()}], core_ids=[0])
    return r.results[0]["out_0"]
```

```python
import numpy as np

import concourse.bass as bass
from concourse import mybir

F32 = mybir.dt.float32
F32R = mybir.dt.float32r
U32 = mybir.dt.uint32
ACT = mybir.ActivationFunctionType
ALU = mybir.AluOpType
AX = mybir.AxisListType.X

P = 128
D = 1024
T = 512
NT = T // P
KD = D // P
MEM = 256
EPS = 1e-6
KB = 1024
WK, WSLOTS = 2, 4
SB_HEADS, SB_DIM = 16, 64
SSM_INNER, SSM_HEADS, SSM_GROUPS, SSM_P = 2048, 32, 4, 64
XA_HEADS, XA_DIM = 4, 256
FFN = 2816
KF = FFN // P
OFF_Q, OFF_K, OFF_V, OFF_Z = 0, 1024, 2048, 3072
OFF_XBC = OFF_Z + SSM_INNER
OFF_DT = OFF_XBC + 3072
OFF_GA = OFF_DT + SSM_HEADS
OFF_GS = OFF_GA + D
SW_HEADS, GLA_HEADS = 8, 4
OFF2_AQ, OFF2_AK, OFF2_AV, OFF2_GQ, OFF2_GK, OFF2_GV, OFF2_GG, OFF2_GLR = 0, 512, 640, 768, 1024, 1280, 1792, 2304
PEER_HEADS, TOPK, NKEYS = 8, 16, 128
SLOTS = PEER_HEADS * TOPK
RING = 8
ROUNDS = SLOTS // RING
LOWEST = -3.4028235e38
TOP_LINKS = 16
DVE_SLOTS = (1, 4, 7)
PE_SLOTS = tuple(j for j in range(RING) if j not in DVE_SLOTS)
LEVELS = 7

C_IDENT, C_NEGGE, C_NEGONE, C_LE, C_GT, C_ONE = (P * i for i in range(6))
C_GLA = 6 * P
C_SWA = C_GLA + LEVELS * P
C_IOTA = C_SWA + 2 * P
C_END = C_IOTA + TOPK


def constant_matrices():
    r = np.arange(P)[:, None]
    c = np.arange(P)[None, :]
    parts = [r == c, -(r >= c).astype(np.float32), -np.ones((P, P)), r <= c, r > c, np.ones((P, P))]
    for level in range(LEVELS):
        half = 1 << level
        parts.append((r // (2 * half) == c // (2 * half)) & (r % (2 * half) < half) & (c % (2 * half) >= half))
    parts.append(np.where(c > r, 0.0, -1e30))
    parts.append(np.where(c <= r, 0.0, -1e30))
    parts.append(np.broadcast_to(np.arange(TOPK), (P, TOPK)))
    return np.concatenate([np.asarray(x, np.float32) for x in parts], axis=1)


V_PRE, V_MEM, V_XA, V_FFN, V_N1, V_N2, V_C = (KD * i for i in range(7))
V_SSM = 7 * KD
V_CB = V_SSM + 16
V_CW = V_CB + 24
V_BADA = V_CW + 96
V_GLAN = V_BADA + 48
V_END = V_GLAN + 1
R_DTB, R_ALOG, R_DSK, R_SINK = 0, 32, 64, 96
R_END = 104


def weight_stream(a):
    groups, chunks = [], []

    def group(name, w, segments, ktiles=KD, jobs=4, evac="av"):
        view = w.rearrange("(k p) n -> p k n", p=P)
        first = len(chunks)
        for k0 in range(0, ktiles, WK):
            kn = min(WK, ktiles - k0)
            chunks.append((len(groups), k0, kn, [(view[:, k0:k0 + kn, c0:c1], dst, c1 - c0) for c0, c1, dst in segments]))
        groups.append((name, first, len(chunks) - 1, jobs, evac))

    def plain(name, w, c0, n, ktiles=KD, jobs=4, evac="av"):
        for i in range(n):
            group(f"{name}{i}", w, [(c0 + 512 * i, c0 + 512 * i + 512, 0)], ktiles, jobs, evac)

    def plain_at(name, w, i):
        group(f"{name}{i}", w, [(512 * i, 512 * i + 512, 0)], jobs=1, evac="v")

    w_in, w_in2 = a["w_in"], a["w_in_2"]
    plain("q", w_in, OFF_Q, 2)
    plain("k", w_in, OFF_K, 2)
    plain("v", w_in, OFF_V, 2)
    plain("br", a["w_br_att"], 0, 2)
    plain("ga", w_in, OFF_GA, 2, evac="a")
    plain("xbc", w_in, OFF_XBC, 6, evac="a")
    group("dt", w_in, [(OFF_DT, OFF_DT + P, 0)], jobs=1, evac="a")
    plain("z", w_in, OFF_Z, 4, evac="a")
    plain("gs", w_in, OFF_GS, 2, evac="a")
    plain("bs", a["w_br_ssm"], 0, 2, 16, evac="v")
    plain("mix", a["w_mix_out"], 0, 2)
    plain("xk", a["w_xkv"], 0, 2)
    plain("xv", a["w_xkv"], 1024, 2)
    plain("xq", a["w_xq"], 0, 2)
    plain("xo", a["w_xo"], 0, 2)
    for i in range(11):
        group(f"gu{i}", a["w_gu"], [(256 * i, 256 * i + 256, 0), (FFN + 256 * i, FFN + 256 * i + 256, 256)])
        plain_at("ada", a["w_ada_2"], i)
    plain_at("ada", a["w_ada_2"], 11)
    plain("dn", a["w_down"], 0, 2, KF)
    group("in0", w_in2, [(OFF2_AQ, OFF2_AQ + 512, 0)])
    group("in1", w_in2, [(OFF2_AK, OFF2_AK + 512, 0)])
    group("in2", w_in2, [(OFF2_GK, OFF2_GK + 256, 0), (OFF2_AK + 64, OFF2_AK + 128, 256), (OFF2_AK, OFF2_AK + 64, 320),
                         (OFF2_GLR, OFF2_GLR + 16, 384)])
    group("in3", w_in2, [(OFF2_GV, OFF2_GV + 512, 0)])
    group("in4", w_in2, [(OFF2_GG, OFF2_GG + 512, 0)])
    plain("out", a["w_out_2"], 0, 2)
    plain("pq", a["peer_wq_2"], 0, 4)
    return groups, chunks


def build_program(nc, a, out):
    from contextlib import ExitStack

    GROUPS, CHUNKS = weight_stream(a)
    G = {name: g for g, (name, *_) in enumerate(GROUPS)}
    acc_before = [sum(x[3] for x in GROUPS[:g]) for g in range(len(GROUPS) + 1)]
    act_evacs = [sum("a" in x[4] for x in GROUPS[:g]) for g in range(len(GROUPS) + 1)]
    dve_evacs = [sum("v" in x[4] for x in GROUPS[:g]) for g in range(len(GROUPS) + 1)]
    last_of_group = {x[2]: g for g, x in enumerate(GROUPS)}
    landed_count = [16 * sum(len(CHUNKS[m][3]) for m in range(n % WSLOTS, n + 1, WSLOTS)) for n in range(len(CHUNKS))]
    open_chunks_before = [sum(m not in last_of_group for m in range(n)) for n in range(len(CHUNKS) + 1)]

    with ExitStack() as ctx:
        def sem(name):
            return ctx.enter_context(nc.semaphore(name))

        CONST = 16512
        WRAW = CONST + 10 * KB
        WHI = WRAW + 16 * KB
        WLO = WHI + 16 * KB
        XRES = WLO + 16 * KB
        HA = XRES + 16 * KB
        HB = HA + 16 * KB
        M = HB + 16 * KB
        A = M + 16 * KB
        TT = A + 48 * KB

        def at(name, base, off_kb, shape, dt=F32):
            return nc.alloc_sbuf_tensor_at(name, shape, dt, offset=base + int(off_kb * KB))

        cst = at("cst", CONST, 0, [P, C_END])
        vec = at("vec", CONST, 7.625, [P, V_END])
        row = at("row", CONST, 8.625, [P, R_END + 24])
        stat = at("stat", CONST, 9.125, [P, 216])
        newt = stat[:, 184:216].rearrange("p (a n) -> p a n", a=2)
        assert C_END * 4 <= 7.625 * KB and V_END * 4 <= KB and R_END + 24 <= 128
        ident = cst[:, C_IDENT:C_IDENT + P]
        ssq = stat[:, 0:4]
        meps = stat[:, 4:8]
        rstd = stat[:, 8:12]
        ssqy = stat[:, 16:32]
        mepsy = stat[:, 32:48]
        rstdy = stat[:, 48:64]
        smx = stat[:, 64:72]
        snm = stat[:, 72:80]
        ssum = stat[:, 80:88]
        ssk = stat[:, 88:96]
        sden = stat[:, 96:104]
        srec = stat[:, 104:112]

        wraw = at("wraw", WRAW, 0, [P, WSLOTS, WK, 512])
        whi = at("whi", WHI, 0, [P, WSLOTS, WK, 512], F32R)
        wlo = at("wlo", WLO, 0, [P, WSLOTS, WK, 512], F32R)
        x_res = at("x_res", XRES, 0, [P, NT, D])
        hhi = at("hhi", HA, 0, [P, KD, T], F32R)
        hlo = at("hlo", HB, 0, [P, KD, T], F32R)
        u_out = at("u_out", HA, 0, [P, NT, D])
        xn = at("xn", TT, 16, [P, NT, D])
        grow = at("grow", TT, 32, [P, D])
        q_t = at("q_t", A, 0, [P, KD, T])
        k_t = at("k_t", A, 16, [P, KD, T])
        v_s = at("v_s", A, 32, [P, NT, D])
        ohi = at("ohi", A, 0, [P, KD, T], F32R)
        olo = at("olo", M, 0, [P, KD, T], F32R)
        sb_l = at("sb_l", TT, 0, [P, 2, 1280])
        sb_p = at("sb_p", TT, 10, [P, 2, 1280])
        sb_w = at("sb_w", TT, 20, [P, 2, 1280])
        attbr = at("attbr", A, 16, [P, KD, T])
        gate_a = at("gate_a", TT, 0, [P, KD, T])
        merged = at("merged", M, 0, [P, KD, T])
        xs = at("xs", A, 0, [P, NT, SSM_INNER])
        b_t = at("b_t", A, 32, [P, SSM_GROUPS, T])
        c_t = at("c_t", A, 40, [P, SSM_GROUPS, T])
        raw = at("raw", TT, 0, [P, 4, 515])
        cacc = at("cacc", TT, 8.25, [P, 4, T])
        xst = at("xst", TT, 16.25, [P, 4, T])
        segl = at("segl", TT, 0, [P, 2, 8, P])
        dec = at("dec", TT, 8, [P, 2, 8, P])
        xd = at("xd", TT, 16, [P, 2, 8, SSM_P])
        xe = at("xe", TT, 20, [P, 2, 8, SSM_P])
        ysum = at("ysum", TT, 24, [P, 2, 8, SSM_P])
        state = at("state", TT, 28, [P, 512])
        btok = at("btok", TT, 30, [P, 2, P])
        cbm = at("cbm", TT, 31, [P, 2, P])
        dtt = at("dtt", TT, 32, [P, NT, 32])
        adt = at("adt", TT, 32.5, [P, NT, 32])
        eacs = at("eacs", TT, 33, [P, NT, 32])
        dtw = at("dtw", TT, 33.5, [P, NT, 32])
        ecd = at("ecd", TT, 34, [P, NT, 32])
        dta = at("dta", TT, 34.5, [P, NT, 32])
        dtb = at("dtb", TT, 35, [P, NT, 32])
        dt_t = at("dt_t", TT, 35.5, [P, T])
        nega = stat[:, 120:152]
        ztmp = at("ztmp", TT, 0, [P, 2, 4, 512])
        gate_s = at("gate_s", TT, 16, [P, KD, T])
        yhi = at("yhi", A, 0, [P, NT, SSM_INNER], F32R)
        ylo = at("ylo", HA, 0, [P, 16, T], F32R)
        mem_s = at("mem_s", TT, 24, [P, 2, D])
        mem_n = at("mem_n", TT, 16, [P, 2, D])
        mhi = at("mhi", A, 32, [P, KD, MEM], F32R)
        mlo = at("mlo", A, 40, [P, KD, MEM], F32R)
        kx = at("kx", A, 16, [P, KD, MEM])
        vx = at("vx", A, 24, [P, 2, D])
        qx = at("qx", A, 32, [P, KD, T])
        px = at("px", TT, 16, [P, 2, 4, MEM])
        ptx = at("ptx", TT, 0, [P, 8, T])
        guhi = at("guhi", M, 0, [P, KF, T], F32R)
        gulo = at("gulo", M, 44, [P, KF, T], F32R)
        gtmp = at("gtmp", TT, 24, [P, 2, 2, T])
        gate1 = at("gate1", M, 0, [P, D])
        gate2 = at("gate2", M, 4, [P, D])
        modx = at("modx", TT, 32, [P, 4, P])
        gdiag = at("gdiag", TT, 0, [P, 2, KD, P])
        chi = at("chi", CONST, 9.125 + 448 / KB, [P, KD], F32R)
        clo = at("clo", CONST, 10 - 32 / KB, [P, KD], F32R)
        modc = stat[:, 136:184]
        csil = row[:, R_END:R_END + 8]
        haff = at("haff", TT, 0, [P, KD, T])
        aq_t = at("aq_t", A, 0, [P, 4, T])
        ak_t = at("ak_t", A, 8, [P, T])
        ak_x = at("ak_x", A, 10, [P, T])
        av_t = at("av_t", A, 12, [P, T])
        av_s = at("av_s", A, 14, [P, NT, P])
        gq_t = at("gq_t", A, 16, [P, 2, T])
        gk_t = at("gk_t", A, 20, [P, 2, T])
        gv_s = at("gv_s", A, 24, [P, NT, 512])
        gg_s = at("gg_s", A, 32, [P, NT, 512])
        glr_t = at("glr_t", A, 40, [32, T])
        gup = at("gup", A, 42, [17, 256])
        la_t = at("la_t", A, 43, [P, 2, T])
        sw_ss = (at("sw_s", TT, 0, [P, SW_HEADS, 2 * P]), at("sw_s1", TT, 16, [P, SW_HEADS, 2 * P]))
        sw_stats = (stat[:, 64:96], stat[:, 16:48])
        sw_pt = at("sw_pt", TT, 8, [P, 16, P])
        b_cs = at("b_cs", TT, 0, [P, 2, T])
        gl_d = at("gl_d", TT, 4, [P, 2, T])
        gl_q = at("gl_q", TT, 8, [P, 2, T])
        gl_k = at("gl_k", TT, 12, [P, 2, T])
        gl_ds = (gl_d, at("gl_d1", HB, 8, [P, 2, T]))
        gl_qs = (gl_q, at("gl_q1", HA, 8, [P, 2, T]))
        gl_ks = (gl_k, at("gl_k1", HA, 12, [P, 2, T]))
        gl_a = at("gl_a", TT, 16, [P, GLA_HEADS, NT, P])
        gl_ms = [at(f"gl_m{h}", base, off, [P, NT, P]) for h, (base, off) in enumerate(((TT, 24), (TT, 26), (HB, 12), (HB, 14)))]
        q_in = at("q_in", M, 8, [P, 2, T])
        k_out = at("k_out", M, 12, [P, 2, T])
        k_tok = at("k_tok", TT, 28, [P, NT, 2 * P])
        g_st = at("g_st", TT, 32, [P, 2, P])
        g_dl = at("g_dl", TT, 33, [P, 2, NT])
        ssg = at("ssg", TT, 33.25, [P, 16])
        mpg = at("mpg", TT, 33.5, [P, 16])
        rsg = at("rsg", TT, 33.75, [P, 16])
        go_q = at("go_q", TT, 8, [P, NT, 512])
        go_s = at("go_s", TT, 0, [P, NT, 512])
        u2 = at("u2", TT, 0, [P, NT, D])
        pq_t = at("pq_t", A, 0, [P, 16, T])
        h2_s = at("h2_s", A, 32, [P, NT, D])
        rows = at("rows", HA, 0, [P, RING, D])
        sc = at("sc", TT, 0, [P, 16 * NKEYS])
        diag = at("diag", WRAW, 8, [P, RING, P])
        vacc = at("vacc", WLO, 4, [P, 3, D])
        hid = at("hid", TT, 8, [P, SLOTS])
        hidg = at("hidg", TT, 8.5, [P, SLOTS])
        hidv = at("hidv", TT, 9, [P, SLOTS])
        gatev = at("gatev", TT, 9.5, [P, SLOTS])
        gatee = at("gatee", TT, 10, [P, SLOTS])
        gates = at("gates", TT, 10.5, [P, SLOTS])
        expert = at("expert", TT, 11, [P, 2 * SLOTS], U32)
        tk_s = at("tk_s", TT, 12, [P, 2, NKEYS])
        tk_r = at("tk_r", TT, 13, [P, 2, NKEYS])
        cand = at("cand", TT, 14, [P, TOPK, TOPK])
        cand_r = at("cand_r", TT, 15, [P, TOPK, TOPK])
        onehot = at("onehot", TT, 33.5, [P, 2, TOPK, TOPK])
        zeros = at("zeros", WRAW, 0, [P, P])
        small = TT + 32 * KB
        tv = at("tv", small, 0, [P, 2, TOPK])
        ti = at("ti", small, 0.125, [P, 2, TOPK], U32)
        tif = at("tif", small, 0.25, [P, 2, TOPK])
        bv = at("bv", small, 0.375, [P, TOPK])
        bp = at("bp", small, 0.4375, [P, TOPK], U32)
        bij = at("bij", small, 0.5, [P, 2, TOPK], U32)
        bijf = at("bijf", small, 0.625, [P, 2, TOPK])
        pick_f = at("pick_f", small, 0.75, [P, 2, TOPK])
        expf = at("expf", small, 0.875, [P, TOPK])
        hidu = at("hidu", small, 1, [P, RING])
        hidw = at("hidw", small, 1.0625, [P, RING])
        hidd = at("hidd", small, 1.125, [P, 2, 4])
        idxw = at("idxw", small, 1.25, [P, 2, RING], U32)
        gsum = at("gsum", small, 1.375, [P, PEER_HEADS])
        grec = at("grec", small, 1.4375, [P, PEER_HEADS])
        subk = at("subk", TT, 16, [P, 16, NKEYS])
        peer_g = at("peer_g", TT, 24, [P, D])
        gfin = at("gfin", TT, 28, [P, D])

        ps = ctx.enter_context(nc.psum_tensor("ps", [P, 8, 512], F32))

        def b4(bank, n=4):
            return ps[:, bank, :].rearrange("p (n c) -> p n c", n=n)

        consts_landed = sem("consts_landed")
        x_landed = sem("x_landed")
        landed = [sem(f"w_landed{j}") for j in range(WSLOTS)]
        w_hi = sem("w_hi")
        w_lo = sem("w_lo")
        w_used = sem("w_used")
        acc_ready = sem("acc_ready")
        act_evac = sem("act_evac")
        dve_evac = sem("dve_evac")
        dve_step = sem("dve_step")
        act_step = sem("act_step")
        sq_ready = sem("sq_ready")
        xn_ready = sem("xn_ready")
        tr_ready = sem("tr_ready")
        h_hi = sem("h_hi")
        h_ready = sem("h_ready")
        usq_ready = sem("usq_ready")
        x_ready = sem("x_ready")
        grow_landed = sem("grow_landed")
        z_ready = sem("z_ready")
        l_ready = sem("l_ready")
        sp_ready = sem("sp_ready")
        sp_masked = sem("sp_masked")
        tail_ready = sem("tail_ready")
        w_ready = sem("w_ready")
        w_masked = sem("w_masked")
        o_ready = sem("o_ready")
        o_hi = sem("o_hi")
        o_lo = sem("o_lo")
        root_in = sem("root_in")
        root_out = sem("root_out")
        row_landed = [sem(f"row_landed{j}") for j in range(RING)]
        row_used = [sem(f"row_used{j}") for j in range(RING)]
        S = {}

        def s(name):
            if name not in S:
                S[name] = sem(name)
            return S[name]

        def used(eng, n):
            if n in last_of_group:
                eng.wait_ge(acc_ready, acc_before[last_of_group[n] + 1])
            else:
                eng.wait_ge(w_used, open_chunks_before[n + 1])

        def acc_wait(eng, g, j):
            eng.wait_ge(acc_ready, acc_before[g] + j + 1)

        block = ctx.enter_context(nc.Block())
        NCHUNK = len(CHUNKS)

        def sync_program(sp):
            sp.dma_start(x_res[:], a["x"][0].rearrange("(i p) d -> p i d", p=P)).then_inc(x_landed, 16)
            sp.dma_start(cst[:], a["cst"]).then_inc(consts_landed, 16)
            sp.dma_start(vec[:], a["vec"]).then_inc(consts_landed, 16)
            sp.dma_start(row[:, 0:R_END], a["row"].broadcast_to((P, R_END))).then_inc(consts_landed, 16)
            for n in range(NCHUNK):
                _, _, kn, segments = CHUNKS[n]
                if n >= WSLOTS:
                    sp.wait_ge(w_lo, n - WSLOTS + 1)
                for src, dst, width in segments:
                    sp.dma_start(wraw[:, n % WSLOTS, 0:kn, dst:dst + width], src).then_inc(landed[n % WSLOTS], 16)
            for i in range(NT):
                sp.wait_ge(s("out_ready"), i + 1)
                sp.dma_start(out[0].rearrange("(i p) d -> p i d", p=P)[:, i, :], h2_s[:, i, :]).then_inc(s("out_stored"), 16)
            sp.wait_ge(s("out_stored"), 16 * NT)

        def scalar_program(act):
            steps = [0]
            rounded = [0]

            def link(ins):
                steps[0] += 1
                ins.then_inc(act_step, 1)
                act.wait_ge(act_step, steps[0])

            def round_upto(n_last):
                while rounded[0] <= min(n_last, NCHUNK - 1):
                    n = rounded[0]
                    kn = CHUNKS[n][2]
                    act.wait_ge(landed[n % WSLOTS], landed_count[n])
                    if n >= WSLOTS:
                        used(act, n - WSLOTS)
                    act.activation(whi[:, n % WSLOTS, 0:kn, :], wraw[:, n % WSLOTS, 0:kn, :], ACT.Copy).then_inc(w_hi, 1)
                    rounded[0] += 1

            def group(g, jobs, evac):
                round_upto(GROUPS[g][2] + WSLOTS)
                for j in jobs:
                    acc_wait(act, g, j)
                    ins = evac(j, 4 * (g % 2) + j)
                ins.then_inc(act_evac, 1)

            def to_features(dst, base_tile, scale=1.0, n=T):
                return lambda j, bank: act.activation(dst[:, base_tile + j, :], ps[:, bank, 0:n], ACT.Copy, scale=scale)

            def to_tokens(dst, half):
                return lambda j, bank: act.activation(dst[:, j, 512 * half:512 * half + 512], ps[:, bank, :], ACT.Copy)

            roots = [0]

            def root(mid):
                roots[0] += 1
                act.wait_ge(root_in, roots[0])
                act.activation(newt[:, 1, 0:mid.shape[-1]], mid, ACT.Sqrt).then_inc(root_out, 1)

            def rms_squares(r):
                for i in range(NT):
                    if r > 0:
                        act.wait_ge(x_ready, NT * (r - 1) + i + 1)
                    if i > 0:
                        act.wait_ge(sq_ready, NT * r + i)
                    else:
                        act.wait_ge(xn_ready, NT * r) if r else None
                    act.activation(xn[:, 0, :], x_res[:, i, :], ACT.Square, accum_out=ssq[:, i:i + 1]).then_inc(sq_ready, 1)
                root(meps)

            def rms_round(r, gain):
                for k in range(KD):
                    act.wait_ge(tr_ready, KD * r + k + 1)
                    act.activation(hhi[:, k, :], ps[:, k, :], ACT.Copy, scale=vec[:, gain + k:gain + k + 1]).then_inc(h_hi, 1)

            def sublayer_squares(r, u):
                for i in range(NT):
                    if i > 0:
                        act.wait_ge(usq_ready, NT * r + i)
                    act.activation(xn[:, 0, :], u[:, i, :], ACT.Square, accum_out=ssq[:, i:i + 1]).then_inc(usq_ready, 1)
                root(meps)

            act.wait_ge(x_landed, 16)
            rms_squares(0)
            round_upto(WSLOTS - 1)
            act.wait_ge(consts_landed, 48)
            rms_round(0, V_PRE)
            for i in range(2):
                group(G[f"q{i}"], (0, 1), to_features(q_t, 4 * i, SB_DIM ** -0.5))
            for i in range(2):
                group(G[f"k{i}"], (0, 1), to_features(k_t, 4 * i))
            for i in range(2):
                group(G[f"v{i}"], (0, 1), to_tokens(v_s, i))
            act.preload_act_table_set("natural_log_exp_and_others")

            def log_part(h):
                zb = 3 * (h % 2)
                act.wait_ge(z_ready, h + 1)
                if h >= 2:
                    act.wait_ge(sp_ready, h - 1)
                act.activation(sb_l[:, h % 2, 0:512], ps[:, zb, :], ACT.Abs)
                act.activation(sb_l[:, h % 2, 512:1024], ps[:, zb + 1, :], ACT.Abs)
                link(act.activation(sb_l[:, h % 2, 1024:1280], ps[:, zb + 2, 0:256], ACT.Abs))
                link(act.activation(sb_l[:, h % 2, :], sb_l[:, h % 2, :], ACT.Exp, scale=-1.0))
                act.activation(sb_l[:, h % 2, :], sb_l[:, h % 2, :], ACT.Ln, bias=1.0).then_inc(l_ready, 1)

            def weights_part(h):
                zb = 3 * (h % 2)
                act.wait_ge(tail_ready, h + 1)
                act.activation(sb_w[:, h % 2, 0:512], ps[:, zb, :], ACT.Exp)
                act.activation(sb_w[:, h % 2, 512:1024], ps[:, zb + 1, :], ACT.Exp)
                act.activation(sb_w[:, h % 2, 1024:1280], ps[:, zb + 2, 0:256], ACT.Exp).then_inc(w_ready, 1)

            def round_heads(hp):
                act.wait_ge(o_ready, 2 * hp + 2)
                act.activation(ohi[:, hp, :], ps[:, 6 + hp % 2, :], ACT.Copy).then_inc(o_hi, 1)

            log_part(0)
            for h in range(SB_HEADS):
                if h + 1 < SB_HEADS:
                    log_part(h + 1)
                weights_part(h)
                if h >= 2 and h % 2 == 0:
                    round_heads(h // 2 - 1)
            round_heads(7)
            for i in range(2):
                group(G[f"br{i}"], (0, 1), to_features(attbr, 4 * i))
            for i in range(2):
                group(G[f"ga{i}"], range(4), lambda j, bank: act.activation(gate_a[:, 4 * i + j, :], ps[:, bank, :], ACT.Sigmoid))

            def silu_tiles(f):
                dst = [xst, xst, xst, xst, b_t, c_t][f]
                for j in range(4):
                    act.wait_ge(s("conv_ready"), 4 * f + j + 1)
                    if 1 <= f < 4:
                        act.wait_ge(s("xtr_ready"), 4 * f)
                    act.activation(dst[:, j, :], cacc[:, j, :], ACT.Silu, bias=vec[:, V_CB + 4 * f + j:V_CB + 4 * f + j + 1]).then_inc(s("xs_ready"), 1)

            def x_tokens(f):
                for j in range(2):
                    act.wait_ge(s("xtr_ready"), 4 * f + j + 1)
                    act.activation(xs[:, :, P * (4 * f + j):P * (4 * f + j + 1)], b4(4 * (G[f"xbc{f}"] % 2) + j), ACT.Copy).then_inc(s("xtok_ready"), 1)

            for f in range(6):
                if f == 0:
                    act.wait_ge(s("merged_done"), 8)

                def copy_raw(j, bank):
                    if f >= 1:
                        act.wait_ge(s("conv_ready"), 4 * f)
                    return act.activation(raw[:, j, 3:515], ps[:, bank, :], ACT.Copy)
                if 1 <= f <= 4:
                    round_upto(GROUPS[G[f"xbc{f}"]][2] + WSLOTS - 2)
                    x_tokens(f - 1)
                group(G[f"xbc{f}"], range(4), copy_raw)
                silu_tiles(f)
            group(G["dt"], (0,), lambda j, bank: act.activation(dt_t[:, :], ps[:, bank, :], ACT.Copy))

            act.preload_act_table_set("natural_log_exp_and_others")
            act.activation(nega, row[:, R_ALOG:R_ALOG + 32], ACT.Exp).then_inc(s("dt_act"), 1)
            act.wait_ge(s("dt_dve"), 1)
            link(act.activation(dtb[:], dta[:], ACT.Abs))
            link(act.activation(dtb[:], dtb[:], ACT.Exp, scale=-1.0))
            act.activation(dtb[:], dtb[:], ACT.Ln, bias=1.0).then_inc(s("dt_act"), 1)
            act.wait_ge(s("acs_ready"), 1)
            act.activation(eacs[:], b4(5)[:, :, 0:32], ACT.Exp)
            act.activation(ecd[:], b4(5)[:, :, 32:64], ACT.Exp)
            act.activation(dta[:], b4(5)[:, :, 32:64], ACT.Copy).then_inc(s("dt_act"), 1)
            act.wait_ge(s("dt_dve"), 3)
            act.activation(dtb[:], dtb[:], ACT.Exp).then_inc(s("dt_act"), 1)
            for u in range(16):
                act.wait_ge(s("cb_ready"), u + 1)
                if u >= 2:
                    act.wait_ge(s("y_mm"), u - 1)
                act.activation(btok[:, u % 2, :], ps[:, 4, P:2 * P], ACT.Copy).then_inc(s("btok_ready"), 1)
                act.wait_ge(s("seg_ready"), u + 1)
                act.activation(dec[:, u % 2, 0:4, :], b4(2 * (u % 2)), ACT.Exp)
                act.activation(dec[:, u % 2, 4:8, :], b4(2 * (u % 2) + 1), ACT.Exp).then_inc(s("dec_ready"), 1)
            act.wait_ge(s("y_done"), 16)
            for i in range(4):
                def gate_z(j, bank):
                    if i >= 2:
                        act.wait_ge(s("yz_done"), 4 * (i - 1))
                    return act.activation(ztmp[:, i % 2, j, :], ps[:, bank, :], ACT.Silu)
                group(G[f"z{i}"], range(4), gate_z)
            def gates_s(i):
                group(G[f"gs{i}"], range(4), lambda j, bank: act.activation(gate_s[:, 4 * i + j, :], ps[:, bank, :], ACT.Sigmoid))

            gates_s(0)
            root(mepsy)
            act.wait_ge(s("rstdy_ready"), 1)
            for n in range(0, 16, 2):
                i, g = n % 4, n // 4
                ysl = xs[:, i, 512 * g:512 * g + 512]
                act.activation(ysl, ysl, ACT.Copy, scale=rstdy[:, n:n + 1]).then_inc(s("ysc_ready"), 1)
            gates_s(1)
            for f in range(16):
                act.wait_ge(s("ytr_ready"), f + 1)
                act.activation(yhi[:, :, P * f:P * f + P], b4(f % 8), ACT.Copy, scale=vec[:, V_SSM + f:V_SSM + f + 1]).then_inc(s("yhi_ready"), 1)
            round_upto(GROUPS[G["bs1"]][2] + WSLOTS)
            for k in range(KD):
                act.wait_ge(s("merged_s"), k + 1)
                if k == 0:
                    acc_wait(act, G["bs1"], 3)
                act.activation(ohi[:, k, :], merged[:, k, :], ACT.Copy).then_inc(o_hi, 1)
            act.dma_start(mem_s[:], a["mem"][0].rearrange("(i p) d -> p i d", p=P)).then_inc(s("vectors_landed"), 16)
            act.wait_ge(s("vectors_landed"), 16)
            for i in range(2):
                if i:
                    act.wait_ge(s("msq_ready"), 1)
                act.activation(mem_n[:, 0, :], mem_s[:, i, :], ACT.Square, accum_out=ssq[:, i:i + 1]).then_inc(s("msq_ready"), 1)
            root(meps[:, 0:2])
            act.dma_start(grow[:], a["g_post_mix"].broadcast_to((P, D))).then_inc(grow_landed, 16)
            for i in range(2):
                group(G[f"mix{i}"], (0, 1), to_tokens(u_out, i))
            for k in range(KD):
                act.wait_ge(s("mtr_ready"), k + 1)
                act.activation(mhi[:, k, :], ps[:, k, 0:MEM], ACT.Copy, scale=vec[:, V_MEM + k:V_MEM + k + 1]).then_inc(s("m_hi"), 1)
            act.wait_ge(dve_evac, dve_evacs[G["mix1"] + 1])
            act.wait_ge(act_evac, act_evacs[G["mix1"] + 1])
            sublayer_squares(0, u_out)
            rms_squares(1)
            for i in range(2):
                group(G[f"xk{i}"], (0, 1), to_features(kx, 4 * i, n=MEM))
            for i in range(2):
                group(G[f"xv{i}"], (0, 1), lambda j, bank: act.activation(vx[:, j // 2, 512 * i + 256 * (j % 2):512 * i + 256 * (j % 2) + 256], ps[:, bank, 0:256], ACT.Copy))
            rms_round(1, V_XA)
            for i in range(2):
                group(G[f"xq{i}"], (0, 1), to_features(qx, 4 * i, XA_DIM ** -0.5))
            for i in range(NT):
                act.wait_ge(s("xmax_ready"), i + 1)
                if i >= 2:
                    act.wait_ge(s("ptr_ready"), 2 * (i - 1))
                for h in range(XA_HEADS):
                    act.activation(px[:, i % 2, h, :], ps[:, 2 * (i % 2) + h // 2, 256 * (h % 2):256 * (h % 2) + 256], ACT.Exp,
                                   bias=snm[:, 4 * (i % 2) + h:4 * (i % 2) + h + 1], accum_out=ssum[:, 4 * (i % 2) + h:4 * (i % 2) + h + 1]).then_inc(s("pexp_ready"), 1)
                act.wait_ge(s("ptr_ready"), 2 * i + 1)
                act.activation(ptx[:, 0:4, P * i:P * i + P], b4(4 + 2 * (i % 2)), ACT.Copy).then_inc(s("pt_act"), 1)
            for d in range(0, KD):
                act.wait_ge(s("ox_ready"), d + 1)
                act.activation(ohi[:, d, :], ps[:, d, :], ACT.Copy).then_inc(o_hi, 1)
            act.dma_start(grow[:], a["g_post_xa"].broadcast_to((P, D))).then_inc(grow_landed, 16)
            for i in range(2):
                group(G[f"xo{i}"], (0, 1), to_tokens(u_out, i))
            act.wait_ge(dve_evac, dve_evacs[G["xo1"] + 1])
            act.wait_ge(act_evac, act_evacs[G["xo1"] + 1])
            sublayer_squares(1, u_out)
            rms_squares(2)
            rms_round(2, V_FFN)
            link(act.activation(csil, vec[:, V_C:V_C + KD], ACT.Silu))
            act.activation(chi[:], csil, ACT.Copy).then_inc(s("c_ready"), 1)

            def round_gu(f):
                for j in range(2):
                    act.wait_ge(dve_evac, dve_evacs[G[f"gu{f}"] + 1])
                    act.activation(guhi[:, 2 * f + j, :], gtmp[:, f % 2, j, :], ACT.Copy).then_inc(s("gu_hi"), 1)

            for f in range(11):
                def gate_up(j, bank):
                    if f >= 2:
                        act.wait_ge(s("gu_lo"), 2 * (f - 1))
                    return act.activation(gtmp[:, f % 2, j, :], ps[:, bank, :], ACT.Silu)
                group(G[f"gu{f}"], (0, 1), gate_up)
                round_upto(GROUPS[G[f"ada{f}"]][2] + 2)
                round_gu(f)
                round_upto(GROUPS[G[f"ada{f}"]][2] + WSLOTS)
            round_upto(GROUPS[G["ada11"]][2] + WSLOTS)
            for i in range(2):
                group(G[f"dn{i}"], (0, 1), to_tokens(u_out, i))
                if i == 0:
                    act.wait_ge(s("mod_done"), 1)
                    act.dma_start(grow[:], a["g_post_ffn"].broadcast_to((P, D))).then_inc(grow_landed, 16)
            act.wait_ge(dve_evac, dve_evacs[G["dn1"] + 1])
            act.wait_ge(act_evac, act_evacs[G["dn1"] + 1])
            sublayer_squares(2, u_out)
            rms_squares(3)
            for k in range(KD):
                act.wait_ge(s("aff_ready"), k + 1)
                act.activation(hhi[:, k, :], haff[:, k, :], ACT.Copy).then_inc(h_hi, 1)
            group(G["in0"], (0, 1), to_features(aq_t, 0, 0.125))
            group(G["in1"], (0, 1), lambda j, bank: act.activation([ak_t, av_t][j][:, :], ps[:, bank, :], ACT.Copy))
            group(G["in2"], (0, 1), to_features(gk_t, 0))
            group(G["in3"], (0, 1), to_tokens(gv_s, 0))
            group(G["in4"], (0, 1), to_tokens(gg_s, 0))
            for n in range(4):
                act.wait_ge(s("gates_mm"), n + 1)
                act.activation((gate1, gate2)[n // 2][:, 512 * (n % 2):512 * (n % 2) + 512], ps[:, 4 + n, :], ACT.Copy).then_inc(s("gates_done"), 1)
            act.preload_act_table_set("natural_log_exp_and_others")

            def sw_exp(b):
                lo = P if b == 0 else 0
                sw, st = sw_ss[b % 2], sw_stats[b % 2]
                act.wait_ge(s("sw_max"), b + 1)
                for h in range(SW_HEADS):
                    act.activation(sw[:, h, lo:], sw[:, h, lo:], ACT.Exp, bias=st[:, 8 + h:9 + h], accum_out=st[:, 16 + h:17 + h])
                act.activation(st[:, 24:32], st[:, 24:32], ACT.Exp).then_inc(s("sw_exp"), 1)

            sw_exp(0)
            for b in range(NT):
                if b + 1 < NT:
                    sw_exp(b + 1)
                for n in range(4):
                    if n % 2 == 0:
                        act.wait_ge(s("sw_tr"), 4 * b + n + 1)
                        if b > 0 and n == 0:
                            act.wait_ge(s("sw_o"), b)
                        m = slice(1, 4, 2) if b == 0 else slice(0, 4)
                        act.activation(sw_pt[:, 4 * n:4 * n + 4, :][:, m, :], b4(4 + n)[:, m, :], ACT.Copy).then_inc(s("sw_pta"), 1)
                act.wait_ge(s("sw_o"), b + 1)
                act.activation(hhi[:, 0:4, P * b:P * b + P], b4(4), ACT.Copy).then_inc(s("sw_ohi"), 1)
            act.dma_start(gup[:], a["gup"]).then_inc(s("vectors_landed"), 16)
            act.wait_ge(s("la_ready"), 1)
            for t2 in range(2):
                act.activation(gl_d[:, t2, :], ps[:, t2, :], ACT.Copy, scale=-1.0)
            act.activation(la_t[:, 0, :], ps[:, 0, :], ACT.Abs)
            link(act.activation(la_t[:, 1, :], ps[:, 1, :], ACT.Abs))
            link(act.activation(la_t[:], la_t[:], ACT.Exp, scale=-1.0))
            act.activation(la_t[:], la_t[:], ACT.Ln, bias=1.0).then_inc(s("gla_act"), 1)
            act.wait_ge(s("bcs_ready"), 8)
            act.activation(gl_q[:], b_cs[:], ACT.Exp).then_inc(s("gla_act"), 1)
            act.wait_ge(s("bd_ready"), 1)
            act.activation(gl_k[:], gl_d[:], ACT.Exp).then_inc(s("gla_act"), 1)
            act.activation(g_dl[:], b_cs[:, :, P - 1::P], ACT.Exp).then_inc(s("gla_act"), 1)
            for lv in range(LEVELS):
                act.wait_ge(s("gd_ready"), lv + 1)
                d = gl_ds[lv % 2]
                link(act.activation(d[:], d[:], ACT.Abs))
                act.activation(d[:], d[:], ACT.Exp, scale=-1.0).then_inc(s("gdec_ready"), 1)
            for c in range(NT):
                act.wait_ge(s("ktr_ready"), c + 1)
                act.activation(k_tok[:, c, :], ps[:, 4 + c, 0:256], ACT.Copy).then_inc(s("ktok_ready"), 1)
            act.activation(gg_s[:], gg_s[:], ACT.Silu).then_inc(s("sgg_ready"), 1)
            root(mpg[:])
            for f in range(4):
                act.wait_ge(s("gotr_ready"), f + 1)
                act.activation(hhi[:, 4 + f, :], ps[:, f, :], ACT.Copy, scale=vec[:, V_GLAN:V_GLAN + 1]).then_inc(s("go_hi"), 1)
            for i in range(2):
                group(G[f"out{i}"], (0, 1), to_tokens(u2, i))
            rms_squares(4)
            for k in range(KD):
                act.wait_ge(s("aff_ready"), KD + k + 1)
                act.activation(hhi[:, k, :], haff[:, k, :], ACT.Copy).then_inc(h_hi, 1)
            for i in range(0, 4):
                act.wait_ge(s("back_ready"), 2 * i + 1)
                act.activation(h2_s[:, i, 0:512], ps[:, 2 * i, :], ACT.Copy).then_inc(s("h2_ready"), 1)
            act.dma_start(subk[:], a["subk"]).then_inc(s("vectors_landed"), 16)
            act.dma_start(gfin[:], a["g_final"].broadcast_to((P, D))).then_inc(s("vectors_landed"), 16)
            for i in range(4):
                group(G[f"pq{i}"], (0, 1), to_features(pq_t, 4 * i))
                act.wait_ge(s("subs_mm"), i + 1)
                act.activation(sc[:, 512 * i:512 * i + 512], ps[:, 4 * (G[f"pq{i}"] % 2), :], ACT.Copy).then_inc(s("sc_ready"), 1)

            def scores_out(t):
                act.wait_ge(s("head_done"), PEER_HEADS * t)
                act.wait_ge(s("subs_mm"), t + 4)
                for n in range(4):
                    ins = act.activation(sc[:, 512 * n:512 * n + 512], ps[:, 4 + n, :], ACT.Copy)
                ins.then_inc(s("sc_ready"), 1)

            for t in range(NT):
                if t + 1 < NT:
                    scores_out(t + 1)
                act.wait_ge(s("head_done"), PEER_HEADS * (t + 1))
                act.activation(gatee[:], gatev[:], ACT.Exp).then_inc(s("gate_act"), 1)
                act.wait_ge(s("hid_ready"), ROUNDS * (t + 1))
                act.activation(hidg[:], hid[:], ACT.Gelu).then_inc(s("gate_act"), 1)
                act.wait_ge(s("hidv_ready"), t + 1)
                with act.Fori(0, ROUNDS) as i:
                    act.activation(hidw[:], hidv[:, bass.ts(i, RING)], ACT.Copy).then_inc(s("win_ready"), 1)
                    act.wait_ge(s("win_ready"), i + (ROUNDS * t + 1))
                    for j in PE_SLOTS:
                        act.wait_ge(row_used[j], i + (ROUNDS * (2 * t + 1) + 1))
                        act.activation(diag[:, j, :], ident, ACT.Copy, scale=hidw[:, j:j + 1]).then_inc(s("diag_ready"), 1)
                    act.wait_ge(s("diag_ready"), i * len(PE_SLOTS) + len(PE_SLOTS) * (ROUNDS * t + 1))
            for i in range(NT):
                act.wait_ge(x_ready, NT * 4 + i + 1)
                if i:
                    act.wait_ge(usq_ready, 3 * NT + i)
                act.activation(sc[:, 0:D], x_res[:, i, :], ACT.Square, accum_out=ssq[:, i:i + 1]).then_inc(usq_ready, 1)
            root(meps)

        def gpsimd_program(pool):
            rests = [0]

            def rest_upto(n_last):
                while rests[0] <= min(n_last, NCHUNK - 1):
                    n = rests[0]
                    kn = CHUNKS[n][2]
                    pool.wait_ge(w_hi, n + 1)
                    pool.tensor_tensor(wlo[:, n % WSLOTS, 0:kn, :], wraw[:, n % WSLOTS, 0:kn, :],
                                       whi[:, n % WSLOTS, 0:kn, :].bitcast(F32), ALU.subtract).then_inc(w_lo, 1)
                    rests[0] += 1

            def after(name):
                rest_upto(GROUPS[G[name]][2] + WSLOTS)

            rest_upto(WSLOTS - 1)
            pool.wait_ge(consts_landed, 48)
            after("v1")

            def mask_logs(h):
                pool.wait_ge(sp_ready, h + 1)
                for view, n in ((sb_p[:, h % 2, :].rearrange("p (n c) -> p n c", c=256)[:, 0::2, 0:P], 3), (sb_p[:, h % 2, 896:1024], 1)):
                    pattern = [[0, n], [1, P]] if n > 1 else [[1, P]]
                    pool.affine_select(out=view, in_=view, compare_op=ALU.is_gt, fill=0.0, base=0, pattern=pattern,
                                       channel_multiplier=-1).then_inc(sp_masked, 1)

            def mask_weights(h):
                pool.wait_ge(w_ready, h + 1)
                for view, n in ((sb_w[:, h % 2, :].rearrange("p (n c) -> p n c", c=256)[:, 0::2, 0:P], 3), (sb_w[:, h % 2, 896:1024], 1)):
                    pattern = [[0, n], [1, P]] if n > 1 else [[1, P]]
                    pool.affine_select(out=view, in_=view, compare_op=ALU.is_gt, fill=0.0, base=0, pattern=pattern,
                                       channel_multiplier=-1).then_inc(w_masked, 1)

            mask_logs(0)
            for h in range(SB_HEADS):
                if h + 1 < SB_HEADS:
                    mask_logs(h + 1)
                mask_weights(h)
            after("dt")
            pool.wait_ge(s("dt_dve"), 2)
            pool.wait_ge(s("dt_dve"), 4)
            gt = cst[:, C_GT:C_GT + P]
            for u in range(16):
                g, c = u // 4, u % 4
                if u >= 2:
                    pool.wait_ge(s("seg_ready"), u - 1)
                pool.tensor_tensor(segl[:, u % 2], gt.unsqueeze(1).to_broadcast([P, 8, P]),
                                   adt[:, c, 8 * g:8 * g + 8].unsqueeze(2).to_broadcast([P, 8, P]), ALU.mult).then_inc(s("segl_ready"), 1)
                xg = xs[:, c, 512 * g:512 * g + 512].rearrange("p (e q) -> p e q", e=8)
                if u >= 2:
                    pool.wait_ge(s("y_mm"), u - 1)
                pool.tensor_tensor(xd[:, u % 2], xg, dtt[:, c, 8 * g:8 * g + 8].unsqueeze(2).to_broadcast([P, 8, SSM_P]), ALU.mult)
                pool.tensor_tensor(xe[:, u % 2], xg, dtw[:, c, 8 * g:8 * g + 8].unsqueeze(2).to_broadcast([P, 8, SSM_P]), ALU.mult).then_inc(s("xde_ready"), 1)
                pool.wait_ge(s("xde_ready"), u + 1)
                pool.tensor_tensor(xg, xg, row[:, R_DSK + 8 * g:R_DSK + 8 * g + 8].unsqueeze(2).to_broadcast([P, 8, SSM_P]), ALU.mult).then_inc(s("dx_ready"), 1)
            after("gs0")
            pool.wait_ge(s("rstdy_ready"), 1)
            for n in range(1, 16, 2):
                i, g = n % 4, n // 4
                ysl = xs[:, i, 512 * g:512 * g + 512]
                pool.tensor_scalar(ysl, ysl, rstdy[:, n:n + 1], None, ALU.mult).then_inc(s("ysc_ready"), 1)
            after("bs1")
            after("mix1")
            after("xq1")
            after("xo1")
            after("ada11")
            after("dn1")
            after("in4")
            pool.wait_ge(s("gla_act"), 2)
            pool.tensor_tensor(q_in[:], gl_q[:], gq_t[:], ALU.mult).then_inc(s("qin_ready"), 1)
            pool.wait_ge(s("gla_act"), 3)
            pool.tensor_tensor(k_out[:], gl_k[:], gk_t[:], ALU.mult).then_inc(s("kout_ready"), 1)
            for lv in range(LEVELS):
                pool.wait_ge(s("gdec_ready"), lv + 1)
                if lv >= 2:
                    pool.wait_ge(s("att_ready"), 4 * (lv - 1))
                else:
                    pool.wait_ge(s("qin_ready"), 1)
                pool.tensor_tensor(gl_qs[lv % 2][:], gl_ds[lv % 2][:], gq_t[:], ALU.mult).then_inc(s("glq_ready"), 1)
            after("out1")
            after("pq3")
            for t in range(NT):
                pool.wait_ge(s("head_done"), PEER_HEADS * (t + 1))
                for phase, table in enumerate((a["u"], a["v"])):
                    with pool.Fori(0, ROUNDS // 2) as i:
                        for w in range(2):
                            first = ROUNDS * (2 * t + phase) + w
                            pool.tensor_copy(idxw[:, w, :], expert[:, bass.ds(i * (2 * RING) + (SLOTS * (t % 2) + RING * w), RING)]).then_inc(s("idx_ready"), 1)
                            pool.wait_ge(s("idx_ready"), i * 2 + (first + 1))
                            for j in range(RING):
                                pool.wait_ge(row_used[j], i * 2 + (first + 1))
                                pool.sem_inc(s("waits_pool"), 1)
                                pool.indirect_dma_start(rows[:, j, :], None, table, bass.IndirectOffsetOnAxis(ap=idxw[:, w, j:j + 1], axis=0)).then_inc(row_landed[j], 16)

        def tensor_program(pe):
            def transpose(dst, src):
                return pe.transpose(dst, src, ident)

            def evacuated(name):
                g = G[name]
                pe.wait_ge(act_evac, act_evacs[g + 1])
                pe.wait_ge(dve_evac, dve_evacs[g + 1])

            def project(g, pick, between=None, behind=1):
                name, first, last, jobs, _ = GROUPS[g]
                if g >= 2:
                    pe.wait_ge(act_evac, act_evacs[g - 1])
                    pe.wait_ge(dve_evac, dve_evacs[g - 1])
                ktiles = CHUNKS[last][1] + CHUNKS[last][2]
                for n in range(first, last + 1):
                    _, k0, kn, _ = CHUNKS[n]
                    if between is not None and n == first + behind:
                        between()
                    pe.wait_ge(w_hi, n + 1)
                    pe.wait_ge(w_lo, n + 1)
                    for j in range(jobs):
                        for kk in range(kn):
                            k = k0 + kk
                            lh, ll, rh, rl, dst = pick(j, n % WSLOTS, kk, k)
                            pe.matmul(dst, lh, rh, start=k == 0, stop=False)
                            pe.matmul(dst, lh, rl, start=False, stop=False)
                            ins = pe.matmul(dst, ll, rh, start=False, stop=k == ktiles - 1)
                        if n == last:
                            ins.then_inc(acc_ready, 1)
                    if n != last:
                        ins.then_inc(w_used, 1)

            def features(g, xh, xl, n=T, cols=lambda j: (P * j, P * j + P), between=None, behind=1):
                def pick(j, slot, kk, k):
                    c0, c1 = cols(j)
                    dst = ps[0:c1 - c0, 4 * (g % 2) + j, 0:n]
                    return whi[:, slot, kk, c0:c1], wlo[:, slot, kk, c0:c1], xh(k), xl(k), dst
                project(g, pick, between, behind)

            def tokens(g, xh, xl):
                def pick(j, slot, kk, k):
                    t = slice(P * j, P * j + P)
                    return xh[:, k, t], xl[:, k, t], whi[:, slot, kk, :], wlo[:, slot, kk, :], ps[:, 4 * (g % 2) + j, :]
                project(g, pick)

            hh, hl = (lambda k: hhi[:, k, :]), (lambda k: hlo[:, k, :])
            oh, ol = (lambda k: ohi[:, k, :]), (lambda k: olo[:, k, :])

            def transpose_normed(r):
                pe.wait_ge(xn_ready, NT * (r + 1))
                for k in range(KD):
                    for i in range(NT):
                        ins = transpose(ps[:, k, P * i:P * i + P], xn[:, i, P * k:P * k + P])
                    ins.then_inc(tr_ready, 1)
                pe.wait_ge(h_ready, KD * (r + 1))

            pe.wait_ge(consts_landed, 48)
            transpose_normed(0)
            for name in ("q0", "q1", "k0", "k1"):
                features(G[name], hh, hl)
            for name in ("v0", "v1"):
                tokens(G[name], hhi, hlo)
            evacuated("v1")
            place = [(0, 0, 512), (1, 0, 384), (2, 0, 256), (1, 384, 128)]

            def scores(h):
                base = 64 * (h % 2)
                if h >= 2:
                    pe.wait_ge(w_ready, h - 1)
                for b in (0, 1, 3, 2):
                    bank, off, n = place[b]
                    ins = pe.matmul(ps[:, 3 * (h % 2) + bank, off:off + n], k_t[base:base + 64, h // 2, P * b:P * b + P],
                                    q_t[base:base + 64, h // 2, P * b:T], start=b != 3, stop=False, skip_group_check=True)
                ins.then_inc(z_ready, 1)

            def tails(h):
                pe.wait_ge(sp_masked, 2 * h + 2)
                p_off = [0, 512, 1024, 896]
                for b in range(4):
                    bank, off, n = place[b]
                    for c in range(b, 4):
                        w = cst[:, C_NEGGE:C_NEGGE + P] if c == b else cst[:, C_NEGONE:C_NEGONE + P]
                        d = P * (c - b)
                        ins = pe.matmul(ps[:, 3 * (h % 2) + bank, off + d:off + n], w,
                                        sb_p[:, h % 2, p_off[c]:p_off[c] + T - P * c], start=False, stop=c == 3, skip_group_check=True)
                ins.then_inc(tail_ready, 1)

            def outputs(h):
                pe.wait_ge(w_masked, 2 * h + 2)
                if h >= 4 and h % 2 == 0:
                    pe.wait_ge(o_hi, h // 2 - 1)
                    pe.wait_ge(o_lo, h // 2 - 1)
                base = 64 * (h % 2)
                w_off = [0, 512, 1024, 896]
                for b in range(4):
                    ins = pe.matmul(ps[base:base + 64, 6 + (h // 2) % 2, P * b:T], v_s[:, b, 64 * h:64 * h + 64],
                                    sb_w[:, h % 2, w_off[b]:w_off[b] + T - P * b], start=b == 0, stop=b == 3, skip_group_check=True)
                ins.then_inc(o_ready, 1)

            scores(0)
            for h in range(SB_HEADS):
                if h + 1 < SB_HEADS:
                    scores(h + 1)
                tails(h)
                if h >= 1:
                    outputs(h - 1)
            outputs(SB_HEADS - 1)
            pe.wait_ge(o_hi, 8)
            pe.wait_ge(o_lo, 8)
            for name in ("br0", "br1"):
                features(G[name], oh, ol)
            for name in ("ga0", "ga1"):
                features(G[name], hh, hl)

            def transpose_x(f):
                pe.wait_ge(s("xs_ready"), 4 * f + 4)
                for j in range(4):
                    for i in range(NT):
                        ins = transpose(ps[:, 4 * (G[f"xbc{f}"] % 2) + j, P * i:P * i + P], xst[:, j, P * i:P * i + P])
                    ins.then_inc(s("xtr_ready"), 1)

            for f in range(6):
                if f >= 2:
                    pe.wait_ge(s("xtok_ready"), 4 * (f - 1))
                features(G[f"xbc{f}"], hh, hl, between=(lambda: transpose_x(f - 1)) if 1 <= f <= 4 else None, behind=3)
            features(G["dt"], hh, hl)
            evacuated("dt")
            pe.wait_ge(s("conv_ready"), 24)
            for c in range(NT):
                ins = transpose(ps[:, 6, P * c:P * c + P], dt_t[:, P * c:P * c + P])
            ins.then_inc(s("dttr_ready"), 1)
            pe.wait_ge(s("dt_dve"), 2)
            pe.matmul(b4(5)[:, :, 0:32], cst[:, C_LE:C_LE + P], adt[:], start=True, stop=True)
            pe.matmul(b4(5)[:, :, 32:64], cst[:, C_ONE:C_ONE + P], adt[:], start=True, stop=True).then_inc(s("acs_ready"), 1)
            pe.wait_ge(s("dt_act"), 4)

            def inside(u):
                g, c = u // 4, u % 4
                t = slice(P * c, P * c + P)
                if u >= 2:
                    pe.wait_ge(s("dec_ready"), u - 1)
                if u:
                    pe.wait_ge(s("cbm_ready"), u)
                pe.matmul(ps[:, 4, 0:P], b_t[:, g, t], c_t[:, g, t], start=True, stop=True)
                transpose(ps[:, 4, P:2 * P], b_t[:, g, t]).then_inc(s("cb_ready"), 1)
                pe.wait_ge(s("segl_ready"), u + 1)
                for e in range(8):
                    ins = pe.matmul(ps[:, 2 * (u % 2) + e // 4, P * (e % 4):P * (e % 4) + P], segl[:, u % 2, e, :], cst[:, C_LE:C_LE + P], start=True, stop=True)
                ins.then_inc(s("seg_ready"), 1)

            inside(0)
            for u in range(16):
                if u < 15:
                    inside(u + 1)
                g, c = u // 4, u % 4
                pe.wait_ge(s("wmat_ready"), u + 1)
                pe.wait_ge(s("xde_ready"), u + 1)
                if u:
                    pe.wait_ge(s("yadd_ready"), u)
                for e in range(8):
                    pe.matmul(ps[:, 5, 64 * e:64 * e + 64], dec[:, u % 2, e, :], xd[:, u % 2, e, :], start=True, stop=True)
                if c > 0:
                    pe.wait_ge(s("state_ready"), 3 * g + c)
                    pe.matmul(ps[:, 6, :], c_t[:, g, P * c:P * c + P], state[:], start=True, stop=True)
                pe.wait_ge(s("btok_ready"), u + 1)
                pe.matmul(ps[:, 7, :], btok[:, u % 2, :], xe[:, u % 2], start=True, stop=True).then_inc(s("y_mm"), 1)
            pe.wait_ge(s("y_done"), 16)
            for i in range(4):
                tokens(G[f"z{i}"], hhi, hlo)
            for i in range(2):
                features(G[f"gs{i}"], hh, hl)
            pe.wait_ge(s("ysc_ready"), 16)
            evacuated("gs1")
            for f in range(16):
                if f >= 8:
                    pe.wait_ge(s("yhi_ready"), f - 7)
                    pe.wait_ge(s("ylo_ready"), f - 7)
                for i in range(NT):
                    ins = transpose(ps[:, f % 8, P * i:P * i + P], xs[:, i, P * f:P * f + P])
                ins.then_inc(s("ytr_ready"), 1)
            pe.wait_ge(s("yhi_ready"), 16)
            pe.wait_ge(s("ylo_ready"), 16)
            for i in range(2):
                features(G[f"bs{i}"], lambda k: yhi[:, :, P * k:P * k + P], lambda k: ylo[:, k, :])
            pe.wait_ge(o_hi, 8 + KD)
            pe.wait_ge(o_lo, 8 + KD)
            for i in range(2):
                tokens(G[f"mix{i}"], ohi, olo)
            pe.wait_ge(s("memn_ready"), 2)
            evacuated("mix1")
            for k in range(KD):
                for i in range(2):
                    ins = transpose(ps[:, k, P * i:P * i + P], mem_n[:, i, P * k:P * k + P])
                ins.then_inc(s("mtr_ready"), 1)
            pe.wait_ge(s("m_lo"), KD)
            for i in range(2):
                features(G[f"xk{i}"], lambda k: mhi[:, k, :], lambda k: mlo[:, k, :], n=MEM)
            for i in range(2):
                g = G[f"xv{i}"]

                def pick(j, slot, kk, k):
                    t, c = slice(P * (j // 2), P * (j // 2) + P), slice(256 * (j % 2), 256 * (j % 2) + 256)
                    return mhi[:, k, t], mlo[:, k, t], whi[:, slot, kk, c], wlo[:, slot, kk, c], ps[:, 4 * (g % 2) + j, 0:256]
                project(g, pick)
            evacuated("xv1")
            transpose_normed(1)
            for i in range(2):
                features(G[f"xq{i}"], hh, hl)
            evacuated("xq1")

            def xa_scores(i):
                if i >= 2:
                    pe.wait_ge(s("pexp_ready"), 4 * (i - 1))
                for h in range(XA_HEADS):
                    for d in range(2):
                        ins = pe.matmul(ps[:, 2 * (i % 2) + h // 2, 256 * (h % 2):256 * (h % 2) + 256],
                                        qx[:, 2 * h + d, P * i:P * i + P], kx[:, 2 * h + d, :], start=d == 0, stop=d == 1)
                ins.then_inc(s("xs_mm"), 1)

            xa_scores(0)
            for i in range(NT):
                if i + 1 < NT:
                    xa_scores(i + 1)
                pe.wait_ge(s("px_ready"), i + 1)
                if i >= 2:
                    pe.wait_ge(s("pt_act"), i - 1)
                    pe.wait_ge(s("pt_dve"), i - 1)
                for n in range(8):
                    ins = transpose(ps[:, 4 + 2 * (i % 2) + n // 4, P * (n % 4):P * (n % 4) + P], px[:, i % 2, n // 2, P * (n % 2):P * (n % 2) + P])
                    if n % 4 == 3:
                        ins.then_inc(s("ptr_ready"), 1)
            pe.wait_ge(s("pt_act"), 4)
            pe.wait_ge(s("pt_dve"), 4)
            for d in range(KD):
                h = d // 2
                for mt in range(2):
                    ins = pe.matmul(ps[:, d, :], vx[:, mt, P * d:P * d + P], ptx[:, 2 * h + mt, :], start=mt == 0, stop=mt == 1)
                ins.then_inc(s("ox_ready"), 1)
            pe.wait_ge(o_hi, 16 + KD)
            pe.wait_ge(o_lo, 16 + KD)
            for i in range(2):
                tokens(G[f"xo{i}"], ohi, olo)
            transpose_normed(2)
            def modulation(i):
                g = G[f"ada{i}"]

                def pick(j, slot, kk, k):
                    return (chi[:, k:k + 1].to_broadcast([P, P]), clo[:, k:k + 1].to_broadcast([P, P]),
                            whi[:, slot, kk, :], wlo[:, slot, kk, :], ps[:, 4 * (g % 2), :])
                project(g, pick)

            pe.wait_ge(s("cb_lo"), 1)
            for f in range(11):
                features(G[f"gu{f}"], hh, hl)
                modulation(f)
            modulation(11)
            pe.wait_ge(s("gu_hi"), KF)
            pe.wait_ge(s("gu_lo"), KF)
            for i in range(2):
                tokens(G[f"dn{i}"], guhi, gulo)
            transpose_normed(3)
            features(G["in0"], hh, hl)
            features(G["in1"], hh, hl)
            features(G["in2"], hh, hl, cols=lambda j: [(0, 128), (128, 256), (256, 384), (384, 400)][j])
            tokens(G["in3"], hhi, hlo)
            tokens(G["in4"], hhi, hlo)
            evacuated("in4")
            pe.wait_ge(s("gdiag_ready"), 2)
            for n in range(4):
                pe.matmul(ps[:, 4 + n, :], cst[:, C_ONE:C_ONE + P], gdiag[:, n // 2, 4 * (n % 2):4 * (n % 2) + 4, :],
                          start=True, stop=True).then_inc(s("gates_mm"), 1)
            for i in range(NT):
                ins = transpose(ps[:, 0, P * i:P * i + P], av_t[:, P * i:P * i + P])
            ins.then_inc(s("avtr_ready"), 1)
            pe.wait_ge(s("av_ready"), 1)

            def sw_scores(b):
                if b:
                    pe.wait_ge(s("sw_sc"), 4 * b)
                for h in (0, 2, 4, 6, 1, 3, 5, 7):
                    base, kv = 64 * (h % 2), h // 4
                    keys = ak_t if base == 64 * kv else ak_x
                    lo = P if b == 0 else 0
                    c0 = 256 * (h // 2 % 2)
                    ins = pe.matmul(ps[:, 2 * (h % 2) + h // 4, c0 + lo:c0 + 256], aq_t[base:base + 64, h // 2, P * b:P * b + P],
                                    keys[base:base + 64, P * (b - 1) + lo:P * (b + 1)], start=True, stop=True)
                    if h // 2 % 2:
                        ins.then_inc(s("sw_mm"), 1)

            sw_scores(0)
            for b in range(NT):
                if b + 1 < NT:
                    sw_scores(b + 1)
                if b:
                    pe.wait_ge(s("sw_ohi"), b)
                    pe.wait_ge(s("sw_olo"), b)
                pe.wait_ge(s("sw_p"), b + 1)
                if b == 0:
                    pe.wait_ge(s("gates_done"), 4)
                if b:
                    pe.wait_ge(s("sw_pta"), 2 * b)
                    pe.wait_ge(s("sw_ptd"), 2 * b)
                for n in range(4):
                    for m in range(4):
                        q = 4 * n + m
                        if b == 0 and q % 2 == 0:
                            continue
                        ins = transpose(ps[:, 4 + n, P * m:P * m + P], sw_ss[b % 2][:, q // 2, P * (q % 2):P * (q % 2) + P])
                    ins.then_inc(s("sw_tr"), 1)
                pe.wait_ge(s("sw_pta"), 2 * b + 2)
                pe.wait_ge(s("sw_ptd"), 2 * b + 2)
                for h in range(SW_HEADS):
                    base, kv = 64 * (h % 2), h // 4
                    for kh in range(1 if b == 0 else 0, 2):
                        ins = pe.matmul(ps[base:base + 64, 4, P * (h // 2):P * (h // 2) + P], av_s[:, b - 1 + kh, 64 * kv:64 * kv + 64],
                                        sw_pt[:, 2 * h + kh, :], start=kh == (1 if b == 0 else 0), stop=kh == 1, skip_group_check=True)
                ins.then_inc(s("sw_o"), 1)
            pe.wait_ge(s("sw_ohi"), 4)
            pe.wait_ge(s("sw_olo"), 4)
            pe.wait_ge(s("vectors_landed"), 32)
            for t2 in range(2):
                ins = pe.matmul(ps[:, t2, :], gup[:, P * t2:P * t2 + P], glr_t[0:17, :], start=True, stop=True)
            ins.then_inc(s("la_ready"), 1)
            pe.wait_ge(s("kout_ready"), 1)
            for c in range(NT):
                for t2 in range(2):
                    ins = transpose(ps[:, 4 + c, P * t2:P * t2 + P], k_out[:, t2, P * c:P * c + P])
                ins.then_inc(s("ktr_ready"), 1)
            for lv in range(LEVELS + 1):
                if lv < LEVELS:
                    pe.wait_ge(s("glq_ready"), lv + 1)
                    pe.wait_ge(s("glk_ready"), lv + 1)
                q, k = (gl_qs[lv % 2], gl_ks[lv % 2]) if lv < LEVELS else (gq_t, gk_t)
                for h in range(GLA_HEADS):
                    if lv:
                        pe.wait_ge(s("att_masked"), 4 * (lv - 1) + h + 1)
                    base = 64 * (h % 2)
                    for c in range(NT):
                        t = slice(P * c, P * c + P)
                        ins = pe.matmul(ps[:, h, t], k[base:base + 64, h // 2, t], q[base:base + 64, h // 2, t], start=True, stop=True)
                    ins.then_inc(s("att_ready"), 1)
            pe.wait_ge(s("att_added"), 4 * LEVELS)
            pe.wait_ge(s("ktok_ready"), 4)
            for c in range(NT):
                for h in range(GLA_HEADS):
                    base = 64 * (h % 2)
                    dst = ps[:, 4 * (1 - c % 2) + h % 2, P * (h // 2):P * (h // 2) + P]
                    if c >= 2 and h == 0:
                        pe.wait_ge(s("go_ready"), c - 1)
                    pe.matmul(dst, gl_a[:, h, c, :], gv_s[:, c, P * h:P * h + P], start=True, stop=c == 0, skip_group_check=True)
                    if c:
                        pe.wait_ge(s("gst_ready"), c)
                        pe.matmul(dst, q_in[base:base + 64, h // 2, P * c:P * c + P], g_st[base:base + 64, h // 2, :], start=False, stop=True, skip_group_check=True)
                for t2 in range(2):
                    if c:
                        pe.wait_ge(s("gst_ready"), c)
                    ins = pe.matmul(ps[:, 6, 256 * t2:256 * t2 + 256], k_tok[:, c, P * t2:P * t2 + P], gv_s[:, c, 256 * t2:256 * t2 + 256], start=True, stop=True)
                ins.then_inc(s("go_mm"), 1)
            pe.wait_ge(s("gon_ready"), 1)
            for f in range(4):
                for i in range(NT):
                    ins = transpose(ps[:, f, P * i:P * i + P], go_s[:, i, P * f:P * f + P])
                ins.then_inc(s("gotr_ready"), 1)
            pe.wait_ge(s("go_hi"), 4)
            pe.wait_ge(s("go_lo"), 4)
            for i in range(2):
                tokens(G[f"out{i}"], hhi, hlo)
            transpose_normed(4)
            for i in range(NT):
                for k in range(KD):
                    ins = transpose(ps[:, 2 * i + k // 4, P * (k % 4):P * (k % 4) + P], haff[:, k, P * i:P * i + P])
                    if k % 4 == 3:
                        ins.then_inc(s("back_ready"), 1)
            pe.wait_ge(s("h2_ready"), 8)
            def first_scores(i):
                evacuated(f"pq{i}")
                if i == 0:
                    pe.wait_ge(s("vectors_landed"), 64)
                for f in range(4):
                    ins = pe.matmul(ps[:, 4 * (G[f"pq{i}"] % 2), P * f:P * f + P], pq_t[:, 4 * i + f, 0:P], subk[:, 4 * i + f, :], start=True, stop=True)
                ins.then_inc(s("subs_mm"), 1)

            for i in range(4):
                if i >= 2:
                    pe.wait_ge(s("sc_ready"), i - 1)
                features(G[f"pq{i}"], hh, hl, between=(lambda: first_scores(i - 1)) if i else None)
            first_scores(3)

            def sub_scores(t):
                pe.wait_ge(s("sc_ready"), t + 3)
                for f in range(16):
                    ins = pe.matmul(ps[:, 4 + f // 4, P * (f % 4):P * (f % 4) + P], pq_t[:, f, P * t:P * t + P], subk[:, f, :], start=True, stop=True)
                ins.then_inc(s("subs_mm"), 1)

            pe.wait_ge(s("zeros_ready"), 1)
            for t in range(NT):
                if t + 1 < NT:
                    sub_scores(t + 1)
                acc = 2 * (t % 2)
                if t >= 2:
                    pe.wait_ge(x_ready, NT * 4 + t - 1)
                for n in range(2):
                    pe.matmul(ps[:, acc + n, :], zeros[:], h2_s[:, t, 512 * n:512 * n + 512], start=True, stop=False, skip_group_check=True)
                with pe.Fori(0, ROUNDS) as i:
                    for jn, j in enumerate(PE_SLOTS):
                        pe.wait_ge(s("diag_ready"), i * len(PE_SLOTS) + (len(PE_SLOTS) * ROUNDS * t + jn + 1))
                        pe.wait_ge(row_landed[j], i * 16 + 16 * (ROUNDS * (2 * t + 1) + 1))
                        for n in range(2):
                            ins = pe.matmul(ps[:, acc + n, :], diag[:, j, :], rows[:, j, 512 * n:512 * n + 512], start=False, stop=False, skip_group_check=True)
                        ins.then_inc(row_used[j], 1)
                for m, j in enumerate(DVE_SLOTS):
                    pe.wait_ge(row_used[j], 2 * ROUNDS * (t + 1) + 1)
                    for n in range(2):
                        ins = pe.matmul(ps[:, acc + n, :], ident, vacc[:, m, 512 * n:512 * n + 512], start=False, stop=m == len(DVE_SLOTS) - 1, skip_group_check=True)
                ins.then_inc(s("peer_ready"), 1)

        def vector_program(v):
            steps = [0]

            def link(ins):
                steps[0] += 1
                ins.then_inc(dve_step, 1)
                v.wait_ge(dve_step, steps[0])

            def col(base, k):
                return vec[:, base + k:base + k + 1]

            def group(g, jobs, evac):
                for j in jobs:
                    acc_wait(v, g, j)
                    ins = evac(j, 4 * (g % 2) + j)
                ins.then_inc(dve_evac, 1)

            def to_features(dst, base_tile, scale=None, n=T):
                def evac(j, bank):
                    if scale is None:
                        return v.tensor_copy(dst[:, base_tile + j, :], ps[:, bank, 0:n])
                    return v.tensor_scalar(dst[:, base_tile + j, :], ps[:, bank, 0:n], scale, None, ALU.mult)
                return evac

            def to_tokens(dst, half):
                return lambda j, bank: v.tensor_copy(dst[:, j, 512 * half:512 * half + 512], ps[:, bank, :])

            roots = [0]

            def inverse_root(dst, mid, sums, count):
                v.tensor_scalar(mid, sums, 1.0 / count, EPS, ALU.mult, ALU.add).then_inc(root_in, 1)
                finish_root(dst, mid)

            def finish_root(dst, mid):
                roots[0] += 1
                v.wait_ge(root_out, roots[0])
                n = mid.shape[-1]
                link(v.reciprocal(newt[:, 0, 0:n], newt[:, 1, 0:n]))
                link(v.tensor_tensor(dst, newt[:, 0, 0:n], newt[:, 0, 0:n], ALU.mult))
                link(v.tensor_tensor(dst, dst, mid, ALU.mult))
                link(v.tensor_scalar(dst, dst, -0.5, 1.5, ALU.mult, ALU.add))
                link(v.tensor_tensor(dst, dst, newt[:, 0, 0:n], ALU.mult))

            def rms_scale(r):
                v.wait_ge(sq_ready, NT * (r + 1))
                inverse_root(rstd, meps, ssq, D)
                for i in range(NT):
                    ins = v.tensor_scalar(xn[:, i, :], x_res[:, i, :], rstd[:, i:i + 1], None, ALU.mult)
                    ins.then_inc(xn_ready, 1)

            def rms_rest(r, gain):
                for k in range(KD):
                    v.wait_ge(h_hi, KD * r + k + 1)
                    v.scalar_tensor_tensor(hlo[:, k, :], ps[:, k, :], col(gain, k), hhi[:, k, :].bitcast(F32), ALU.mult, ALU.subtract).then_inc(h_ready, 1)

            def affine(r, mod):
                for k in range(KD):
                    v.wait_ge(tr_ready, KD * r + k + 1)
                    v.tensor_scalar(haff[:, k, :], ps[:, k, :], modc[:, 24 * mod + 8 + k:24 * mod + 9 + k], modc[:, 24 * mod + k:24 * mod + k + 1],
                                    ALU.mult, ALU.add).then_inc(s("aff_ready"), 1)
                for k in range(KD):
                    v.wait_ge(h_hi, KD * r + k + 1)
                    v.tensor_tensor(hlo[:, k, :], haff[:, k, :], hhi[:, k, :].bitcast(F32), ALU.subtract).then_inc(h_ready, 1)

            def add_sublayer(r, name, u):
                v.wait_ge(grow_landed, 16 * (r + 1))
                for i in range(NT):
                    v.wait_ge(usq_ready, NT * r + i + 1)
                    if i == NT - 1:
                        v.tensor_scalar(meps, ssq, 1.0 / D, EPS, ALU.mult, ALU.add).then_inc(root_in, 1)
                    ins = v.tensor_tensor(u[:, i, :], u[:, i, :], grow[:], ALU.mult)
                link(ins)
                finish_root(rstd, meps)
                for i in range(NT):
                    v.scalar_tensor_tensor(x_res[:, i, :], u[:, i, :], rstd[:, i:i + 1], x_res[:, i, :], ALU.mult, ALU.add).then_inc(x_ready, 1)

            v.wait_ge(x_landed, 16)
            rms_scale(0)
            v.wait_ge(consts_landed, 48)
            rms_rest(0, V_PRE)
            for i in range(2):
                group(G[f"q{i}"], (2, 3), to_features(q_t, 4 * i, SB_DIM ** -0.5))
            for i in range(2):
                group(G[f"k{i}"], (2, 3), to_features(k_t, 4 * i))
            for i in range(2):
                group(G[f"v{i}"], (2, 3), to_tokens(v_s, i))

            def softplus(h):
                zb = 3 * (h % 2)
                v.wait_ge(l_ready, h + 1)
                if h >= 2:
                    v.wait_ge(tail_ready, h - 1)
                for n, (o, w) in enumerate(((0, 512), (512, 512), (1024, 256))):
                    ins = v.scalar_tensor_tensor(sb_p[:, h % 2, o:o + w], ps[:, zb + n, 0:w], 0.0, sb_l[:, h % 2, o:o + w], ALU.max, ALU.add)
                ins.then_inc(sp_ready, 1)

            def rest_heads(hp):
                v.wait_ge(o_hi, hp + 1)
                v.tensor_tensor(olo[:, hp, :], ps[:, 6 + hp % 2, :], ohi[:, hp, :].bitcast(F32), ALU.subtract).then_inc(o_lo, 1)

            softplus(0)
            for h in range(SB_HEADS):
                if h + 1 < SB_HEADS:
                    softplus(h + 1)
                if h >= 2 and h % 2 == 0:
                    rest_heads(h // 2 - 1)
            rest_heads(7)
            for i in range(2):
                group(G[f"br{i}"], (2, 3), to_features(attbr, 4 * i))
            v.wait_ge(act_evac, act_evacs[G["br1"] + 1])
            v.wait_ge(dve_evac, dve_evacs[G["br1"] + 1])
            for i in range(2):
                v.wait_ge(act_evac, act_evacs[G[f"ga{i}"] + 1])
                for k in range(4 * i, 4 * i + 4):
                    v.tensor_tensor(merged[:, k, :], gate_a[:, k, :], attbr[:, k, :], ALU.mult).then_inc(s("merged_done"), 1)
            v.wait_ge(s("merged_done"), 8)
            link(v.memset(raw[:, :, 0:3], 0.0))

            def x_tokens(f):
                for j in range(2, 4):
                    v.wait_ge(s("xtr_ready"), 4 * f + j + 1)
                    v.tensor_copy(xs[:, :, P * (4 * f + j):P * (4 * f + j + 1)], b4(4 * (G[f"xbc{f}"] % 2) + j)).then_inc(s("xtok_ready"), 1)

            for f in range(6):
                if 1 <= f <= 4:
                    x_tokens(f - 1)
                v.wait_ge(act_evac, act_evacs[G[f"xbc{f}"] + 1])
                if f:
                    v.wait_ge(s("xs_ready"), 4 * f)
                for tap in range(4):
                    for j in range(4):
                        w = col(V_CW, 24 * tap + 4 * f + j)
                        if tap == 0:
                            ins = v.tensor_scalar(cacc[:, j, :], raw[:, j, 0:512], w, None, ALU.mult)
                        else:
                            ins = v.scalar_tensor_tensor(cacc[:, j, :], raw[:, j, tap:tap + 512], w, cacc[:, j, :], ALU.mult, ALU.add)
                        if tap == 3:
                            ins.then_inc(s("conv_ready"), 1)
                    if tap < 3:
                        link(ins)
            v.wait_ge(s("dttr_ready"), 1)
            v.tensor_tensor(dta[:], b4(6)[:, :, 0:32], row[:, R_DTB:R_DTB + 32].unsqueeze(1).to_broadcast([P, NT, 32]), ALU.add).then_inc(s("dt_dve"), 1)
            v.wait_ge(s("dt_act"), 1)
            link(v.tensor_scalar(nega, nega, -1.0, None, ALU.mult))
            v.wait_ge(s("dt_act"), 2)
            link(v.scalar_tensor_tensor(dtt[:], dta[:], 0.0, dtb[:], ALU.max, ALU.add))
            v.tensor_tensor(adt[:], dtt[:], nega.unsqueeze(1).to_broadcast([P, NT, 32]), ALU.mult).then_inc(s("dt_dve"), 1)
            v.wait_ge(s("dt_act"), 3)
            v.tensor_tensor(dtb[:], dta[:], b4(5)[:, :, 0:32], ALU.subtract).then_inc(s("dt_dve"), 1)
            v.wait_ge(s("dt_act"), 4)
            v.tensor_tensor(dtw[:], dtt[:], dtb[:], ALU.mult).then_inc(s("dt_dve"), 1)

            def inside(u):
                v.wait_ge(s("btok_ready"), u + 1)
                v.tensor_tensor(cbm[:, u % 2, :], ps[:, 4, 0:P], cst[:, C_LE:C_LE + P], ALU.mult).then_inc(s("cbm_ready"), 1)
                v.wait_ge(s("dec_ready"), u + 1)
                v.wait_ge(s("cbm_ready"), u + 1)
                v.tensor_tensor(dec[:, u % 2], dec[:, u % 2], cbm[:, u % 2, :].unsqueeze(1).to_broadcast([P, 8, P]), ALU.mult).then_inc(s("wmat_ready"), 1)

            inside(0)
            for u in range(16):
                if u < 15:
                    inside(u + 1)
                g, c = u // 4, u % 4
                hs = slice(8 * g, 8 * g + 8)
                b8 = lambda bank: ps[:, bank, :].rearrange("p (e q) -> p e q", e=8)
                st = state[:].rearrange("p (e q) -> p e q", e=8)
                v.wait_ge(s("y_mm"), u + 1)
                if c == 0:
                    v.tensor_copy(state[:], ps[:, 7, :]).then_inc(s("state_ready"), 1)
                elif c < 3:
                    v.wait_ge(s("state_ready"), 3 * g + c)
                    link(v.tensor_tensor(st, st, ecd[:, c, hs].unsqueeze(2).to_broadcast([P, 8, SSM_P]), ALU.mult))
                    v.tensor_tensor(state[:], state[:], ps[:, 7, :], ALU.add).then_inc(s("state_ready"), 1)
                ys = ysum[:, u % 2]
                if c:
                    link(v.tensor_tensor(ys, b8(6), eacs[:, c, hs].unsqueeze(2).to_broadcast([P, 8, SSM_P]), ALU.mult))
                    v.tensor_tensor(ys, ys, b8(5), ALU.add).then_inc(s("yadd_ready"), 1)
                else:
                    v.tensor_copy(ys, b8(5)).then_inc(s("yadd_ready"), 1)
                v.wait_ge(s("yadd_ready"), u + 1)
                v.wait_ge(s("dx_ready"), u + 1)
                xg = xs[:, c, 512 * g:512 * g + 512].rearrange("p (e q) -> p e q", e=8)
                v.tensor_tensor(xg, xg, ys, ALU.add).then_inc(s("y_done"), 1)
            for i in range(4):
                v.wait_ge(act_evac, act_evacs[G[f"z{i}"] + 1])
                for j in range(NT):
                    ysl = xs[:, j, 512 * i:512 * i + 512]
                    ins = v.tensor_tensor(ysl, ysl, ztmp[:, i % 2, j, :], ALU.mult)
                link(ins)
                for j in range(NT):
                    ysl = xs[:, j, 512 * i:512 * i + 512]
                    n = 4 * i + j
                    v.tensor_tensor_reduce(ztmp[:, i % 2, j, :], ysl, ysl, 1.0, 0.0, ALU.mult, ALU.add, ssqy[:, n:n + 1]).then_inc(s("yz_done"), 1)
            v.wait_ge(s("yz_done"), 16)
            inverse_root(rstdy, mepsy, ssqy, 512)
            v.tensor_copy(row[:, R_END + 8:R_END + 9], rstdy[:, 0:1]).then_inc(s("rstdy_ready"), 1)
            for f in range(16):
                v.wait_ge(s("yhi_ready"), f + 1)
                v.scalar_tensor_tensor(ylo[:, f, :].rearrange("p (i t) -> p i t", i=NT), b4(f % 8), col(V_SSM, f), yhi[:, :, P * f:P * f + P].bitcast(F32),
                                       ALU.mult, ALU.subtract).then_inc(s("ylo_ready"), 1)
            for i in range(2):
                g = G[f"bs{i}"]
                v.wait_ge(act_evac, act_evacs[G["gs1"] + 1])
                group(g, range(4), lambda j, bank: v.tensor_tensor(gate_s[:, 4 * i + j, :], gate_s[:, 4 * i + j, :], ps[:, bank, :], ALU.mult))
                v.wait_ge(dve_evac, dve_evacs[g + 1])
                for k in range(4 * i, 4 * i + 4):
                    v.tensor_tensor(merged[:, k, :], merged[:, k, :], gate_s[:, k, :], ALU.add).then_inc(s("merged_s"), 1)
            for k in range(KD):
                v.wait_ge(o_hi, 8 + k + 1)
                v.tensor_tensor(olo[:, k, :], merged[:, k, :], ohi[:, k, :].bitcast(F32), ALU.subtract).then_inc(o_lo, 1)
            v.wait_ge(s("msq_ready"), 2)
            inverse_root(rstd[:, 0:2], meps[:, 0:2], ssq[:, 0:2], D)
            for i in range(2):
                v.tensor_scalar(mem_n[:, i, :], mem_s[:, i, :], rstd[:, i:i + 1], None, ALU.mult).then_inc(s("memn_ready"), 1)
            for i in range(2):
                group(G[f"mix{i}"], (2, 3), to_tokens(u_out, i))
            for k in range(KD):
                v.wait_ge(s("m_hi"), k + 1)
                v.scalar_tensor_tensor(mlo[:, k, :], ps[:, k, 0:MEM], col(V_MEM, k), mhi[:, k, :].bitcast(F32), ALU.mult, ALU.subtract).then_inc(s("m_lo"), 1)
            add_sublayer(0, "mix", u_out)
            rms_scale(1)
            for i in range(2):
                group(G[f"xk{i}"], (2, 3), to_features(kx, 4 * i, n=MEM))
            for i in range(2):
                group(G[f"xv{i}"], (2, 3), lambda j, bank: v.tensor_copy(vx[:, j // 2, 512 * i + 256 * (j % 2):512 * i + 256 * (j % 2) + 256], ps[:, bank, 0:256]))
            rms_rest(1, V_XA)
            for i in range(2):
                group(G[f"xq{i}"], (2, 3), to_features(qx, 4 * i, XA_DIM ** -0.5))

            def xa_max(i):
                p4 = slice(4 * (i % 2), 4 * (i % 2) + 4)
                v.wait_ge(s("xs_mm"), i + 1)
                if i >= 2:
                    v.wait_ge(s("pexp_ready"), 4 * (i - 1))
                link(v.tensor_reduce(smx[:, p4], ps[:, 2 * (i % 2):2 * (i % 2) + 2, :].rearrange("p b (h m) -> p (b h) m", h=2), AX, ALU.max))
                v.tensor_scalar(snm[:, p4], smx[:, p4], -1.0, None, ALU.mult).then_inc(s("xmax_ready"), 1)

            xa_max(0)
            for i in range(NT):
                if i + 1 < NT:
                    xa_max(i + 1)
                p4 = slice(4 * (i % 2), 4 * (i % 2) + 4)
                v.wait_ge(s("pexp_ready"), 4 * (i + 1))
                link(v.reciprocal(srec[:, p4], ssum[:, p4]))
                v.tensor_tensor(px[:, i % 2], px[:, i % 2], srec[:, p4].unsqueeze(2).to_broadcast([P, XA_HEADS, MEM]), ALU.mult).then_inc(s("px_ready"), 1)
                v.wait_ge(s("ptr_ready"), 2 * i + 2)
                v.tensor_copy(ptx[:, 4:8, P * i:P * i + P], b4(5 + 2 * (i % 2))).then_inc(s("pt_dve"), 1)
            for d in range(KD):
                v.wait_ge(o_hi, 16 + d + 1)
                v.tensor_tensor(olo[:, d, :], ps[:, d, :], ohi[:, d, :].bitcast(F32), ALU.subtract).then_inc(o_lo, 1)
            for i in range(2):
                group(G[f"xo{i}"], (2, 3), to_tokens(u_out, i))
            add_sublayer(1, "xo", u_out)
            rms_scale(2)
            rms_rest(2, V_FFN)
            v.wait_ge(s("c_ready"), 1)
            v.tensor_tensor(clo[:], csil, chi[:].bitcast(F32), ALU.subtract).then_inc(s("cb_lo"), 1)

            def modulation(i):
                group(G[f"ada{i}"], (0,), lambda j, bank: v.tensor_tensor(modx[:], b4(bank), ident.unsqueeze(1).to_broadcast([P, 4, P]), ALU.mult))
                v.wait_ge(dve_evac, dve_evacs[G[f"ada{i}"] + 1])
                link(v.tensor_reduce(modc[:, 4 * i:4 * i + 4], modx[:], AX, ALU.add))

            for f in range(11):
                g = G[f"gu{f}"]
                v.wait_ge(act_evac, act_evacs[g + 1])
                group(g, (2, 3), lambda j, bank: v.tensor_tensor(gtmp[:, f % 2, j - 2, :], gtmp[:, f % 2, j - 2, :], ps[:, bank, :], ALU.mult))
                for j in range(2):
                    v.wait_ge(s("gu_hi"), 2 * f + j + 1)
                    v.tensor_tensor(gulo[:, 2 * f + j, :], gtmp[:, f % 2, j, :], guhi[:, 2 * f + j, :].bitcast(F32), ALU.subtract).then_inc(s("gu_lo"), 1)
                modulation(f)
            modulation(11)
            v.tensor_tensor(modc, modc, vec[:, V_BADA:V_BADA + 48], ALU.add).then_inc(s("mod_done"), 1)
            v.wait_ge(s("mod_done"), 1)
            for mod, gain in enumerate((V_N1, V_N2)):
                mc = modc[:, 24 * mod + 8:24 * mod + 16]
                link(v.scalar_tensor_tensor(mc, mc, 1.0, vec[:, gain:gain + 8], ALU.add, ALU.mult))
            for i in range(2):
                group(G[f"dn{i}"], (2, 3), to_tokens(u_out, i))
            add_sublayer(2, "dn", u_out)
            rms_scale(3)
            affine(3, 0)
            group(G["in0"], (2, 3), to_features(aq_t, 0, 0.125))
            group(G["in1"], (2, 3), to_features(gq_t, -2, 0.125))
            link(v.memset(glr_t[:], 1.0))
            group(G["in2"], (2, 3), lambda j, bank: v.tensor_copy(ak_x[:, :], ps[:, bank, :]) if j == 2 else v.tensor_copy(glr_t[0:16, :], ps[0:16, bank, :]))
            group(G["in3"], (2, 3), to_tokens(gv_s, 0))
            group(G["in4"], (2, 3), to_tokens(gg_s, 0))
            for mod in range(2):
                v.tensor_tensor(gdiag[:, mod], ident.unsqueeze(1).to_broadcast([P, KD, P]),
                                modc[:, 24 * mod + 16:24 * mod + 24].unsqueeze(2).to_broadcast([P, KD, P]), ALU.mult).then_inc(s("gdiag_ready"), 1)
            v.wait_ge(s("avtr_ready"), 1)
            v.tensor_copy(av_s[:], b4(0)).then_inc(s("av_ready"), 1)

            def sw_max(b):
                lo = P if b == 0 else 0
                sw, st = sw_ss[b % 2], sw_stats[b % 2]
                if b >= 2:
                    v.wait_ge(s("sw_tr"), 4 * (b - 1))
                for n in range(4):
                    v.wait_ge(s("sw_mm"), 4 * b + n + 1)
                    h0 = 4 * (n % 2) + n // 2
                    ins = v.tensor_tensor(sw[:, h0:h0 + 3:2, lo:], ps[:, n, :].rearrange("p (h c) -> p h c", h=2)[:, :, lo:],
                                          cst[:, C_SWA + lo:C_SWA + 256].unsqueeze(1).to_broadcast([P, 2, 256 - lo]), ALU.add)
                    ins.then_inc(s("sw_sc"), 1)
                v.wait_ge(s("sw_sc"), 4 * b + 4)
                link(v.tensor_reduce(st[:, 0:8], sw[:, :, lo:], AX, ALU.max))
                link(v.tensor_tensor(st[:, 0:8], st[:, 0:8], row[:, R_SINK:R_SINK + 8], ALU.max))
                v.tensor_scalar(st[:, 8:16], st[:, 0:8], -1.0, None, ALU.mult)
                v.tensor_tensor(st[:, 24:32], row[:, R_SINK:R_SINK + 8], st[:, 0:8], ALU.subtract).then_inc(s("sw_max"), 1)

            sw_max(0)
            for b in range(NT):
                lo = P if b == 0 else 0
                sw, st = sw_ss[b % 2], sw_stats[b % 2]
                if b + 1 < NT:
                    sw_max(b + 1)
                v.wait_ge(s("sw_exp"), b + 1)
                link(v.tensor_tensor(sden, st[:, 16:24], st[:, 24:32], ALU.add))
                link(v.reciprocal(srec, sden))
                v.tensor_tensor(sw[:, :, lo:], sw[:, :, lo:], srec.unsqueeze(2).to_broadcast([P, 8, 256 - lo]), ALU.mult).then_inc(s("sw_p"), 1)
                if b:
                    v.wait_ge(s("sw_o"), b)
                for n in (1, 3):
                    v.wait_ge(s("sw_tr"), 4 * b + n + 1)
                    m = slice(1, 4, 2) if b == 0 else slice(0, 4)
                    v.tensor_copy(sw_pt[:, 4 * n:4 * n + 4, :][:, m, :], b4(4 + n)[:, m, :]).then_inc(s("sw_ptd"), 1)
                v.wait_ge(s("sw_ohi"), b + 1)
                v.tensor_tensor(hlo[:, 0:4, P * b:P * b + P], b4(4), hhi[:, 0:4, P * b:P * b + P].bitcast(F32), ALU.subtract).then_inc(s("sw_olo"), 1)
            v.wait_ge(s("gla_act"), 1)
            link(v.scalar_tensor_tensor(la_t[:], gl_d[:], 0.0, la_t[:], ALU.max, ALU.add))
            link(v.tensor_scalar(la_t[:], la_t[:], -1.0 / 16, None, ALU.mult))
            for t2 in range(2):
                for c in range(NT):
                    v.tensor_tensor_scan(b_cs[:, t2, P * c:P * c + P], cst[:, C_ONE:C_ONE + P], la_t[:, t2, P * c:P * c + P], 0.0, ALU.mult, ALU.add).then_inc(s("bcs_ready"), 1)
            v.wait_ge(s("bcs_ready"), 8)
            b_chunks = b_cs[:].rearrange("p a (c l) -> p (a c) l", c=NT)
            v.tensor_tensor(gl_d[:].rearrange("p a (c l) -> p (a c) l", c=NT), b_chunks[:, :, P - 1:P].to_broadcast([P, 8, P]), b_chunks, ALU.subtract).then_inc(s("bd_ready"), 1)

            def level_difference(lv):
                half = 1 << lv
                view = b_cs[:].rearrange("p a (n l) -> p (a n) l", l=2 * half)
                v.tensor_tensor(gl_ds[lv % 2][:].rearrange("p a (n l) -> p (a n) l", l=2 * half), view,
                                view[:, :, half - 1:half].to_broadcast([P, T // half, 2 * half]), ALU.subtract).then_inc(s("gd_ready"), 1)

            v.wait_ge(s("gla_act"), 3)

            def level_masks(lv):
                mask = cst[:, C_GLA + P * lv:C_GLA + P * lv + P] if lv < LEVELS else ident
                mask = mask.unsqueeze(1).to_broadcast([P, NT, P])
                for h in range(GLA_HEADS):
                    v.wait_ge(s("att_ready"), 4 * lv + h + 1)
                    if lv == 0:
                        v.tensor_tensor(gl_a[:, h], b4(h), mask, ALU.mult).then_inc(s("att_masked"), 1)
                    else:
                        v.tensor_tensor(gl_ms[h][:], b4(h), mask, ALU.mult).then_inc(s("att_masked"), 1)
                        if h:
                            v.wait_ge(s("att_masked"), 4 * lv + h)
                            v.tensor_tensor(gl_a[:, h - 1], gl_a[:, h - 1], gl_ms[h - 1][:], ALU.add).then_inc(s("att_added"), 1)
                if lv:
                    v.wait_ge(s("att_masked"), 4 * lv + 4)
                    v.tensor_tensor(gl_a[:, 3], gl_a[:, 3], gl_ms[3][:], ALU.add).then_inc(s("att_added"), 1)

            level_difference(0)
            level_difference(1)
            v.wait_ge(s("kout_ready"), 1)
            for lv in range(LEVELS):
                v.wait_ge(s("gdec_ready"), lv + 1)
                v.tensor_tensor(gl_ks[lv % 2][:], gl_ds[lv % 2][:], gk_t[:], ALU.mult).then_inc(s("glk_ready"), 1)
                if lv:
                    level_masks(lv - 1)
                if lv + 2 < LEVELS:
                    v.wait_ge(s("glq_ready"), lv + 1)
                    v.wait_ge(s("glk_ready"), lv + 1)
                    level_difference(lv + 2)
            level_masks(LEVELS - 1)
            level_masks(LEVELS)
            v.wait_ge(s("gla_act"), 4)
            for c in range(NT):
                v.wait_ge(s("go_mm"), c + 1)
                if c < 3:
                    for t2 in range(2):
                        for hh in range(2):
                            pr = slice(64 * hh, 64 * hh + 64)
                            new = ps[pr, 6, 256 * t2 + P * hh:256 * t2 + P * hh + P]
                            if c == 0:
                                ins = v.tensor_copy(g_st[pr, t2, :], new)
                            else:
                                ins = v.scalar_tensor_tensor(g_st[pr, t2, :], g_st[pr, t2, :], g_dl[pr, t2, c:c + 1], new, ALU.mult, ALU.add)
                    ins.then_inc(s("gst_ready"), 1)
                b0 = 4 * (1 - c % 2)
                v.tensor_copy(go_s[:, c, :].rearrange("p (a b e) -> p b a e", a=2, b=2),
                              ps[:, b0:b0 + 2, 0:256].rearrange("p b (a e) -> p b a e", a=2)).then_inc(s("go_ready"), 1)
                if 0 < c + 1 < 3:
                    v.wait_ge(s("gst_ready"), c + 1)
            v.wait_ge(s("go_ready"), 4)
            link(v.tensor_tensor(go_q[:], go_s[:], go_s[:], ALU.mult))
            link(v.tensor_reduce(ssg[:], go_q[:].rearrange("p i (h e) -> p (i h) e", h=GLA_HEADS), AX, ALU.add))
            inverse_root(rsg[:], mpg[:], ssg[:], P)
            gview = go_s[:].rearrange("p i (h e) -> p (i h) e", h=GLA_HEADS)
            link(v.tensor_tensor(gview, gview, rsg[:].unsqueeze(2).to_broadcast([P, 16, P]), ALU.mult))
            v.wait_ge(s("sgg_ready"), 1)
            v.tensor_tensor(go_s[:], go_s[:], gg_s[:], ALU.mult).then_inc(s("gon_ready"), 1)
            for f in range(4):
                v.wait_ge(s("go_hi"), f + 1)
                v.scalar_tensor_tensor(hlo[:, 4 + f, :], ps[:, f, :], col(V_GLAN, 0), hhi[:, 4 + f, :].bitcast(F32), ALU.mult, ALU.subtract).then_inc(s("go_lo"), 1)
            for i in range(2):
                group(G[f"out{i}"], (2, 3), to_tokens(u2, i))
            v.wait_ge(act_evac, act_evacs[G["out1"] + 1])
            v.wait_ge(dve_evac, dve_evacs[G["out1"] + 1])
            for i in range(NT):
                ins = v.tensor_tensor(u2[:, i, :], u2[:, i, :], gate1[:], ALU.mult)
            link(ins)
            for i in range(NT):
                v.tensor_tensor(x_res[:, i, :], x_res[:, i, :], u2[:, i, :], ALU.add).then_inc(x_ready, 1)
            rms_scale(4)
            affine(4, 1)
            for i in range(NT):
                v.wait_ge(s("back_ready"), 2 * i + 2)
                v.tensor_copy(h2_s[:, i, 512:1024], ps[:, 2 * i + 1, :]).then_inc(s("h2_ready"), 1)
            linked = [0]

            def top_keys(t, i, step, first=0, between=lambda: None):
                step(v.tensor_copy(tk_s[:].rearrange("p a n -> p (a n)"), sc[:, bass.ds(i * (2 * NKEYS) + 2 * NKEYS * first, 2 * NKEYS)]), fixed=True)
                for h in range(2):
                    ins = v.max(tv[:, h, 0:8], tk_s[:, h, :])
                step(ins, fixed=True)
                between()
                for h in range(2):
                    v.max_index(ti[:, h, 0:8], tv[:, h, 0:8], tk_s[:, h, :])
                    ins = v.match_replace(tk_r[:, h, :], tv[:, h, 0:8], tk_s[:, h, :], LOWEST)
                step(ins, fixed=True)
                for h in range(2):
                    ins = v.max(tv[:, h, 8:16], tk_r[:, h, :])
                step(ins, fixed=True)
                between()
                for h in range(2):
                    v.max_index(ti[:, h, 8:16], tv[:, h, 8:16], tk_r[:, h, :])
                step(v.tensor_tensor(cand[:], tv[:, 0, :].unsqueeze(2).to_broadcast([P, TOPK, TOPK]),
                                     tv[:, 1, :].unsqueeze(1).to_broadcast([P, TOPK, TOPK]), ALU.add))
                cflat, rflat = cand[:].rearrange("p a b -> p (a b)"), cand_r[:].rearrange("p a b -> p (a b)")
                v.tensor_copy(tif[:], ti[:])
                step(v.max(bv[:, 0:8], cflat), fixed=True)
                v.max_index(bp[:, 0:8], bv[:, 0:8], cflat)
                step(v.match_replace(rflat, bv[:, 0:8], cflat, LOWEST), fixed=True)
                between()
                step(v.max(bv[:, 8:16], rflat), fixed=True)
                step(v.max_index(bp[:, 8:16], bv[:, 8:16], rflat))
                v.tensor_scalar(bij[:, 0, :], bp[:], 4, None, ALU.logical_shift_right)
                step(v.tensor_scalar(bij[:, 1, :], bp[:], TOPK - 1, None, ALU.bitwise_and))
                step(v.tensor_copy(bijf[:], bij[:]))
                iota = cst[:, C_IOTA:C_IOTA + TOPK].unsqueeze(1).to_broadcast([P, TOPK, TOPK])
                for h in range(2):
                    ins = v.tensor_tensor(onehot[:, h], bijf[:, h, :].unsqueeze(2).to_broadcast([P, TOPK, TOPK]), iota, ALU.is_equal)
                step(ins)
                between()
                for h in range(2):
                    ins = v.tensor_tensor(onehot[:, h], onehot[:, h], tif[:, h, :].unsqueeze(1).to_broadcast([P, TOPK, TOPK]), ALU.mult)
                step(ins)
                step(v.tensor_reduce(pick_f[:], onehot[:], AX, ALU.add))
                step(v.scalar_tensor_tensor(expf[:], pick_f[:, 0, :], float(NKEYS), pick_f[:, 1, :], ALU.mult, ALU.add))
                v.tensor_copy(expert[:, bass.ds(i * TOPK + (TOPK * first + SLOTS * (t % 2)), TOPK)], expf[:])
                step(v.tensor_scalar(bv[:], bv[:], bv[:, 0:1], None, ALU.subtract))
                v.tensor_copy(gatev[:, bass.ds(i * TOPK + TOPK * first, TOPK)], bv[:]).then_inc(s("head_done"), 1)

            def loop(n, links, body):
                base, k = linked[0], [0]
                with v.Fori(0, n) as i:
                    def step(ins, fixed=False):
                        k[0] += 1
                        ins.then_inc(s("chain"), 1)
                        v.wait_ge(s("chain"), i * links + (base + k[0]))
                        if fixed:
                            v.sem_inc(s("waits_dve"), 1)
                    body(i, step)
                assert k[0] == links, k[0]
                linked[0] += n * links

            for i in range(4):
                group(G[f"pq{i}"], (2, 3), to_features(pq_t, 4 * i))
                v.wait_ge(s("sc_ready"), i + 1)
                loop(2, TOP_LINKS, lambda head, step: top_keys(0, head, step, first=2 * i))
            v.memset(zeros[:], 0.0).then_inc(s("zeros_ready"), 1)
            for j in range(RING):
                v.sem_inc(row_used[j], 1)

            def v_row(t, i, r, m, step):
                j = DVE_SLOTS[m]
                v.wait_ge(row_landed[j], i * 32 + 16 * (ROUNDS * (2 * t + 1) + r + 1))
                v.scalar_tensor_tensor(vacc[:, m, :], rows[:, j, :], hidd[:, r, m:m + 1], vacc[:, m, :], ALU.mult, ALU.add).then_inc(row_used[j], 1)

            def v_rounds(t, i, step, top):
                for r in range(2):
                    ins = v.tensor_copy(hidd[:, r, 0:3], hidv[:, bass.ds(i * (2 * RING) + (r * RING + DVE_SLOTS[0]), 7)][:, 0::3])
                step(ins)
                todo = [(r, m) for r in range(2) for m in range(len(DVE_SLOTS))]
                v_row(t, i, *todo.pop(0), step)
                if top:
                    top_keys(t + 1, i, step, between=lambda: v_row(t, i, *todo.pop(0), step))
                while todo:
                    v_row(t, i, *todo.pop(0), step)
                v.wait_ge(row_used[DVE_SLOTS[-1]], i * 2 + (ROUNDS * (2 * t + 1) + 3))

            def add_peer(t):
                acc = 2 * (t % 2)
                v.wait_ge(s("peer_ready"), t + 1)
                link(v.tensor_tensor(peer_g[:], ps[:, acc:acc + 2, :].rearrange("p b c -> p (b c)"), gate2[:], ALU.mult))
                v.tensor_tensor(x_res[:, t, :], x_res[:, t, :], peer_g[:], ALU.add).then_inc(x_ready, 1)

            for t in range(NT):
                def u_rows(i, step):
                    for j in range(RING):
                        v.wait_ge(row_landed[j], i * 16 + 16 * (2 * ROUNDS * t + 1))
                        ins = v.tensor_tensor_reduce(rows[:, j, :], rows[:, j, :], h2_s[:, t, :], 1.0, 0.0, ALU.mult, ALU.add, hidu[:, j:j + 1])
                        ins.then_inc(row_used[j], 1)
                    v.wait_ge(row_used[RING - 1], i + (2 * ROUNDS * t + 2))
                    v.tensor_copy(hid[:, bass.ts(i, RING)], hidu[:]).then_inc(s("hid_ready"), 1)
                    v.wait_ge(s("hid_ready"), i + (ROUNDS * t + 1))
                loop(ROUNDS, 0, u_rows)
                v.wait_ge(s("gate_act"), 2 * t + 1)
                ge = gatee[:].rearrange("p (h k) -> p h k", h=PEER_HEADS)
                link(v.tensor_reduce(gsum[:], ge, AX, ALU.add))
                link(v.reciprocal(grec[:], gsum[:]))
                link(v.tensor_tensor(gates[:].rearrange("p (h k) -> p h k", h=PEER_HEADS), ge, grec[:].unsqueeze(2).to_broadcast([P, PEER_HEADS, TOPK]), ALU.mult))
                v.wait_ge(s("gate_act"), 2 * t + 2)
                v.tensor_tensor(hidv[:], hidg[:], gates[:], ALU.mult).then_inc(s("hidv_ready"), 1)
                if t:
                    add_peer(t - 1)
                v.wait_ge(s("hidv_ready"), t + 1)
                link(v.memset(vacc[:], 0.0))
                if t + 1 < NT:
                    v.wait_ge(s("sc_ready"), t + 5)
                    loop(ROUNDS // 2, 1 + TOP_LINKS, lambda i, step: v_rounds(t, i, step, top=True))
                else:
                    loop(ROUNDS // 2, 1, lambda i, step: v_rounds(t, i, step, top=False))
            add_peer(NT - 1)
            v.wait_ge(usq_ready, 4 * NT)
            v.wait_ge(s("vectors_landed"), 64)
            inverse_root(rstd, meps, ssq, D)
            for i in range(NT):
                v.scalar_tensor_tensor(h2_s[:, i, :], x_res[:, i, :], rstd[:, i:i + 1], gfin[:], ALU.mult, ALU.mult).then_inc(s("out_ready"), 1)

        @block.sync
        def _(sp):
            sync_program(sp)

        @block.tensor
        def _(pe):
            tensor_program(pe)

        @block.vector
        def _(v):
            vector_program(v)

        @block.scalar
        def _(act):
            scalar_program(act)

        @block.gpsimd
        def _(pool):
            gpsimd_program(pool)


def lay_out(inputs):
    i = {k: np.asarray(v) for k, v in inputs.items()}

    def cols(v):
        return v.reshape(-1, P).T

    ada = i["b_ada_2"].reshape(6, D)
    arrays = {
        "x": i["x"], "mem": i["mem"], "w_in": i["w_in"][0], "w_br_att": i["w_br_att"][0], "w_br_ssm": i["w_br_ssm"][0],
        "w_mix_out": i["w_mix_out"][0], "w_xq": i["w_xq"][0], "w_xkv": i["w_xkv"][0], "w_xo": i["w_xo"][0],
        "w_gu": i["w_gu"][0], "w_down": i["w_down"][0], "w_ada_2": i["w_ada_2"][0], "w_in_2": i["w_in_2"][0],
        "w_out_2": i["w_out_2"][0], "peer_wq_2": i["peer_wq_2"][0], "u": i["peer_u_2"][0], "v": i["peer_v_2"][0],
        "g_post_mix": i["g_post_mix"], "g_post_xa": i["g_post_xa"], "g_post_ffn": i["g_post_ffn"],
        "g_final": i["final_norm_w_2"].reshape(1, D), "b_ada": i["b_ada_2"],
        "gup": np.concatenate([i["gla_gate_up_2"][0], i["gla_gate_bias_2"]], axis=0),
        "subk": i["peer_subkeys_2"][0].reshape(16, NKEYS, P).transpose(2, 0, 1),
        "cst": constant_matrices(),
        "vec": np.concatenate([cols(i["g_pre_mix"][0]), cols(i["g_mem"][0]), cols(i["g_pre_xa"][0]), cols(i["g_pre_ffn"][0]),
                               cols(i["norm1_w_2"][0]), cols(i["norm2_w_2"][0]), cols(i["c_2"][0]), cols(i["g_ssm_norm"][0]),
                               cols(i["conv_b"][0])] + [cols(i["conv_w"][0, t]) for t in range(4)]
                              + [cols(ada[n]) for n in range(6)] + [cols(i["gla_norm_w_2"][0])], axis=1),
        "row": np.concatenate([i["dt_bias"], i["a_log"], i["d_skip"], i["attn_sinks_2"]], axis=1),
    }
    return {k: np.ascontiguousarray(v) for k, v in arrays.items()}


def kernel(**inputs):
    import concourse.bacc as bacc
    from concourse.bass_utils import run_bass_kernel_spmd

    nc = bacc.Bacc("TRN2", target_bir_lowering=False, num_devices=1)
    arrays = lay_out(inputs)
    aps = {k: nc.dram_tensor(f"in_{k}", v.shape, mybir.dt.from_np(v.dtype), kind="ExternalInput").ap() for k, v in arrays.items()}
    out = nc.dram_tensor("out_0", (1, T, D), F32, kind="ExternalOutput").ap()
    build_program(nc, aps, out)
    r = run_bass_kernel_spmd(nc, [{f"in_{k}": v for k, v in arrays.items()}], core_ids=[0])
    return r.results[0]["out_0"]
```
